# Optimizing a Trainium2 kernel written in Bass

```python
import math
import jax, jax.numpy as jnp
from jax import lax
import numpy as np

D_MODEL = 2048
BATCH = 1
SEQ = 256
DEPTH = 1

CHUNK = 64
N_META = 16
HEAD_DIM = 128
SB_HEADS = 8
FOX_HEADS = 8
SB_WIDTH = SB_HEADS * HEAD_DIM
FOX_WIDTH = FOX_HEADS * HEAD_DIM
MIX_WIDTH = SB_WIDTH + FOX_WIDTH
C_IN = 3 * SB_WIDTH + 4 * FOX_WIDTH + FOX_HEADS
Q_BLOCK = 128
PEER_HEADS = 8
PEER_TOPK = 16
N_KEYS = 128
N_EXPERTS = N_KEYS * N_KEYS
D_KEY = 256
PEER_BLOCK = 128
EPS = 1e-6


def rms_norm(x, gain):
    xf = x.astype(jnp.float32)
    y = xf * lax.rsqrt(jnp.mean(xf * xf, axis=-1, keepdims=True) + EPS)
    return y.astype(x.dtype) * gain

def to_query_blocks(a):
    b, l = a.shape[:2]
    return jnp.moveaxis(a.reshape((b, l // Q_BLOCK, Q_BLOCK) + a.shape[2:]), 1, 0)

def from_query_blocks(a):
    a = jnp.moveaxis(a, 0, 1)
    b, nb, qb = a.shape[:3]
    return a.reshape(b, nb * qb, -1)

def stick_breaking_attention(q, k, v):
    L = k.shape[1]
    k_pos = jnp.arange(L)
    scale = 1.0 / math.sqrt(HEAD_DIM)
    starts = jnp.arange(L // Q_BLOCK, dtype=jnp.int32) * Q_BLOCK

    def block(args):
        qb, start = args
        q_pos = start + jnp.arange(Q_BLOCK)
        z = jnp.einsum('bqhd,bkhd->bhqk', qb, k).astype(jnp.float32) * scale
        visible = k_pos[None, :] < q_pos[:, None]
        log_1mb = jnp.where(visible, jax.nn.log_sigmoid(-z), 0.0)
        after = lax.cumsum(log_1mb, axis=3, reverse=True) - log_1mb
        w = jnp.where(visible, jnp.exp(jax.nn.log_sigmoid(z) + after), 0.0)
        return jnp.einsum('bhqk,bkhd->bqhd', w.astype(v.dtype), v)

    out = lax.map(block, (to_query_blocks(q), starts))
    return from_query_blocks(out)

def forgetting_attention(q, k, v, log_f):
    L = k.shape[1]
    k_pos = jnp.arange(L)
    scale = 1.0 / math.sqrt(HEAD_DIM)
    cum_f = lax.cumsum(log_f, axis=1)
    cum_f_k = jnp.transpose(cum_f, (0, 2, 1))
    starts = jnp.arange(L // Q_BLOCK, dtype=jnp.int32) * Q_BLOCK

    def block(args):
        qb, fq, start = args
        q_pos = start + jnp.arange(Q_BLOCK)
        z = jnp.einsum('bqhd,bkhd->bhqk', qb, k).astype(jnp.float32) * scale
        logits = z + jnp.transpose(fq, (0, 2, 1))[..., None] - cum_f_k[:, :, None, :]
        visible = k_pos[None, :] <= q_pos[:, None]
        p = jax.nn.softmax(jnp.where(visible, logits, -jnp.inf), axis=-1)
        return jnp.einsum('bhqk,bkhd->bqhd', p.astype(v.dtype), v)

    out = lax.map(block, (to_query_blocks(q), to_query_blocks(cum_f), starts))
    return from_query_blocks(out)

def mixer_sublayer(h, w_in, b_forget, fox_q_gain, fox_k_gain, sb_out_gain, fox_out_gain, w_out):
    B, L, _ = h.shape
    proj = h @ w_in
    s3 = 3 * SB_WIDTH
    sb_q, sb_k, sb_v, fq, fk, fv, fgate, flogit = jnp.split(
        proj,
        [SB_WIDTH, 2 * SB_WIDTH, s3, s3 + FOX_WIDTH, s3 + 2 * FOX_WIDTH,
         s3 + 3 * FOX_WIDTH, s3 + 4 * FOX_WIDTH],
        axis=-1)

    def heads(a, n):
        return a.reshape(B, L, n, HEAD_DIM)

    sb = stick_breaking_attention(heads(sb_q, SB_HEADS), heads(sb_k, SB_HEADS), heads(sb_v, SB_HEADS))
    log_f = jax.nn.log_sigmoid((flogit + b_forget).astype(jnp.float32))
    fox = forgetting_attention(rms_norm(heads(fq, FOX_HEADS), fox_q_gain),
                               rms_norm(heads(fk, FOX_HEADS), fox_k_gain),
                               heads(fv, FOX_HEADS), log_f)
    merged = jnp.concatenate(
        [rms_norm(sb, sb_out_gain),
         rms_norm(fox, fox_out_gain) * jax.nn.sigmoid(fgate)], axis=-1)
    return merged @ w_out

def peer_sublayer(h, w_query, sub_keys, u, v):
    B, L, D = h.shape
    blocks = h.reshape(-1, PEER_BLOCK, D)

    def block(hb):
        q = (hb @ w_query).reshape(PEER_BLOCK, PEER_HEADS, 2, D_KEY // 2)
        s = jnp.einsum('thpc,hpnc->thpn', q, sub_keys).astype(jnp.float32)
        top_s, top_i = lax.top_k(s, PEER_TOPK)
        cand_s = (top_s[:, :, 0, :, None] + top_s[:, :, 1, None, :]).reshape(PEER_BLOCK, PEER_HEADS, -1)
        cand_i = (top_i[:, :, 0, :, None] * N_KEYS + top_i[:, :, 1, None, :]).reshape(PEER_BLOCK, PEER_HEADS, -1)
        best_s, best_j = lax.top_k(cand_s, PEER_TOPK)
        idx = jnp.take_along_axis(cand_i, best_j, axis=-1)
        g = jax.nn.softmax(best_s, axis=-1)
        u_sel = jnp.take(u, idx, axis=0)
        a = jax.nn.gelu(jnp.einsum('thkd,td->thk', u_sel, hb), approximate=False)
        v_sel = jnp.take(v, idx, axis=0)
        return jnp.einsum('thk,thkd->td', (g * a).astype(hb.dtype), v_sel)

    return lax.map(block, blocks).reshape(B, L, D)

def first_inputs(seed: int = 0) -> dict:
    key = jax.random.key(seed)
    ks = jax.random.split(key, 15)
    f32 = jnp.float32
    nrm = lambda k, shape, s: jax.random.normal(k, shape, f32) * s
    gain = lambda k, shape: 1.0 + 0.02 * jax.random.normal(k, shape, f32)
    return {
        "x": nrm(ks[0], (BATCH, SEQ, D_MODEL), 1.0),
        "meta_tokens": nrm(ks[1], (N_META, D_MODEL), 1.0),
        "norm_mix": gain(ks[2], (DEPTH, D_MODEL)),
        "w_in": nrm(ks[3], (DEPTH, D_MODEL, C_IN), D_MODEL ** -0.5),
        "b_forget": jax.random.uniform(ks[4], (DEPTH, FOX_HEADS), f32, 1.0, 4.0),
        "fox_q_gain": gain(ks[5], (DEPTH, HEAD_DIM)),
        "fox_k_gain": gain(ks[6], (DEPTH, HEAD_DIM)),
        "sb_out_gain": gain(ks[7], (DEPTH, SB_WIDTH)),
        "fox_out_gain": gain(ks[8], (DEPTH, FOX_WIDTH)),
        "w_out": nrm(ks[9], (DEPTH, MIX_WIDTH, D_MODEL), MIX_WIDTH ** -0.5),
        "norm_ffn": gain(ks[10], (DEPTH, D_MODEL)),
        "peer_w_query": nrm(ks[11], (DEPTH, D_MODEL, PEER_HEADS * D_KEY), D_MODEL ** -0.5),
        "peer_sub_keys": nrm(ks[12], (DEPTH, PEER_HEADS, 2, N_KEYS, D_KEY // 2), (D_KEY // 2) ** -0.5),
        "peer_u": nrm(ks[13], (DEPTH, N_EXPERTS, D_MODEL), D_MODEL ** -0.5),
        "peer_v": nrm(ks[14], (DEPTH, N_EXPERTS, D_MODEL), PEER_HEADS ** -0.5),
    }

def first_block(x, meta_tokens, norm_mix, w_in, b_forget, fox_q_gain, fox_k_gain,
              sb_out_gain, fox_out_gain, w_out, norm_ffn, peer_w_query, peer_sub_keys,
              peer_u, peer_v):
    B, S, D = x.shape
    l_pad = ((S + N_META + Q_BLOCK - 1) // Q_BLOCK) * Q_BLOCK
    meta = jnp.broadcast_to(meta_tokens[None].astype(x.dtype), (B, N_META, D))
    pad = jnp.zeros((B, l_pad - S - N_META, D), x.dtype)
    h = jnp.concatenate([meta, x, pad], axis=1)
    for l in range(DEPTH):
        h = h + mixer_sublayer(rms_norm(h, norm_mix[l]), w_in[l], b_forget[l],
                               fox_q_gain[l], fox_k_gain[l], sb_out_gain[l],
                               fox_out_gain[l], w_out[l])
        h = h + peer_sublayer(rms_norm(h, norm_ffn[l]), peer_w_query[l],
                              peer_sub_keys[l], peer_u[l], peer_v[l])
    return h[:, N_META:N_META + S]


N_ATTN_HEADS = 8
ATTN_WIDTH = N_ATTN_HEADS * HEAD_DIM
MOBA_BLOCK = 256
MOBA_TOPK = 3
Q_CHUNK = 32
ROPE_THETA = 10000.0
SSM_WIDTH = D_MODEL // 2
SSM_GROUP = 16
SSM_GROUPS = SSM_WIDTH // SSM_GROUP
SSM_STATE = 64
FFN_HIDDEN = 5632
CONV_WIDTH = 3
N_BRANCHES = 2
N_MOD = 6
IN_WIDTH = 3 * ATTN_WIDTH + SSM_WIDTH + N_BRANCHES * D_MODEL
NEG_INF = -1e30


def rms_norm_2(x, g):
    xf = x.astype(jnp.float32)
    y = xf * lax.rsqrt(jnp.mean(xf * xf, axis=-1, keepdims=True) + EPS)
    return y.astype(x.dtype) * g

def rotary(x, positions):
    half = HEAD_DIM // 2
    inv_freq = ROPE_THETA ** (-jnp.arange(half, dtype=jnp.float32) / half)
    ang = positions.astype(jnp.float32)[..., None] * inv_freq
    cos = jnp.cos(ang)[:, :, None, :].astype(x.dtype)
    sin = jnp.sin(ang)[:, :, None, :].astype(x.dtype)
    x1, x2 = x[..., :half], x[..., half:]
    return jnp.concatenate([x1 * cos - x2 * sin, x1 * sin + x2 * cos], axis=-1)

def moba_attention(q, k, v):
    b, h, s, dh = q.shape
    n_blocks = -(-s // MOBA_BLOCK)
    s_pad = n_blocks * MOBA_BLOCK
    topk = min(MOBA_TOPK, n_blocks)
    pad = ((0, 0), (0, 0), (0, s_pad - s), (0, 0))
    k_p = jnp.pad(k, pad)
    v_p = jnp.pad(v, pad)
    k_blocks = k_p.reshape(b, h, n_blocks, MOBA_BLOCK, dh)
    v_blocks = v_p.reshape(b, h, n_blocks, MOBA_BLOCK, dh)
    k_mean = jnp.mean(k_blocks.astype(jnp.float32), axis=3).astype(k.dtype)
    scale = HEAD_DIM ** -0.5
    gather = jax.vmap(jax.vmap(lambda blocks, idx: blocks[idx]))

    def chunk(ci):
        start = ci * Q_CHUNK
        q_c = lax.dynamic_slice_in_dim(q, start, Q_CHUNK, axis=2)
        t = start + jnp.arange(Q_CHUNK)
        cur = start // MOBA_BLOCK
        blk_scores = jnp.einsum('bhqd,bhnd->bhqn', q_c, k_mean).astype(jnp.float32)
        past = jnp.arange(n_blocks) < cur
        blk_scores = jnp.where(past, blk_scores, NEG_INF)
        _, idx = lax.top_k(blk_scores, topk)
        slot_ok = jnp.arange(topk) < cur
        k_sel = gather(k_blocks, idx)
        v_sel = gather(v_blocks, idx)
        s_sel = jnp.einsum('bhqd,bhqnjd->bhqnj', q_c, k_sel).astype(jnp.float32) * scale
        s_sel = jnp.where(slot_ok[:, None], s_sel, NEG_INF).reshape(b, h, Q_CHUNK, topk * MOBA_BLOCK)
        k_own = lax.dynamic_slice_in_dim(k_p, cur * MOBA_BLOCK, MOBA_BLOCK, axis=2)
        v_own = lax.dynamic_slice_in_dim(v_p, cur * MOBA_BLOCK, MOBA_BLOCK, axis=2)
        s_own = jnp.einsum('bhqd,bhjd->bhqj', q_c, k_own).astype(jnp.float32) * scale
        key_pos = cur * MOBA_BLOCK + jnp.arange(MOBA_BLOCK)
        s_own = jnp.where(key_pos[None, :] <= t[:, None], s_own, NEG_INF)
        p = jax.nn.softmax(jnp.concatenate([s_sel, s_own], axis=-1), axis=-1).astype(v.dtype)
        p_sel = p[..., :topk * MOBA_BLOCK].reshape(b, h, Q_CHUNK, topk, MOBA_BLOCK)
        p_own = p[..., topk * MOBA_BLOCK:]
        return (jnp.einsum('bhqnj,bhqnjd->bhqd', p_sel, v_sel)
                + jnp.einsum('bhqj,bhjd->bhqd', p_own, v_own))

    out = lax.map(chunk, jnp.arange(s // Q_CHUNK))
    return out.transpose(1, 2, 0, 3, 4).reshape(b, h, s, dh)

def s5_branch(u, lam_re, lam_im, log_dt, b_re, b_im, c_re, c_im, d_skip, w_glu, b_glu):
    bsz, s, _ = u.shape
    f32 = jnp.float32
    ug = u.reshape(bsz, s, SSM_GROUPS, SSM_GROUP).astype(f32)
    dt = jnp.exp(log_dt.astype(f32))[:, None]
    lr = lam_re.astype(f32)
    li = lam_im.astype(f32)
    mag = jnp.exp(lr * dt)
    ab_re = mag * jnp.cos(li * dt)
    ab_im = mag * jnp.sin(li * dt)
    den = lr * lr + li * li
    nr = ab_re - 1.0
    ni = ab_im
    coef_re = (nr * lr + ni * li) / den
    coef_im = (ni * lr - nr * li) / den
    bu_re = jnp.einsum('bsgh,gph->bsgp', ug, b_re.astype(f32))
    bu_im = jnp.einsum('bsgh,gph->bsgp', ug, b_im.astype(f32))
    x_re0 = coef_re * bu_re - coef_im * bu_im
    x_im0 = coef_re * bu_im + coef_im * bu_re
    a_re = jnp.broadcast_to(ab_re, x_re0.shape)
    a_im = jnp.broadcast_to(ab_im, x_re0.shape)

    def combine(e1, e2):
        a1r, a1i, b1r, b1i = e1
        a2r, a2i, b2r, b2i = e2
        return (a2r * a1r - a2i * a1i, a2r * a1i + a2i * a1r,
                a2r * b1r - a2i * b1i + b2r, a2r * b1i + a2i * b1r + b2i)

    _, _, xr, xi = lax.associative_scan(combine, (a_re, a_im, x_re0, x_im0), axis=1)
    y = (jnp.einsum('bsgp,ghp->bsgh', xr, c_re.astype(f32))
         - jnp.einsum('bsgp,ghp->bsgh', xi, c_im.astype(f32))
         + d_skip.astype(f32).reshape(SSM_GROUPS, SSM_GROUP) * ug)
    y = jax.nn.gelu(y.reshape(bsz, s, SSM_WIDTH)).astype(u.dtype)
    return y * jax.nn.sigmoid(y @ w_glu + b_glu)

def causal_dwconv(u, w, bias):
    ch = u.shape[-1]
    y = lax.conv_general_dilated(u, w[:, None, :].astype(u.dtype), window_strides=(1,),
                                 padding=[(CONV_WIDTH - 1, 0)],
                                 dimension_numbers=('NWC', 'WIO', 'NWC'),
                                 feature_group_count=ch)
    return y + bias

def second_inputs(seed: int = 0) -> dict:
    key = jax.random.key(seed)
    ks = jax.random.split(key, 32)
    nrm = jax.random.normal
    L = DEPTH
    x = nrm(ks[0], (BATCH, SEQ, D_MODEL), jnp.float32)
    c = nrm(ks[1], (BATCH, D_MODEL), jnp.float32)
    offsets = jax.random.randint(ks[2], (BATCH, 1), 0, 1024, dtype=jnp.int32)
    positions = offsets + jnp.arange(SEQ, dtype=jnp.int32)[None, :]
    w_mod = nrm(ks[3], (L, D_MODEL, N_MOD * D_MODEL), jnp.float32) * (0.5 * D_MODEL ** -0.5)
    b_mod = nrm(ks[4], (L, N_MOD * D_MODEL), jnp.float32) * 0.01
    norm1_g = 1.0 + 0.02 * nrm(ks[5], (L, D_MODEL), jnp.float32)
    w_in = nrm(ks[6], (L, D_MODEL, IN_WIDTH), jnp.float32) * D_MODEL ** -0.5
    q_norm_g = 1.0 + 0.02 * nrm(ks[7], (L, HEAD_DIM), jnp.float32)
    k_norm_g = 1.0 + 0.02 * nrm(ks[8], (L, HEAD_DIM), jnp.float32)
    n_idx = jnp.arange(SSM_STATE, dtype=jnp.float32)
    ssm_lambda_re = -0.5 + 0.01 * nrm(ks[9], (L, SSM_GROUPS, SSM_STATE), jnp.float32)
    ssm_lambda_im = math.pi * n_idx + 0.01 * nrm(ks[10], (L, SSM_GROUPS, SSM_STATE), jnp.float32)
    ssm_log_dt = jax.random.uniform(ks[11], (L, SSM_GROUPS), jnp.float32, math.log(1e-3), math.log(1e-1))
    b_scale = (2.0 * SSM_GROUP) ** -0.5
    ssm_b_re = nrm(ks[12], (L, SSM_GROUPS, SSM_STATE, SSM_GROUP), jnp.float32) * b_scale
    ssm_b_im = nrm(ks[13], (L, SSM_GROUPS, SSM_STATE, SSM_GROUP), jnp.float32) * b_scale
    c_scale = (2.0 * SSM_STATE) ** -0.5
    ssm_c_re = nrm(ks[14], (L, SSM_GROUPS, SSM_GROUP, SSM_STATE), jnp.float32) * c_scale
    ssm_c_im = nrm(ks[15], (L, SSM_GROUPS, SSM_GROUP, SSM_STATE), jnp.float32) * c_scale
    ssm_d = nrm(ks[16], (L, SSM_WIDTH), jnp.float32)
    w_glu = nrm(ks[17], (L, SSM_WIDTH, SSM_WIDTH), jnp.float32) * SSM_WIDTH ** -0.5
    b_glu = nrm(ks[18], (L, SSM_WIDTH), jnp.float32) * 0.01
    w_attn_br = nrm(ks[19], (L, ATTN_WIDTH, D_MODEL), jnp.float32) * ATTN_WIDTH ** -0.5
    w_ssm_br = nrm(ks[20], (L, SSM_WIDTH, D_MODEL), jnp.float32) * SSM_WIDTH ** -0.5
    w_out = nrm(ks[21], (L, D_MODEL, D_MODEL), jnp.float32) * D_MODEL ** -0.5
    norm2_g = 1.0 + 0.02 * nrm(ks[22], (L, D_MODEL), jnp.float32)
    w_up = nrm(ks[23], (L, D_MODEL, 2 * FFN_HIDDEN), jnp.float32) * D_MODEL ** -0.5
    conv_w = nrm(ks[24], (L, CONV_WIDTH, 2 * FFN_HIDDEN), jnp.float32) * CONV_WIDTH ** -0.5
    conv_b = nrm(ks[25], (L, 2 * FFN_HIDDEN), jnp.float32) * 0.01
    w_down = nrm(ks[26], (L, FFN_HIDDEN, D_MODEL), jnp.float32) * FFN_HIDDEN ** -0.5
    return {'x': x, 'c': c, 'positions': positions, 'w_mod': w_mod, 'b_mod': b_mod,
            'norm1_g': norm1_g, 'w_in': w_in, 'q_norm_g': q_norm_g, 'k_norm_g': k_norm_g,
            'ssm_lambda_re': ssm_lambda_re, 'ssm_lambda_im': ssm_lambda_im, 'ssm_log_dt': ssm_log_dt,
            'ssm_b_re': ssm_b_re, 'ssm_b_im': ssm_b_im, 'ssm_c_re': ssm_c_re, 'ssm_c_im': ssm_c_im,
            'ssm_d': ssm_d, 'w_glu': w_glu, 'b_glu': b_glu, 'w_attn_br': w_attn_br,
            'w_ssm_br': w_ssm_br, 'w_out': w_out, 'norm2_g': norm2_g, 'w_up': w_up,
            'conv_w': conv_w, 'conv_b': conv_b, 'w_down': w_down}

def second_block(x, c, positions, w_mod, b_mod, norm1_g, w_in, q_norm_g, k_norm_g,
              ssm_lambda_re, ssm_lambda_im, ssm_log_dt, ssm_b_re, ssm_b_im, ssm_c_re, ssm_c_im,
              ssm_d, w_glu, b_glu, w_attn_br, w_ssm_br, w_out, norm2_g, w_up, conv_w, conv_b,
              w_down):
    bsz, s, _ = x.shape
    split_pts = [ATTN_WIDTH, 2 * ATTN_WIDTH, 3 * ATTN_WIDTH, 3 * ATTN_WIDTH + SSM_WIDTH]
    for l in range(DEPTH):
        mod = jax.nn.silu(c) @ w_mod[l] + b_mod[l]
        sh1, sc1, g1, sh2, sc2, g2 = jnp.split(mod, N_MOD, axis=-1)

        h = rms_norm_2(x, norm1_g[l]) * (1.0 + sc1[:, None]) + sh1[:, None]
        proj = h @ w_in[l]
        q, k, v, u, gates = jnp.split(proj, split_pts, axis=-1)
        q = rotary(rms_norm_2(q.reshape(bsz, s, N_ATTN_HEADS, HEAD_DIM), q_norm_g[l]), positions)
        k = rotary(rms_norm_2(k.reshape(bsz, s, N_ATTN_HEADS, HEAD_DIM), k_norm_g[l]), positions)
        v = v.reshape(bsz, s, N_ATTN_HEADS, HEAD_DIM)
        attn = moba_attention(q.transpose(0, 2, 1, 3), k.transpose(0, 2, 1, 3), v.transpose(0, 2, 1, 3))
        y_attn = attn.transpose(0, 2, 1, 3).reshape(bsz, s, ATTN_WIDTH)
        y_ssm = s5_branch(u, ssm_lambda_re[l], ssm_lambda_im[l], ssm_log_dt[l], ssm_b_re[l], ssm_b_im[l],
                          ssm_c_re[l], ssm_c_im[l], ssm_d[l], w_glu[l], b_glu[l])
        gate_a, gate_s = jnp.split(gates, N_BRANCHES, axis=-1)
        merged = (jax.nn.sigmoid(gate_a) * (y_attn @ w_attn_br[l])
                  + jax.nn.sigmoid(gate_s) * (y_ssm @ w_ssm_br[l]))
        x = x + g1[:, None] * (merged @ w_out[l])

        h2 = rms_norm_2(x, norm2_g[l]) * (1.0 + sc2[:, None]) + sh2[:, None]
        up = causal_dwconv(h2 @ w_up[l], conv_w[l], conv_b[l])
        val, gt = jnp.split(up, 2, axis=-1)
        x = x + g2[:, None] * ((jax.nn.silu(gt) * val) @ w_down[l])
    return x


def setup_inputs(seed=0):
    out = dict(first_inputs(seed))
    for name, value in second_inputs(seed + 1).items():
        if name != "x":
            out[name + "_2"] = value
    return out


def reference(
    x, meta_tokens, norm_mix, w_in, b_forget, fox_q_gain, fox_k_gain, sb_out_gain, fox_out_gain,
    w_out, norm_ffn, peer_w_query, peer_sub_keys, peer_u, peer_v, c_2, positions_2, w_mod_2,
    b_mod_2, norm1_g_2, w_in_2, q_norm_g_2, k_norm_g_2, ssm_lambda_re_2, ssm_lambda_im_2,
    ssm_log_dt_2, ssm_b_re_2, ssm_b_im_2, ssm_c_re_2, ssm_c_im_2, ssm_d_2, w_glu_2, b_glu_2,
    w_attn_br_2, w_ssm_br_2, w_out_2, norm2_g_2, w_up_2, conv_w_2, conv_b_2, w_down_2,
):
    x = first_block(
        x, meta_tokens, norm_mix, w_in, b_forget, fox_q_gain, fox_k_gain, sb_out_gain,
        fox_out_gain, w_out, norm_ffn, peer_w_query, peer_sub_keys, peer_u, peer_v,
    )
    return second_block(
        x, c_2, positions_2, w_mod_2, b_mod_2, norm1_g_2, w_in_2, q_norm_g_2, k_norm_g_2,
        ssm_lambda_re_2, ssm_lambda_im_2, ssm_log_dt_2, ssm_b_re_2, ssm_b_im_2, ssm_c_re_2,
        ssm_c_im_2, ssm_d_2, w_glu_2, b_glu_2, w_attn_br_2, w_ssm_br_2, w_out_2, norm2_g_2,
        w_up_2, conv_w_2, conv_b_2, w_down_2,
    )


_drawn_inputs = setup_inputs


def setup_inputs(seed=0):
    import zlib

    import numpy as np

    out = dict(_drawn_inputs(seed))
    spreads = {}
    factors = {'fox_q_gain': 4.75,
     'fox_k_gain': 5.353,
     'sb_out_gain': 2.991,
     'fox_out_gain': 4.491,
     'norm_ffn': 2.714,
     'b_mod_2': 7.94,
     'norm1_g_2': 8.0,
     'q_norm_g_2': 8.0,
     'k_norm_g_2': 8.0,
     'ssm_lambda_re_2': 64.0,
     'ssm_lambda_im_2': 64.0,
     'ssm_log_dt_2': 64.0,
     'ssm_b_re_2': 64.0,
     'ssm_b_im_2': 64.0,
     'ssm_c_re_2': 64.0,
     'ssm_c_im_2': 64.0,
     'w_glu_2': 3.336,
     'b_glu_2': 196.793,
     'norm2_g_2': 8.0,
     'conv_b_2': 33.473}
    for name, (base, spread) in spreads.items():
        noise = np.random.default_rng([zlib.crc32(name.encode()), seed]).standard_normal(out[name].shape)
        drawn = base * np.exp(spread * noise) if base else spread * noise
        out[name] = __import__('jax').numpy.asarray(drawn.astype(out[name].dtype))
    for name, factor in factors.items():
        out[name] = (out[name] * factor).astype(out[name].dtype)
    return out
```

```python
from contextlib import ExitStack, contextmanager

import numpy as np
import concourse.bass as bass
from concourse import mybir

F32 = mybir.dt.float32
I32 = mybir.dt.int32
U32 = mybir.dt.uint32
ALU = mybir.AluOpType
ACT = mybir.ActivationFunctionType
AX = mybir.AxisListType

P = 128
SEQ = 256
META = 16
KEYS = META + SEQ
D = 2048
KC = D // P
HEADS = 8
RING = 4
TILE = 2048
SCALE = float(P) ** -0.5
EPS = 1e-6
TOPK = 16
N_SUB = 128
SLOTS = HEADS * TOPK
FFN = 5632
FC = FFN // P
DOWN_KC = 11
N_MOD = 6
NEG = -1e30
LOWEST = -3.0e38
ROUND = 12582912.0
INV_2PI = 0.15915494309189535
TWO_PI_PARTS = (6.28125, 2029 / 2.0**20, 2 * np.pi - 6.28125 - 2029 / 2.0**20)
PI_BELOW = 3.1415925

STREAM = [("w_in", 56, 2048), ("w_out", 16, 2048), ("w_query", 16, 2048), ("peer_u", 128, 2048),
          ("peer_v", 128, 2048), ("w_in_2", 64, 2048), ("w_glu", 4, 2048), ("w_attn_br", 8, 2048),
          ("w_ssm_br", 8, 2048), ("w_out_2", 16, 2048), ("w_up", 88, 2048), ("w_down", 64, DOWN_KC * P)]
FIRST = {}
_n = 0
for _name, _tiles, _ in STREAM:
    FIRST[_name] = _n
    _n += _tiles


class Steps:

    def __init__(self, eng, sem):
        self.eng, self.sem, self.done, self.turn = eng, sem, 0, 0

    def link(self, ins):
        ins.then_inc(self.sem, 1)
        self.done += 1
        self.eng.wait_ge(self.sem, self.turn + self.done)

    @contextmanager
    def loop(self, turns, links):
        with self.eng.Fori(0, turns) as i:
            before, self.turn = self.done, i * links
            yield i
            assert self.done - before == links, (self.done - before, links)
            self.turn = 0
            self.done = before + links * turns


def build(nc, d, out, last_stage=99):
    ctx = ExitStack()
    with ctx:
        def sb(name, shape, dt=F32):
            return ctx.enter_context(nc.sbuf_tensor(name, shape, dt))

        def sem(name):
            return ctx.enter_context(nc.semaphore(name))

        ring = sb("ring", [P, RING, TILE])
        xT = sb("xT", [P, KC, KEYS])
        hT = sb("hT", [P, KC, KEYS])
        big = sb("big", [P, 128 * SEQ])
        ident = sb("ident", [P, P])
        ones = sb("ones", [P, P])
        later = sb("later", [P, P])
        swap = sb("swap", [P, P])
        ramp = sb("ramp", [P, SEQ])
        causal = sb("causal", [P, 2, KEYS])
        vecs = sb("vecs", [P, 240])
        mod = sb("mod", [P, N_MOD * KC])
        gmod = sb("gmod", [P, KC])
        rstd = sb("rstd", [P, 2, KEYS])
        small = sb("small", [P, 32])
        late = sb("late", [P, 768])
        picked = late[:, :].rearrange("p (a b) -> p a b", a=3)
        convw = late[:, 0:352].rearrange("p (a b) -> p a b", a=4)
        posi = late[:, 352:608].bitcast(I32)
        lamp = late[:, 608:768].rearrange("p (a b) -> p a b", a=5)
        small_t = sb("small_t", [P, 10, 16])
        small2 = sb("small2", [P, 2, 32])
        idx = sb("idx", [P, 3, 16], U32)
        wf = sb("wf", [P, KC, HEADS])

        PS = ctx.enter_context(nc.psum_tensor("PS", [P, 8, 512], F32))

        def region(start, *shape):
            n = 1
            for s in shape:
                n *= s
            assert start + n <= 128 * SEQ
            v = big[:, start:start + n]
            if len(shape) == 1:
                return v
            names = "abcd"[:len(shape)]
            return v.rearrange(f"p ({' '.join(names)}) -> p {' '.join(names)}",
                               **{k: s for k, s in zip(names, shape)})

        V_MIX, V_SBG, V_FOXG, V_QG, V_KG, V_FFN = 0, 16, 24, 32, 33, 34
        V_N1, V_QG2, V_KG2, V_D, V_BGLU, V_N2, V_BMOD, V_C, V_FREQ, V_BF = 50, 66, 67, 68, 76, 84, 100, 196, 212, 213

        p1 = region(0, 56, KEYS)
        B1 = 56 * KEYS
        modring = region(B1, 2, TILE)
        modacc = region(B1 + 2 * TILE, N_MOD, TILE)
        seen = region(B1 + 2 * TILE + N_MOD * TILE, 3, SEQ)
        sq1 = region(B1, 16, KEYS)
        rs1 = region(B1 + 16 * KEYS, 16, KEYS)
        sumf = big[0:HEADS, B1 + 32 * KEYS:B1 + 33 * KEYS]
        pickh = big[0:HEADS, B1 + 33 * KEYS:B1 + 41 * KEYS].rearrange("p (a b) -> p a b", a=HEADS)
        negf = big[0:HEADS, B1 + 41 * KEYS:B1 + 49 * KEYS].rearrange("p (a b) -> p a b", a=HEADS)
        logf = big[0:HEADS, B1 + 49 * KEYS:B1 + 50 * KEYS]
        logt = big[0:HEADS, B1 + 50 * KEYS:B1 + 51 * KEYS]

        def attention_parts(at):
            parts, out = [("q", 256), ("k", 384), ("v", 384), ("vn", 384), ("a", 768), ("e", 768), ("L", 768),
                          ("w", 768), ("P", 2 * KEYS), ("PT", 768)], {}
            for n, size in parts:
                out[n] = region(at, size)
                at += size
            return out

        a1 = attention_parts(B1)
        ga = region(0, N_SUB, SEQ)
        TAIL = 88
        qx = region(TAIL * SEQ, 16, SEQ)
        sx = region((TAIL + 16) * SEQ, 2, 16, N_SUB)
        T0 = (TAIL + 32) * SEQ
        st = region(T0, 256)
        st2 = region(T0 + 256, 256)
        cand = region(T0 + 512, 256)
        oneh = region(T0 + 768, 16, 16)
        sel = region(T0 + 1024, 3, 2, SLOTS)
        sel8 = region(T0 + 1024, 3, 2 * HEADS, TOPK)
        best = region(T0 + 1024 + 768, 16)
        hTf = hT[:, :, :].rearrange("p a b -> p (a b)")
        oneA = hTf[:, 0:1024].rearrange("p (g t i) -> p g t i", g=2, t=4)
        oneB = hTf[:, 1024:2048].rearrange("p (g t i) -> p g t i", g=2, t=4)
        p2 = region(0, 64, SEQ)
        B2 = 64 * SEQ
        sq2 = region(B2, 16, SEQ)
        rs2 = region(B2 + 4096, 16, SEQ)
        cosr = region(B2 + 8192, SEQ)
        sinr = region(B2 + 8448, SEQ)
        angr = region(B2 + 8704, SEQ)
        numr = region(B2 + 8960, SEQ)
        a2 = attention_parts(B2 + 9216)
        ust = region(B2, SEQ)
        bst = region(B2 + 256, 2, P)
        cst = region(B2 + 512, 2, 4, 32)
        cc = region(B2 + 768, 2, 4, 32)
        ct = region(B2 + 1024, 2, 4, 32)
        ysum = region(B2 + 1280, SEQ)
        s5 = [region(B2 + 1536 + 1024 * k, 4, SEQ) for k in range(10)]
        s5_ang, s5_num, s5_sin, s5_cos, s5_p, s5_q, s5_zr, s5_zi, s5_xr, s5_xi = s5
        glug = region(B2, 8, SEQ)
        mtmp = region(B2 + 2048, 2, SEQ)
        act = region(0, FC, SEQ)
        cva = region(B2, SEQ)
        cgt = region(B2 + 256, SEQ)
        keysx = region((TAIL - 8) * SEQ, TILE)

        tile_loaded = [sem(f"tile_loaded{s}") for s in range(RING)]
        tiles_used = sem("tiles_used")
        banks_free = sem("banks_free")
        vecs_in = sem("vecs_in")
        x_in = sem("x_in")
        pool_steps = sem("pool_steps")
        consts_ready = sem("consts_ready")
        dve_steps = sem("dve_steps")
        act_steps = sem("act_steps")
        squares = sem("squares")
        sums = sem("sums")
        var_ready = sem("var_ready")
        rstd_ready = sem("rstd_ready")
        h_ready = sem("h_ready")
        modw_in = [sem(f"modw_in{s}") for s in range(2)]
        modw_used = sem("modw_used")
        c_ready = sem("c_ready")
        mod_summed = sem("mod_summed")
        flog = sem("flog")
        flog_in = sem("flog_in")
        flog_abs = sem("flog_abs")
        flog_ln = sem("flog_ln")
        decay_ready = sem("decay_ready")
        head_sq = sem("head_sq")
        head_sum = sem("head_sum")
        head_var = sem("head_var")
        head_rstd = sem("head_rstd")
        qk_ready = sem("qk_ready")
        stage_zero = sem("stage_zero")
        sb_staged, sb_z, sb_soft, sb_v, sb_log, sb_after, sb_logw, sb_expw, sb_w, sb_out = (
            sem("sb_" + n) for n in "staged z soft v log after logw expw w out".split())
        fa_staged, fa_scores, fa_v, fa_max, fa_exp, fa_p, fa_pt, fa_ptc, fa_out = (
            sem("fa_" + n) for n in "staged scores v max exp p pt ptc out".split())
        ma_staged, ma_scores, ma_v, ma_max, ma_exp, ma_p, ma_pt, ma_ptc, ma_out = (
            sem("ma_" + n) for n in "staged scores v max exp p pt ptc out".split())
        msq, msum, mvar, mrstd, merged_ready = (sem("m_" + n) for n in "sq sum var rstd ready".split())
        x1_ready = sem("x1_ready")
        keys_in = sem("keys_in")
        sx_done = sem("sx_done")
        sx_copied = sem("sx_copied")
        best_ready, best_exp, picks_done, picks_turned, picks_ready = (
            sem("pk_" + n) for n in "best exp done turned ready".split())
        hots, weighted, gates_done, gates_used = (sem("g_" + n) for n in "hots weighted done used".split())
        experts_done = sem("experts_done")
        x2_ready = sem("x2_ready")
        ang_ready, sin_ready, rot_sq, swapped, rot_done = (sem("r_" + n) for n in "ang sin sq swapped done".split())
        lam_in, lam_a, lam_b, lam_c, lam_d = (sem("l_" + n) for n in "in a b c d".split())
        bc_in, bc_used, s5_u, s5_bu, s5_angr, s5_sinr, s5_x, s5_y, s5_ys, s5_gel = (
            sem("s5_" + n) for n in "bcin bcused u bu ang sin x y ys gelu".split())
        glu_ready = sem("glu_ready")
        gated = sem("gated")
        m_done = sem("m_done")
        x3_ready = sem("x3_ready")
        up_pre, up_silu, act_ready = (sem("up_" + n) for n in "pre silu ready".split())
        y_ready = sem("y_ready")
        y_out = sem("y_out")

        block = ctx.enter_context(nc.Block())
        stage = lambda n: n <= last_stage

        @block.sync
        def _(sp):
            sp.dma_start(xT[:, :, :], d["x"]).then_inc(x_in, 16)
            sp.dma_start(vecs[:, :], d["vecs"]).then_inc(vecs_in, 16)
            sp.dma_start(wf[:, :, :], d["w_f"]).then_inc(vecs_in, 16)
            done_at = {"w_in": 1, "w_out": 4, "w_query": 5, "peer_u": 6, "peer_v": 7, "w_in_2": 8, "w_glu": 11,
                       "w_attn_br": 11, "w_ssm_br": 11, "w_out_2": 11, "w_up": 12, "w_down": 12}
            for name, tiles, cols in STREAM:
                if not stage(done_at[name]):
                    continue
                with sp.Fori(0, tiles // RING) as g:
                    for s in range(RING):
                        sp.wait_ge(tiles_used, g * RING + FIRST[name] + s + 1)
                        sp.dma_start(ring[:, s, 0:cols], d[name][g * RING + s]).then_inc(tile_loaded[s], 16)
            if stage(12):
                sp.wait_ge(y_ready, 16)
                sp.dma_start(out, xT[:, :, META:]).then_inc(y_out, 16)
                sp.wait_ge(y_out, 16)

        @block.gpsimd
        def _(pool):
            s = Steps(pool, pool_steps)
            s.link(pool.memset(ident[:, :], 0.0))
            s.link(pool.memset(later[:, :], 1.0))
            s.link(pool.memset(swap[:, :], 0.0))
            s.link(pool.memset(causal[:, :, :], 0.0))
            s.link(pool.memset(seen[:, :, :], 1.0))
            s.link(pool.affine_select(out=ident[:, :], in_=ident[:, :], compare_op=ALU.not_equal, fill=1.0,
                                      base=0, pattern=[[-1, P]], channel_multiplier=1))
            s.link(pool.affine_select(out=later[:, :], in_=later[:, :], compare_op=ALU.is_gt, fill=0.0,
                                      base=0, pattern=[[-1, P]], channel_multiplier=1))
            for shift in (64, -64):
                s.link(pool.affine_select(out=swap[:, :], in_=swap[:, :], compare_op=ALU.not_equal, fill=1.0,
                                          base=shift, pattern=[[-1, P]], channel_multiplier=1))
            s.link(pool.affine_select(out=causal[:, :, :], in_=causal[:, :, :], compare_op=ALU.is_ge, fill=NEG,
                                      base=META, pattern=[[P, 2], [-1, KEYS]], channel_multiplier=1))
            s.link(pool.affine_select(out=seen[:, :, :], in_=seen[:, :, :], compare_op=ALU.is_gt, fill=0.0,
                                      base=META, pattern=[[-P, 3], [1, SEQ]], channel_multiplier=-1))
            pool.iota(ramp[:, :], pattern=[[1, SEQ]], base=0, channel_multiplier=0,
                      allow_small_or_imprecise_dtypes=True).then_inc(consts_ready, 1)
            if stage(1):
                with pool.Fori(0, N_MOD) as part:
                    for kc in range(KC):
                        pool.wait_ge(modw_used, part * KC + kc + 1)
                        pool.dma_start(modring[:, kc % 2, :], d["w_mod"][part * KC + kc]).then_inc(modw_in[kc % 2], 16)
            if stage(2):
                pool.wait_ge(mod_summed, 1)
                s.link(pool.memset(pickh[:, :, :], 0.0))
                pool.affine_select(out=pickh[:, :, :], in_=pickh[:, :, :], compare_op=ALU.not_equal, fill=1.0,
                                   base=0, pattern=[[-1, HEADS], [0, KEYS]],
                                   channel_multiplier=1).then_inc(stage_zero, 1)
            if stage(7):
                with pool.Fori(0, SEQ // 8) as g:
                    for b in range(2):
                        pool.wait_ge(hots, g * 4 + b * 2 + 2)
                        pool.tensor_tensor(oneA[:, b, :, :], oneA[:, b, :, :],
                                           picked[:, 2, bass.ds(g * 8 + b * 4, 4)].unsqueeze(2).to_broadcast([P, 4, P]),
                                           ALU.mult).then_inc(weighted, 1)
            if stage(10):
                pool.wait_ge(ma_out, HEADS)
                with pool.Fori(0, 8) as k:
                    pool.wait_ge(bc_used, k + 1)
                    pool.dma_start(bst[:, :, :], d["s5_b"][k]).then_inc(bc_in, 16)
                    pool.dma_start(cst[:, :, :, :], d["s5_c"][k]).then_inc(bc_in, 16)

        @block.tensor
        def _(pe):
            def sum_features(of, n, bank, width, at, sem_in, value, sem_out):
                pe.wait_ge(sem_in, value)
                for c in range(n):
                    last = pe.matmul(PS[:, bank, at:at + width], ones[:, :], of[:, c, :], start=c == 0, stop=c == n - 1)
                last.then_inc(sem_out, 1)

            def dense(name, chunk0, rhs, turns=None):
                tiles = dict((n, t) for n, t, _ in STREAM)[name]
                t0 = FIRST[name]
                with pe.Fori(*(turns or (0, tiles // RING))) as g:
                    for s in range(RING):
                        pe.wait_ge(tile_loaded[s], (g + (t0 // RING + 1)) * 16)
                        pe.wait_ge(banks_free, g * RING + chunk0 + s + 1)
                        w = rhs(0).shape[-1]
                        for kc in range(KC):
                            last = pe.matmul(PS[:, s, 0:w], ring[:, s, kc * P:(kc + 1) * P], rhs(kc),
                                             start=kc == 0, stop=kc == KC - 1)
                        last.then_inc(tiles_used, 1)

            def dense_half(name, chunk0, rhs):
                tiles = dict((n, t) for n, t, _ in STREAM)[name]
                t0 = FIRST[name]
                with pe.Fori(0, tiles // RING) as g:
                    for s in range(RING):
                        pe.wait_ge(tile_loaded[s], (g + (t0 // RING + 1)) * 16)
                        for half in range(2):
                            bank = (2 * s + half) % 4
                            pe.wait_ge(banks_free, g * 2 * RING + chunk0 + 2 * s + half + 1)
                            for kc in range(8):
                                last = pe.matmul(PS[:, bank, 0:SEQ], ring[:, s, (half * 8 + kc) * P:(half * 8 + kc + 1) * P],
                                                 rhs(kc), start=kc == 0, stop=kc == 7)
                        last.then_inc(tiles_used, 1)

            def softmax_heads(a, keys, kbase, src, staged, scores, v_ready, p_ready, pt, ptc, done, decays):
                nk = -(-keys // P)
                width = [min(P, keys - P * j) for j in range(nk)]
                with pe.Fori(0, HEADS) as h:
                    pe.wait_ge(staged, h * 2 + 2)
                    for t in range(2):
                        pe.matmul(PS[:, t, 0:keys], a["q"][:, t * P:(t + 1) * P], src[:, h + kbase, 0:keys],
                                  start=True, stop=not decays)
                        if decays:
                            pe.matmul(PS[:, t, 0:keys], sumf[:, META + t * P:META + (t + 1) * P], pickh[:, h, :],
                                      start=False, stop=False)
                            pe.matmul(PS[:, t, 0:keys], ones[0:HEADS, :], negf[:, h, :], start=False, stop=True)
                    for j in range(nk):
                        last = pe.transpose(PS[0:width[j], 2, j * P:(j + 1) * P],
                                            a["v"][:, j * P:j * P + width[j]], ident[:, :])
                    last.then_inc(scores, 1)
                    pe.wait_ge(p_ready, h + 1)
                    for t in range(2):
                        for j in range(nk):
                            last = pe.transpose(PS[0:width[j], 3 + j // 2, (j % 2) * SEQ + t * P:(j % 2) * SEQ + (t + 1) * P],
                                                a["P"].rearrange("p (t s) -> p t s", t=2)[:, t, j * P:j * P + width[j]],
                                                ident[:, :])
                    last.then_inc(pt, 1)
                    pe.wait_ge(ptc, h * (nk - 1) + nk - 1)
                    pe.wait_ge(v_ready, h * (nk - 1) + nk - 1)
                    for j in range(nk):
                        last = pe.matmul(PS[:, 5, 0:SEQ], a["vn"][0:width[j], j * P:(j + 1) * P],
                                         a["PT"][0:width[j], j * SEQ:(j + 1) * SEQ], start=j == 0, stop=j == nk - 1)
                    last.then_inc(done, 1)

            pe.wait_ge(consts_ready, 2)
            if stage(1):
                sum_features(hT, KC, 7, KEYS, 0, squares, 1, sums)
                pe.wait_ge(h_ready, KC)
                dense("w_in", 0, lambda kc: hT[:, kc, :])
                pe.wait_ge(modw_used, N_MOD * KC + 2)
                for n in range(N_MOD * KC):
                    last = pe.matmul(PS[:, 6, n:n + 1], modacc[:, n // KC, (n % KC) * P:(n % KC + 1) * P], ones[:, 0:1],
                                     start=True, stop=True)
                last.then_inc(mod_summed, 1)
            if stage(2):
                for kc in range(KC):
                    last = pe.matmul(PS[0:HEADS, 5, 0:KEYS], wf[:, kc, :], hT[:, kc, :], start=kc == 0, stop=kc == KC - 1)
                last.then_inc(flog, 1)
                pe.wait_ge(head_sq, 1)
                pe.wait_ge(banks_free, 4 + 56)
                for n in range(16):
                    if n >= 4:
                        pe.wait_ge(head_var, n - 3)
                    pe.matmul(PS[:, n % 4, 0:KEYS], ones[:, :], sq1[:, n, :], start=True, stop=True).then_inc(head_sum, 1)
                with pe.Fori(0, HEADS) as h:
                    pe.wait_ge(sb_staged, h * 3 + 3)
                    for j in range(3):
                        pe.matmul(PS[:, j // 2, (j % 2) * SEQ:(j % 2 + 1) * SEQ], a1["k"][:, j * P:(j + 1) * P], a1["q"],
                                  start=True, stop=True)
                    for j in range(3):
                        last = pe.transpose(PS[:, 2, j * P:(j + 1) * P], a1["v"][:, j * P:(j + 1) * P], ident[:, :])
                    last.then_inc(sb_z, 1)
                    pe.wait_ge(sb_log, h + 1)
                    for j in range(3):
                        for k in range(j, 3):
                            last = pe.matmul(PS[:, 3 + j // 2, (j % 2) * SEQ:(j % 2 + 1) * SEQ],
                                             later[:, :] if k == j else ones[:, :], a1["L"][:, k * SEQ:(k + 1) * SEQ],
                                             start=k == j, stop=k == 2)
                    last.then_inc(sb_after, 1)
                    pe.wait_ge(sb_v, h + 1)
                    pe.wait_ge(sb_w, h + 1)
                    for j in range(3):
                        last = pe.matmul(PS[:, 5, 0:SEQ], a1["vn"][:, j * P:(j + 1) * P], a1["w"][:, j * SEQ:(j + 1) * SEQ],
                                         start=j == 0, stop=j == 2)
                    last.then_inc(sb_out, 1)
            if stage(3):
                pe.wait_ge(stage_zero, 1)
                softmax_heads(a1, KEYS, 32, p1, fa_staged, fa_scores, fa_v, fa_p, fa_pt, fa_ptc, fa_out, True)
            if stage(4):
                for part in range(2):
                    pe.wait_ge(msq, 2)
                    for c in range(8):
                        last = pe.matmul(PS[:, 7, part * SEQ:(part + 1) * SEQ], ones[:, :],
                                         sq1[:, part * 8 + c, 0:SEQ], start=c == 0, stop=c == 7)
                    last.then_inc(msum, 1)
                pe.wait_ge(merged_ready, 2)
                dense("w_out", 56, lambda kc: hT[:, kc, META:])
            if stage(5):
                sum_features(hT[:, :, META:], KC, 7, SEQ, 0, squares, 2, sums)
                pe.wait_ge(h_ready, 2 * KC)
                dense("w_query", 72, lambda kc: hT[:, kc, META:])
                pe.wait_ge(banks_free, 4 + 88)
                pe.wait_ge(keys_in, 16)
                for n in range(8):
                    t, q4 = n // 4, n % 4
                    for k in range(4):
                        hp = q4 * 4 + k
                        last = pe.matmul(PS[:, n, k * P:(k + 1) * P], qx[:, hp, t * P:(t + 1) * P],
                                         keysx[:, hp * P:(hp + 1) * P], start=True, stop=True)
                    last.then_inc(sx_done, 1)
            if stage(6):
                pe.wait_ge(sx_copied, 8)
                dense("peer_u", 88, lambda kc: hT[:, kc, META:], (0, TAIL // RING))
                pe.wait_ge(picks_done, 48)
                for n in range(6):
                    pe.transpose(PS[:, 4 + n // 4, (n % 4) * P:(n % 4 + 1) * P], sel[:, n % 3, n // 3, :],
                                 ident[:, :]).then_inc(picks_turned, 1)
                dense("peer_u", 88, lambda kc: hT[:, kc, META:], (TAIL // RING, N_SUB // RING))
            if stage(7):
                with pe.Fori(0, SEQ // 8) as g:
                    for b in range(2):
                        pe.wait_ge(weighted, g * 2 + b + 1)
                        pe.wait_ge(gates_used, g * 2 + b + 1)
                        for k in range(4):
                            last = pe.matmul(PS[:, b, k * P:(k + 1) * P], oneA[:, b, k, :], oneB[:, b, k, :],
                                             start=True, stop=True)
                        last.then_inc(gates_done, 1)
                pe.wait_ge(gates_used, 2 + SEQ // 4)

                def expert_tile(s, rhs, first):
                    for m in range(KC):
                        last = pe.matmul(PS[:, m // 2, (m % 2) * SEQ:(m % 2 + 1) * SEQ], ring[:, s, m * P:(m + 1) * P],
                                         rhs, start=first and m % 2 == 0, stop=False, skip_group_check=True)
                    last.then_inc(tiles_used, 1)

                t0 = FIRST["peer_v"]
                for s in range(RING):
                    pe.wait_ge(tile_loaded[s], (t0 // RING + 1) * 16)
                    expert_tile(s, ga[:, s, :], s == 0)
                with pe.Fori(1, N_SUB // RING) as g:
                    for s in range(RING):
                        pe.wait_ge(tile_loaded[s], (g + (t0 // RING + 1)) * 16)
                        expert_tile(s, ga[:, g * RING + s, :], False)
            if stage(8):
                pe.wait_ge(experts_done, 1)
                sum_features(hT[:, :, META:], KC, 7, SEQ, 0, squares, 3, sums)
                pe.wait_ge(h_ready, 3 * KC)
                dense("w_in_2", 216, lambda kc: hT[:, kc, META:])
                pe.wait_ge(head_sq, 2)
                pe.wait_ge(banks_free, 4 + 280)
                for n in range(16):
                    if n >= 4:
                        pe.wait_ge(head_var, 17 + n - 3)
                    pe.matmul(PS[:, n % 4, 0:SEQ], ones[:, :], sq2[:, n, :], start=True, stop=True).then_inc(head_sum, 1)
            if stage(9):
                pe.wait_ge(qk_ready, 4)
                with pe.Fori(0, 8) as g:
                    for b in range(2):
                        pe.wait_ge(rot_done, g * 2 + b + 1)
                        pe.matmul(PS[:, b, 0:SEQ], swap[:, :], p2[:, g * 2 + b, :], start=True, stop=True).then_inc(swapped, 1)
                softmax_heads(a2, SEQ, 8, p2, ma_staged, ma_scores, ma_v, ma_p, ma_pt, ma_ptc, ma_out, False)
            if stage(10):
                with pe.Fori(0, 8) as k:
                    pe.wait_ge(bc_in, k * 32 + 32)
                    pe.wait_ge(s5_u, k + 1)
                    for q in range(4):
                        for part in range(2):
                            last = pe.matmul(PS[:, q, part * SEQ:(part + 1) * SEQ],
                                             bst[32 * q:32 * q + 32, part, :], ust[32 * q:32 * q + 32, :],
                                             start=True, stop=True)
                    last.then_inc(s5_bu, 1)
                    pe.wait_ge(s5_x, k + 1)
                    for q in range(4):
                        pe.matmul(PS[32 * q:32 * q + 32, 4, 0:SEQ], cc[:, 0, q, :], s5_xr[:, q, :], start=True, stop=False)
                        last = pe.matmul(PS[32 * q:32 * q + 32, 4, 0:SEQ], cc[:, 1, q, :], s5_xi[:, q, :],
                                         start=False, stop=True)
                    last.then_inc(s5_y, 1)
            if stage(11):
                pe.wait_ge(s5_gel, 8)
                dense_half("w_glu", 280, lambda kc: p2[:, 24 + kc, :])
                dense_half("w_attn_br", 288, lambda kc: p2[:, kc, :])
                pe.wait_ge(glu_ready, 1)
                dense_half("w_ssm_br", 304, lambda kc: p2[:, 24 + kc, :])
                pe.wait_ge(m_done, 16)
                dense("w_out_2", 320, lambda kc: hT[:, kc, META:])
            if stage(12):
                sum_features(hT[:, :, META:], KC, 7, SEQ, 0, squares, 4, sums)
                pe.wait_ge(h_ready, 4 * KC)
                dense("w_up", 336, lambda kc: hT[:, kc, META:])
                pe.wait_ge(act_ready, FC + 1)
                t0 = FIRST["w_down"]
                with pe.Fori(0, 8) as g:
                    for half in range(2):
                        pe.wait_ge(banks_free, g * 2 + (424 + half + 3))
                        for s in range(RING):
                            pe.wait_ge(tile_loaded[s], (g * 2 + (half + t0 // RING + 1)) * 16)
                            for k in range(DOWN_KC):
                                last = pe.matmul(PS[:, half, 0:SEQ], ring[:, s, k * P:(k + 1) * P],
                                                 act[:, s * DOWN_KC + k, :], start=s == 0 and k == 0,
                                                 stop=s == RING - 1 and k == DOWN_KC - 1)
                            last.then_inc(tiles_used, 1)

        @block.scalar
        def _(sc):
            s = Steps(sc, act_steps)
            f = sc.activation

            def copy_out(name, chunk0, tiles, at, dst, func, width):
                with sc.Fori(0, tiles // 4) as g:
                    for k in range(4):
                        sc.wait_ge(tiles_used, g * 4 + (RING + FIRST[name] + at + k + 1))
                        f(dst(g * 4 + (at + k)), PS[:, k, 0:width], func).then_inc(banks_free, 1)

            def root(n):
                sc.wait_ge(var_ready, n)
                f(rstd[:, 0, :], rstd[:, 0, :], ACT.Sqrt).then_inc(rstd_ready, 1)

            def softmax_heads(a, keys, scores, v_ready, mx, ex, pt, ptc):
                nk = -(-keys // P)
                Pm = a["P"].rearrange("p (t s) -> p t s", t=2)
                with sc.Fori(0, HEADS) as h:
                    sc.wait_ge(scores, h + 1)
                    f(a["vn"][:, 0:SEQ], PS[:, 2, 0:SEQ], ACT.Copy).then_inc(v_ready, 1)
                    if nk == 3:
                        f(a["vn"][0:META, SEQ:SEQ + P], PS[0:META, 2, SEQ:SEQ + P], ACT.Copy).then_inc(v_ready, 1)
                    sc.wait_ge(mx, h + 1)
                    for t in range(2):
                        f(Pm[:, t, 0:keys], Pm[:, t, 0:keys], ACT.Exp, bias=small[:, 2 + t:3 + t],
                          accum_out=small[:, 4 + t:5 + t]).then_inc(ex, 1)
                    sc.wait_ge(pt, h + 1)
                    f(a["PT"][:, 0:2 * SEQ], PS[:, 3, :], ACT.Copy).then_inc(ptc, 1)
                    if nk == 3:
                        f(a["PT"][0:META, 2 * SEQ:3 * SEQ], PS[0:META, 4, 0:SEQ], ACT.Copy).then_inc(ptc, 1)

            sc.wait_ge(vecs_in, 32)
            sc.wait_ge(x_in, 16)
            if stage(1):
                f(small[:, 8:24], vecs[:, V_C:V_C + KC], ACT.Silu).then_inc(c_ready, 1)
                f(hT[:, :, :], xT[:, :, :], ACT.Square).then_inc(squares, 1)
                root(1)
                copy_out("w_in", 0, 48, 0, lambda c: p1[:, c, :], ACT.Copy, KEYS)
                copy_out("w_in", 0, 8, 48, lambda c: p1[:, c, :], ACT.Sigmoid, KEYS)
            if stage(2):
                sc.wait_ge(flog_in, 1)
                s.link(f(logt, logf, ACT.Abs))
                s.link(f(logt, logt, ACT.Exp, scale=-1.0))
                f(logt, logt, ACT.Ln, bias=1.0).then_inc(flog_ln, 1)
                sc.wait_ge(mod_summed, 1)
                sc.wait_ge(banks_free, 4 + 56)
                f(sq1[:, :, :], p1[:, 24:40, :], ACT.Square).then_inc(head_sq, 1)
                sc.wait_ge(head_var, 17)
                f(rs1[:, :, :], rs1[:, :, :], ACT.Sqrt).then_inc(head_rstd, 1)
                with s.loop(HEADS, 2) as h:
                    sc.wait_ge(sb_z, h + 1)
                    s.link(f(a1["a"], PS[:, 0:2, :].rearrange("p a b -> p (a b)")[:, 0:768], ACT.Abs))
                    s.link(f(a1["e"], a1["a"], ACT.Exp, scale=-1.0))
                    f(a1["e"], a1["e"], ACT.Ln, bias=1.0).then_inc(sb_soft, 1)
                    f(a1["vn"], PS[:, 2, 0:384], ACT.Copy).then_inc(sb_v, 1)
                    sc.wait_ge(sb_logw, h + 1)
                    f(a1["w"], a1["w"], ACT.Exp).then_inc(sb_expw, 1)
            if stage(3):
                softmax_heads(a1, KEYS, fa_scores, fa_v, fa_max, fa_exp, fa_pt, fa_ptc)
            if stage(4):
                sc.wait_ge(fa_ptc, 16)
                sc.wait_ge(fa_staged, 17)
                f(sq1[:, 0:8, 0:SEQ], p1[:, 0:8, META:], ACT.Square).then_inc(msq, 1)
                f(sq1[:, 8:16, 0:SEQ], p1[:, 24:32, META:], ACT.Square).then_inc(msq, 1)
                sc.wait_ge(mvar, 1)
                sc.dma_start(keysx[:, :], d["keys"]).then_inc(keys_in, 16)
                f(rstd[:, :, 0:SEQ], rstd[:, :, 0:SEQ], ACT.Sqrt).then_inc(mrstd, 1)
            if stage(5):
                sc.wait_ge(banks_free, 4 + 72)
                f(hT[:, :, META:], xT[:, :, META:], ACT.Square).then_inc(squares, 1)
                root(2)
                copy_out("w_query", 72, 16, 0, lambda c: qx[:, c, :], ACT.Copy, SEQ)
                for n in range(8):
                    sc.wait_ge(sx_done, n + 1)
                    f(sx[:, n // 4, (n % 4) * 4:(n % 4) * 4 + 4, :],
                      PS[:, n, :].rearrange("p (a b) -> p a b", a=4), ACT.Copy).then_inc(sx_copied, 1)
            if stage(6):
                def gelu_out(start, turns):
                    with sc.Fori(0, turns) as g:
                        for k in range(4):
                            sc.wait_ge(tiles_used, g * 4 + (RING + FIRST["peer_u"] + start + k + 1))
                            f(ga[:, g * 4 + (start + k), :], PS[:, k, 0:SEQ], ACT.Gelu).then_inc(banks_free, 1)
                with sc.Fori(0, 16) as u:
                    sc.wait_ge(best_ready, u + 1)
                    f(best, best, ACT.Exp, bias=small[:, 6:7], accum_out=small[:, 7:8]).then_inc(best_exp, 1)
                    for k in range(4):
                        sc.wait_ge(tiles_used, u * 4 + (RING + FIRST["peer_u"] + k + 1))
                        f(ga[:, u * 4 + k, :], PS[:, k, 0:SEQ], ACT.Gelu).then_inc(banks_free, 1)
                gelu_out(64, (TAIL - 64) // 4)
                sc.wait_ge(picks_ready, 6)
                gelu_out(TAIL, (N_SUB - TAIL) // 4)
            if stage(8):
                sc.wait_ge(experts_done, 1)
                sc.wait_ge(x2_ready, 1)
                sc.dma_start(convw, d["convw"]).then_inc(lam_in, 16)
                sc.dma_start(posi, d["pos"]).then_inc(lam_in, 16)
                sc.dma_start(lamp[:, 0:3, :], d["lam"]).then_inc(lam_in, 16)
                f(hT[:, :, META:], xT[:, :, META:], ACT.Square).then_inc(squares, 1)
                root(3)
                copy_out("w_in_2", 216, 32, 0, lambda c: p2[:, c, :], ACT.Copy, SEQ)
                copy_out("w_in_2", 216, 32, 32, lambda c: p2[:, c, :], ACT.Sigmoid, SEQ)
                sc.wait_ge(banks_free, 4 + 280)
                f(sq2[:, :, :], p2[:, 0:16, :], ACT.Square).then_inc(head_sq, 1)
                sc.wait_ge(head_var, 17 + 17)
                f(rs2[:, :, :], rs2[:, :, :], ACT.Sqrt).then_inc(head_rstd, 1)
            if stage(9):
                sc.wait_ge(ang_ready, 1)
                s.link(f(sinr, angr, ACT.Sin))
                s.link(f(cosr, angr, ACT.Sin, scale=0.5))
                f(cosr, cosr, ACT.Square).then_inc(sin_ready, 1)
                softmax_heads(a2, SEQ, ma_scores, ma_v, ma_max, ma_exp, ma_pt, ma_ptc)
            if stage(10):
                sc.wait_ge(lam_in, 48)
                f(lamp[:, 2, :], lamp[:, 2, :], ACT.Exp).then_inc(lam_a, 1)
                sc.wait_ge(lam_b, 1)
                f(lamp[:, 3, :], lamp[:, 3, :], ACT.Exp).then_inc(lam_c, 1)
                f(sq2[:, 12, 0:32], lamp[:, 4, :], ACT.Sin).then_inc(lam_c, 1)
                f(sq2[:, 13, 0:32], lamp[:, 4, :], ACT.Sin, scale=0.5).then_inc(lam_c, 1)
                with s.loop(8, 2) as k:
                    sc.wait_ge(s5_angr, k + 1)
                    s.link(f(s5_sin[:, :, :], s5_ang[:, :, :], ACT.Sin))
                    s.link(f(s5_cos[:, :, :], s5_ang[:, :, :], ACT.Sin, scale=0.5))
                    f(s5_cos[:, :, :], s5_cos[:, :, :], ACT.Square).then_inc(s5_sinr, 1)
                    sc.wait_ge(s5_ys, k + 1)
                    f(p2[:, k + 24, :], ysum, ACT.Gelu_apprx_tanh).then_inc(s5_gel, 1)
            if stage(11):
                for k in range(8):
                    sc.wait_ge(tiles_used, RING + FIRST["w_glu"] + k // 2 + 1)
                    f(glug[:, k, :], PS[:, k % 4, 0:SEQ], ACT.Sigmoid,
                      bias=vecs[:, V_BGLU + k:V_BGLU + k + 1]).then_inc(banks_free, 1)
            if stage(12):
                sc.wait_ge(banks_free, 4 + 336)
                f(hT[:, :, META:], xT[:, :, META:], ACT.Square).then_inc(squares, 1)
                root(4)
                with sc.Fori(0, 22) as g:
                    for k in range(4):
                        sc.wait_ge(tiles_used, g * 4 + (RING + FIRST["w_up"] + k + 1))
                        sc.wait_ge(act_ready, g * 2 + k // 2 + 1)
                        f(cva if k % 2 == 0 else cgt, PS[:, k, 0:SEQ], ACT.Identity,
                          scale=convw[:, 2, bass.ds(g * 4 + k, 1)], bias=convw[:, 3, bass.ds(g * 4 + k, 1)]).then_inc(up_pre, 1)
                        if k % 2 == 1:
                            sc.wait_ge(banks_free, g * 4 + (4 + 336 + k + 1))
                            f(cgt, cgt, ACT.Silu).then_inc(up_silu, 1)

        @block.vector
        def _(dv):
            s = Steps(dv, dve_steps)
            link = s.link

            def move(to, of):
                return dv.tensor_scalar(to, of, 1.0, None, ALU.mult)

            def hold():
                dv.memset(small[:, 30:31], 0.0)

            def normalise(turn, width, gain, shift=None):
                o = KEYS - width
                dv.wait_ge(sums, turn)
                link(dv.tensor_scalar(rstd[:, 1, 0:width], PS[:, 7, 0:width], 1.0 / D, EPS, ALU.mult, ALU.add))
                dv.reciprocal(rstd[:, 0, 0:width], rstd[:, 1, 0:width]).then_inc(var_ready, 1)
                dv.wait_ge(rstd_ready, turn)
                for c in range(KC):
                    i = dv.scalar_tensor_tensor(hT[:, c, o:], xT[:, c, o:], gain(c), rstd[:, 0, 0:width], ALU.mult, ALU.mult)
                    if shift is not None:
                        link(i)
                        i = dv.tensor_scalar(hT[:, c, o:], hT[:, c, o:], shift(c), None, ALU.add)
                    i.then_inc(h_ready, 1)

            def head_norms(turn, sq, rs, src, base, width, gains):
                for n in range(16):
                    dv.wait_ge(head_sum, turn * 16 + n + 1)
                    dv.tensor_scalar(rs[:, n, :], PS[:, n % 4, 0:width], 1.0 / P, EPS, ALU.mult, ALU.add).then_inc(head_var, 1)
                dv.wait_ge(head_var, turn * 17 + 16)
                dv.reciprocal(rs[:, :, :], rs[:, :, :]).then_inc(head_var, 1)
                dv.wait_ge(head_rstd, turn + 1)
                for half in range(2):
                    dv.scalar_tensor_tensor(src[:, base + half * 8:base + half * 8 + 8, :],
                                            src[:, base + half * 8:base + half * 8 + 8, :],
                                            vecs[:, gains[half]:gains[half] + 1], rs[:, half * 8:half * 8 + 8, :],
                                            ALU.mult, ALU.mult).then_inc(qk_ready, 1)
                dv.wait_ge(qk_ready, turn * 2 + 2)

            def softmax_heads(a, keys, src, qbase, vbase, o, staged, scores, mx, ex, p_ready, done):
                Pm = a["P"].rearrange("p (t s) -> p t s", t=2)[:, :, 0:keys]
                cm = causal[:, :, KEYS - keys:]
                with s.loop(HEADS, 4) as h:
                    dv.tensor_scalar(a["q"], src[:, h + qbase, o:], SCALE, None, ALU.mult).then_inc(staged, 1)
                    dv.tensor_copy(a["v"][:, 0:keys], src[:, h + vbase, 0:keys]).then_inc(staged, 1)
                    dv.wait_ge(scores, h + 1)
                    link(dv.tensor_tensor(Pm, PS[:, 0:2, 0:keys], cm, ALU.add))
                    link(dv.tensor_reduce(small[:, 0:2], Pm, AX.X, ALU.max))
                    dv.tensor_scalar(small[:, 2:4], small[:, 0:2], -1.0, None, ALU.mult).then_inc(mx, 1)
                    dv.wait_ge(ex, h * 2 + 2)
                    link(dv.reciprocal(small[:, 24:26], small[:, 4:6]))
                    dv.tensor_tensor(Pm, Pm, small[:, 24:26].unsqueeze(2).to_broadcast([P, 2, keys]),
                                     ALU.mult).then_inc(p_ready, 1)
                    dv.wait_ge(done, h + 1)
                    link(move(src[:, h + qbase, o:], PS[:, 5, 0:SEQ]))

            def reduce_angle(ang, num):
                link(dv.tensor_scalar(num, num, ROUND, -ROUND, ALU.add, ALU.add))
                for c in TWO_PI_PARTS:
                    link(dv.scalar_tensor_tensor(ang, num, -float(c), ang, ALU.mult, ALU.add))
                return dv.tensor_scalar(ang, ang, PI_BELOW, -PI_BELOW, ALU.min, ALU.max)

            link(dv.memset(ones[:, :], 1.0))
            link(dv.memset(rstd[:, :, :], 1.0))
            dv.memset(small[:, 26:27], 0.0).then_inc(tiles_used, RING)
            dv.memset(small[:, 27:28], 0.0).then_inc(banks_free, 4)
            dv.memset(small[:, 28:29], 0.0).then_inc(modw_used, 2)
            for n, one in enumerate((rot_done, bc_used, act_ready)):
                dv.memset(gmod[:, n:n + 1], 0.0).then_inc(one, 1)
            dv.memset(small[:, 29:30], 0.0).then_inc(consts_ready, 1)
            dv.wait_ge(consts_ready, 2)
            dv.wait_ge(vecs_in, 32)
            dv.wait_ge(x_in, 16)
            vec = lambda c: vecs[:, c:c + 1]
            if stage(1):
                normalise(1, KEYS, lambda c: vec(V_MIX + c))
                dv.wait_ge(c_ready, 1)
                with dv.Fori(0, N_MOD) as part:
                    for kc in range(KC):
                        dv.wait_ge(modw_in[kc % 2], (part * (KC // 2) + (kc // 2 + 1)) * 16)
                        dv.wait_ge(modw_used, part * KC + (kc + 2))
                        if kc == 0:
                            i = dv.tensor_scalar(modacc[:, part, :], modring[:, 0, :], small[:, 8:9], None, ALU.mult)
                        else:
                            i = dv.scalar_tensor_tensor(modacc[:, part, :], modring[:, kc % 2, :],
                                                        small[:, 8 + kc:9 + kc], modacc[:, part, :], ALU.mult, ALU.add)
                        i.then_inc(modw_used, 1)
                dv.wait_ge(mod_summed, 1)
                link(dv.tensor_tensor(mod[:, :], PS[:, 6, 0:N_MOD * KC], vecs[:, V_BMOD:V_BMOD + N_MOD * KC], ALU.add))
            if stage(2):
                dv.wait_ge(flog, 1)
                dv.tensor_scalar(logf, PS[0:HEADS, 5, 0:KEYS], vecs[0:HEADS, V_BF:V_BF + 1], None, ALU.add).then_inc(flog_in, 1)
                dv.wait_ge(flog_ln, 1)
                link(dv.scalar_tensor_tensor(logf, logf, 0.0, logt, ALU.min, ALU.subtract))
                link(dv.tensor_tensor_scan(sumf, ones[0:HEADS, 0:1].to_broadcast([HEADS, KEYS]), logf, 0.0, ALU.mult, ALU.add))
                dv.wait_ge(stage_zero, 1)
                link(dv.scalar_tensor_tensor(negf[:, :, :], pickh[:, :, :], -1.0,
                                             sumf.unsqueeze(1).to_broadcast([HEADS, HEADS, KEYS]), ALU.mult, ALU.mult))
                head_norms(0, sq1, rs1, p1, 24, KEYS, (V_QG, V_KG))
                link(dv.memset(a1["k"][:, KEYS:], 0.0))
                link(dv.memset(a1["v"][:, KEYS:], 0.0))
                z = PS[:, 0:2, :].rearrange("p a b -> p (a b)")[:, 0:768]
                after = PS[:, 3:5, :].rearrange("p a b -> p (a b)")[:, 0:768]
                seenf = seen[:, :, :].rearrange("p a b -> p (a b)")
                with s.loop(HEADS, 4) as h:
                    dv.tensor_scalar(a1["q"], p1[:, h, META:], SCALE, None, ALU.mult).then_inc(sb_staged, 1)
                    dv.tensor_copy(a1["k"][:, 0:KEYS], p1[:, h + 8, :]).then_inc(sb_staged, 1)
                    dv.tensor_copy(a1["v"][:, 0:KEYS], p1[:, h + 16, :]).then_inc(sb_staged, 1)
                    dv.wait_ge(sb_soft, h + 1)
                    link(dv.scalar_tensor_tensor(a1["L"], z, 0.0, a1["e"], ALU.max, ALU.add))
                    link(dv.tensor_tensor(a1["w"], z, a1["L"], ALU.subtract))
                    dv.scalar_tensor_tensor(a1["L"], a1["L"], -1.0, seenf, ALU.mult, ALU.mult).then_inc(sb_log, 1)
                    dv.wait_ge(sb_after, h + 1)
                    link(dv.tensor_tensor(a1["w"], a1["w"], after, ALU.add))
                    dv.tensor_scalar(a1["w"], a1["w"], 0.0, None, ALU.min).then_inc(sb_logw, 1)
                    dv.wait_ge(sb_expw, h + 1)
                    dv.tensor_tensor(a1["w"], a1["w"], seenf, ALU.mult).then_inc(sb_w, 1)
                    dv.wait_ge(sb_out, h + 1)
                    link(move(p1[:, h, META:], PS[:, 5, 0:SEQ]))
            if stage(3):
                softmax_heads(a1, KEYS, p1, 24, 40, META, fa_staged, fa_scores, fa_max, fa_exp, fa_p, fa_out)
                dv.memset(small[:, 26:27], 0.0).then_inc(fa_staged, 1)
            if stage(4):
                dv.wait_ge(msum, 2)
                link(dv.tensor_scalar(rs1[:, 0:2, 0:SEQ], PS[:, 7, :].rearrange("p (a b) -> p a b", a=2),
                                      1.0 / 1024, EPS, ALU.mult, ALU.add))
                dv.reciprocal(rstd[:, :, 0:SEQ], rs1[:, 0:2, 0:SEQ]).then_inc(mvar, 1)
                dv.wait_ge(mrstd, 1)
                for c in range(8):
                    link(dv.scalar_tensor_tensor(hT[:, c, META:], p1[:, c, META:], vec(V_SBG + c), rstd[:, 0, 0:SEQ],
                                                 ALU.mult, ALU.mult))
                    link(dv.scalar_tensor_tensor(hT[:, 8 + c, META:], p1[:, 24 + c, META:], vec(V_FOXG + c),
                                                 rstd[:, 1, 0:SEQ], ALU.mult, ALU.mult))
                dv.memset(small[:, 26:27], 0.0).then_inc(merged_ready, 1)
                dv.tensor_tensor(hT[:, 8:16, META:], hT[:, 8:16, META:], p1[:, 48:56, META:], ALU.mult).then_inc(merged_ready, 1)
                with dv.Fori(0, 4) as g:
                    for k in range(4):
                        dv.wait_ge(tiles_used, g * 4 + (RING + FIRST["w_out"] + k + 1))
                        dv.tensor_tensor(xT[:, g * 4 + k, META:], xT[:, g * 4 + k, META:], PS[:, k, 0:SEQ],
                                         ALU.add).then_inc(banks_free, 1)
            if stage(5):
                normalise(2, SEQ, lambda c: vec(V_FFN + c))
            if stage(6):
                dv.wait_ge(sx_copied, 8)
                v1, v2, vb = (small_t[:, k, :] for k in range(3))
                with s.loop(16, 28) as u:
                    t_h = sx.rearrange("p t (h s) n -> p (t h) (s n)", s=2)
                    link(move(st, t_h[:, u, :]))
                    for side, v in ((0, v1), (1, v2)):
                        a = st[:, side * N_SUB:(side + 1) * N_SUB]
                        b = st2[:, side * N_SUB:(side + 1) * N_SUB]
                        hold()
                        link(dv.max(v[:, 0:8], a))
                        hold()
                        dv.max_index(idx[:, side, 0:8], v[:, 0:8], a)
                        link(dv.match_replace(b, v[:, 0:8], a, LOWEST))
                        hold()
                        link(dv.max(v[:, 8:16], b))
                        hold()
                        link(dv.max_index(idx[:, side, 8:16], v[:, 8:16], b))
                    link(dv.tensor_copy(small_t[:, 3:5, :], idx[:, 0:2, :]))
                    c3 = cand.rearrange("p (a b) -> p a b", a=16)
                    link(dv.tensor_tensor(c3, v1.unsqueeze(2).to_broadcast([P, 16, 16]),
                                          v2.unsqueeze(1).to_broadcast([P, 16, 16]), ALU.add))
                    hold()
                    link(dv.max(vb[:, 0:8], cand))
                    link(dv.tensor_scalar(small[:, 6:7], vb[:, 0:1], -1.0, None, ALU.mult))
                    hold()
                    dv.max_index(idx[:, 2, 0:8], vb[:, 0:8], cand)
                    link(dv.match_replace(st2, vb[:, 0:8], cand, LOWEST))
                    hold()
                    link(dv.max(vb[:, 8:16], st2))
                    link(dv.tensor_copy(best, vb))
                    dv.memset(small[:, 26:27], 0.0).then_inc(best_ready, 1)
                    link(dv.max_index(idx[:, 2, 8:16], vb[:, 8:16], st2))
                    link(dv.tensor_scalar(idx[:, 0, :], idx[:, 2, :], 4, None, ALU.logical_shift_right))
                    link(dv.tensor_scalar(idx[:, 1, :], idx[:, 2, :], 15, None, ALU.bitwise_and))
                    link(dv.tensor_copy(small_t[:, 5:7, :], idx[:, 0:2, :]))
                    for side in range(2):
                        link(dv.tensor_tensor(oneh, ramp[:, 0:16].unsqueeze(1).to_broadcast([P, 16, 16]),
                                              small_t[:, 5 + side, :].unsqueeze(2).to_broadcast([P, 16, 16]), ALU.is_equal))
                        link(dv.tensor_tensor(oneh, oneh, small_t[:, 3 + side, :].unsqueeze(1).to_broadcast([P, 16, 16]),
                                              ALU.mult))
                        link(dv.tensor_reduce(small_t[:, 7 + side, :], oneh, AX.X, ALU.add))
                    dv.wait_ge(best_exp, u + 1)
                    link(dv.reciprocal(small[:, 27:28], small[:, 7:8]))
                    link(dv.tensor_scalar(small_t[:, 9, :], best, small[:, 27:28], None, ALU.mult))
                    for c in range(3):
                        move(sel8[:, c, u, :], small_t[:, 7 + c, :]).then_inc(picks_done, 1)
                dv.wait_ge(picks_turned, 6)
                for n in range(6):
                    dv.tensor_copy(picked[:, n % 3, (n // 3) * P:(n // 3 + 1) * P],
                                   PS[:, 4 + n // 4, (n % 4) * P:(n % 4 + 1) * P]).then_inc(picks_ready, 1)
            if stage(7):
                dv.wait_ge(picks_ready, 6)
                dv.wait_ge(banks_free, 4 + 216)
                dv.wait_ge(tiles_used, RING + FIRST["peer_v"])
                dv.memset(small[:, 26:27], 0.0).then_inc(gates_used, 2)

                with dv.Fori(0, SEQ // 8) as g:
                    for b in range(2):
                        for side, one in ((1, oneB), (0, oneA)):
                            dv.tensor_tensor(one[:, b, :, :], ramp[:, 0:P].unsqueeze(1).to_broadcast([P, 4, P]),
                                             picked[:, side, bass.ds(g * 8 + b * 4, 4)].unsqueeze(2).to_broadcast([P, 4, P]),
                                             ALU.is_equal).then_inc(hots, 1)
                    for b in range(2):
                        dv.wait_ge(gates_done, g * 2 + b + 1)
                        part = ga[:, :, bass.ds(g * 8 + b * 4, 4)]
                        dv.tensor_tensor(part, part, PS[:, b, :].rearrange("p (t j) -> p j t", t=4),
                                         ALU.mult).then_inc(gates_used, 1)
                dv.wait_ge(tiles_used, RING + FIRST["w_in_2"])
                link(dv.tensor_tensor(xT[:, :, META:], xT[:, :, META:],
                                      PS[:, :, :].rearrange("p a (b t) -> p (a b) t", b=2), ALU.add))
                dv.memset(small[:, 26:27], 0.0).then_inc(experts_done, 1)
                dv.memset(small[:, 27:28], 0.0).then_inc(x2_ready, 1)
            if stage(8):
                link(dv.scalar_tensor_tensor(gmod[:, :], mod[:, 16:32], 1.0, vecs[:, V_N1:V_N1 + KC], ALU.add, ALU.mult))
                normalise(3, SEQ, lambda c: gmod[:, c:c + 1], lambda c: mod[:, c:c + 1])
                head_norms(1, sq2, rs2, p2, 0, SEQ, (V_QG2, V_KG2))
            if stage(9):
                dv.wait_ge(lam_in, 48)
                link(dv.tensor_copy(numr, posi))
                link(dv.tensor_scalar(angr, numr, vec(V_FREQ), None, ALU.mult))
                link(dv.tensor_scalar(numr, angr, INV_2PI, None, ALU.mult))
                reduce_angle(angr, numr).then_inc(ang_ready, 1)
                dv.wait_ge(sin_ready, 1)
                link(dv.tensor_scalar(cosr, cosr, -2.0, 1.0, ALU.mult, ALU.add))
                link(dv.tensor_scalar(sinr[0:64, :], sinr[0:64, :], -1.0, None, ALU.mult))
                with s.loop(8, 4) as g:
                    for b in range(2):
                        dv.wait_ge(swapped, g * 2 + b + 1)
                        link(dv.tensor_tensor(numr, PS[:, b, 0:SEQ], sinr, ALU.mult))
                        link(dv.tensor_tensor(p2[:, g * 2 + b, :], p2[:, g * 2 + b, :], cosr, ALU.mult))
                        dv.tensor_tensor(p2[:, g * 2 + b, :], p2[:, g * 2 + b, :], numr, ALU.add).then_inc(rot_done, 1)
                        dv.wait_ge(rot_done, g * 2 + b + 2)
                softmax_heads(a2, SEQ, p2, 0, 16, 0, ma_staged, ma_scores, ma_max, ma_exp, ma_p, ma_out)
            if stage(10):
                lr, li, dt, mag, phi = (lamp[:, k, :] for k in range(5))
                t = [sq2[:, 8 + k, 0:32] for k in range(4)]
                sn, sh = sq2[:, 12, 0:32], sq2[:, 13, 0:32]
                cre, cim = small2[:, 0, :], small2[:, 1, :]
                dv.wait_ge(lam_a, 1)
                link(dv.tensor_tensor(mag, lr, dt, ALU.mult))
                link(dv.tensor_tensor(phi, li, dt, ALU.mult))
                link(dv.tensor_scalar(t[0], phi, INV_2PI, None, ALU.mult))
                reduce_angle(phi, t[0]).then_inc(lam_b, 1)
                dv.wait_ge(lam_c, 3)
                link(dv.tensor_tensor(t[0], sh, sh, ALU.mult))
                link(dv.tensor_tensor(t[0], t[0], mag, ALU.mult))
                link(dv.tensor_scalar(t[1], mag, -1.0, None, ALU.add))
                link(dv.scalar_tensor_tensor(t[0], t[0], -2.0, t[1], ALU.mult, ALU.add))
                link(dv.tensor_tensor(t[1], mag, sn, ALU.mult))
                link(dv.tensor_tensor(t[2], lr, lr, ALU.mult))
                link(dv.tensor_tensor(t[3], li, li, ALU.mult))
                link(dv.tensor_tensor(t[2], t[2], t[3], ALU.add))
                link(dv.reciprocal(t[3], t[2]))
                link(dv.tensor_tensor(cre, t[0], lr, ALU.mult))
                link(dv.tensor_tensor(t[2], t[1], li, ALU.mult))
                link(dv.tensor_tensor(cre, cre, t[2], ALU.add))
                link(dv.tensor_tensor(cre, cre, t[3], ALU.mult))
                link(dv.tensor_tensor(cim, t[1], lr, ALU.mult))
                link(dv.tensor_tensor(t[2], t[0], li, ALU.mult))
                link(dv.tensor_tensor(cim, cim, t[2], ALU.subtract))
                link(dv.tensor_tensor(cim, cim, t[3], ALU.mult))
                link(dv.tensor_scalar(dt, phi, INV_2PI, None, ALU.mult))
                wide = lambda v, k, n: v[:, bass.ds(k * 4, 4)].unsqueeze(2).to_broadcast([P, 4, n])
                steps = ramp[:, :].unsqueeze(1).to_broadcast([P, 4, SEQ])
                bre = PS[:, 0:4, 0:SEQ]
                bim = PS[:, 0:4, SEQ:]
                with s.loop(8, 22) as k:
                    move(ust, p2[:, k + 24, :]).then_inc(s5_u, 1)
                    dv.tensor_tensor(s5_num, steps, wide(dt, k, SEQ), ALU.mult)
                    link(dv.tensor_tensor(s5_ang, steps, wide(phi, k, SEQ), ALU.mult))
                    reduce_angle(s5_ang, s5_num).then_inc(s5_angr, 1)
                    dv.wait_ge(bc_in, k * 32 + 32)
                    link(dv.tensor_tensor(cc[:, 0, :, :], cst[:, 0, :, :], wide(cre, k, 32), ALU.mult))
                    link(dv.tensor_tensor(ct[:, 0, :, :], cst[:, 1, :, :], wide(cim, k, 32), ALU.mult))
                    link(dv.tensor_tensor(cc[:, 0, :, :], cc[:, 0, :, :], ct[:, 0, :, :], ALU.subtract))
                    link(dv.tensor_tensor(cc[:, 1, :, :], cst[:, 0, :, :], wide(cim, k, 32), ALU.mult))
                    link(dv.tensor_tensor(ct[:, 1, :, :], cst[:, 1, :, :], wide(cre, k, 32), ALU.mult))
                    link(dv.scalar_tensor_tensor(cc[:, 1, :, :], cc[:, 1, :, :], -1.0, ct[:, 1, :, :], ALU.mult, ALU.subtract))
                    dv.wait_ge(s5_sinr, k + 1)
                    link(dv.tensor_scalar(s5_cos, s5_cos, -2.0, 1.0, ALU.mult, ALU.add))
                    dv.wait_ge(s5_bu, k + 1)
                    dv.tensor_tensor(s5_p, s5_cos, bre, ALU.mult)
                    link(dv.tensor_tensor(s5_xr, s5_sin, bim, ALU.mult))
                    link(dv.tensor_tensor(s5_p, s5_p, s5_xr, ALU.add))
                    dv.tensor_tensor(s5_q, s5_cos, bim, ALU.mult)
                    link(dv.tensor_tensor(s5_xi, s5_sin, bre, ALU.mult))
                    link(dv.tensor_tensor(s5_q, s5_q, s5_xi, ALU.subtract))
                    for q in range(4):
                        decay = mag[:, bass.ds(k * 4 + q, 1)].to_broadcast([P, SEQ])
                        dv.tensor_tensor_scan(s5_zr[:, q, :], decay, s5_p[:, q, :], 0.0, ALU.mult, ALU.add)
                        i = dv.tensor_tensor_scan(s5_zi[:, q, :], decay, s5_q[:, q, :], 0.0, ALU.mult, ALU.add)
                    link(i)
                    dv.tensor_tensor(s5_xr, s5_cos, s5_zr, ALU.mult)
                    link(dv.tensor_tensor(s5_p, s5_sin, s5_zi, ALU.mult))
                    link(dv.tensor_tensor(s5_xr, s5_xr, s5_p, ALU.subtract))
                    dv.tensor_tensor(s5_xi, s5_cos, s5_zi, ALU.mult)
                    link(dv.tensor_tensor(s5_q, s5_sin, s5_zr, ALU.mult))
                    link(dv.tensor_tensor(s5_xi, s5_xi, s5_q, ALU.add))
                    dv.memset(small[:, 26:27], 0.0).then_inc(s5_x, 1)
                    dv.wait_ge(s5_y, k + 1)
                    link(dv.scalar_tensor_tensor(ysum, ust, vecs[:, bass.ds(k + V_D, 1)], PS[:, 4, 0:SEQ], ALU.mult, ALU.add))
                    dv.memset(small[:, 27:28], 0.0).then_inc(s5_ys, 1)
                    dv.wait_ge(s5_gel, k + 1)
                    dv.memset(small[:, 28:29], 0.0).then_inc(bc_used, 1)
            if stage(11):
                dv.wait_ge(bc_used, 9)
                dv.wait_ge(banks_free, 4 + 288)
                dv.tensor_tensor(p2[:, 24:32, :], p2[:, 24:32, :], glug[:, :, :], ALU.mult).then_inc(glu_ready, 1)
                with dv.Fori(0, 2) as g:
                    for k in range(8):
                        dv.wait_ge(tiles_used, g * 4 + (RING + FIRST["w_attn_br"] + k // 2 + 1))
                        dv.tensor_tensor(hT[:, g * 8 + k, META:], PS[:, k % 4, 0:SEQ], p2[:, g * 8 + (32 + k), :],
                                         ALU.mult).then_inc(banks_free, 1)
                with s.loop(2, 8) as g:
                    for k in range(8):
                        dv.wait_ge(tiles_used, g * 4 + (RING + FIRST["w_ssm_br"] + k // 2 + 1))
                        dv.tensor_tensor(mtmp[:, k % 2, :], PS[:, k % 4, 0:SEQ], p2[:, g * 8 + (48 + k), :],
                                         ALU.mult).then_inc(banks_free, 1)
                        dv.wait_ge(banks_free, g * 8 + (4 + 304 + k + 1))
                        link(dv.tensor_tensor(hT[:, g * 8 + k, META:], hT[:, g * 8 + k, META:], mtmp[:, k % 2, :], ALU.add))
                dv.memset(small[:, 26:27], 0.0).then_inc(m_done, 16)
                with dv.Fori(0, 4) as g:
                    for k in range(4):
                        dv.wait_ge(tiles_used, g * 4 + (RING + FIRST["w_out_2"] + k + 1))
                        dv.scalar_tensor_tensor(xT[:, g * 4 + k, META:], PS[:, k, 0:SEQ], mod[:, bass.ds(g * 4 + (32 + k), 1)],
                                                xT[:, g * 4 + k, META:], ALU.mult, ALU.add).then_inc(banks_free, 1)
            if stage(12):
                dv.wait_ge(banks_free, 4 + 336)
                link(dv.scalar_tensor_tensor(gmod[:, :], mod[:, 64:80], 1.0, vecs[:, V_N2:V_N2 + KC], ALU.add, ALU.mult))
                normalise(4, SEQ, lambda c: gmod[:, c:c + 1], lambda c: mod[:, 48 + c:49 + c])
                with s.loop(22, 4) as g:
                    for k in range(4):
                        dst = cva if k % 2 == 0 else cgt
                        dv.wait_ge(up_pre, g * 4 + (k + 1))
                        link(dv.scalar_tensor_tensor(dst[:, 1:], PS[:, k, 0:SEQ - 1], convw[:, 1, bass.ds(g * 4 + k, 1)],
                                                     dst[:, 1:], ALU.mult, ALU.add))
                        dv.scalar_tensor_tensor(dst[:, 2:], PS[:, k, 0:SEQ - 2], convw[:, 0, bass.ds(g * 4 + k, 1)],
                                                dst[:, 2:], ALU.mult, ALU.add).then_inc(banks_free, 1)
                        if k % 2 == 1:
                            dv.wait_ge(banks_free, g * 4 + (4 + 336 + k + 1))
                            dv.wait_ge(up_silu, g * 2 + (k // 2 + 1))
                            dv.tensor_tensor(act[:, g * 2 + k // 2, :], cva, cgt, ALU.mult).then_inc(act_ready, 1)
                with dv.Fori(0, 8) as g:
                    for half in range(2):
                        dv.wait_ge(tiles_used, g * 8 + (RING + FIRST["w_down"] + 4 * half + 4))
                        dv.scalar_tensor_tensor(xT[:, g * 2 + half, META:], PS[:, half, 0:SEQ],
                                                mod[:, bass.ds(g * 2 + (80 + half), 1)], xT[:, g * 2 + half, META:],
                                                ALU.mult, ALU.add).then_inc(banks_free, 1)
                dv.wait_ge(banks_free, 4 + 424 + 16)
                dv.memset(small[:, 26:27], 0.0).then_inc(y_ready, 16)


INPUTS = ("x", "vecs", "convw", "w_f", "keys", "pos", "lam", "s5_b", "s5_c", "w_mod") + tuple(n for n, _, _ in STREAM)


def kernel(x, meta_tokens, norm_mix, w_in, b_forget, fox_q_gain, fox_k_gain, sb_out_gain, fox_out_gain, w_out,
           norm_ffn, peer_w_query, peer_sub_keys, peer_u, peer_v, c_2, positions_2, w_mod_2, b_mod_2, norm1_g_2,
           w_in_2, q_norm_g_2, k_norm_g_2, ssm_lambda_re_2, ssm_lambda_im_2, ssm_log_dt_2, ssm_b_re_2, ssm_b_im_2,
           ssm_c_re_2, ssm_c_im_2, ssm_d_2, w_glu_2, b_glu_2, w_attn_br_2, w_ssm_br_2, w_out_2, norm2_g_2, w_up_2,
           conv_w_2, conv_b_2, w_down_2):
    import concourse.bacc as bacc
    from concourse.bass_utils import run_bass_kernel_spmd

    def columns(v):
        return np.asarray(v).reshape(-1, P).T

    def chunks(w):
        w = np.asarray(w).reshape(-1, P, w.shape[-1] // P, P)
        return w.transpose(2, 1, 0, 3).reshape(w.shape[2], P, -1)

    def half_chunks(w):
        w = chunks(w)
        return w.reshape(-1, 2, P, w.shape[-1]).transpose(0, 2, 1, 3).reshape(-1, P, TILE)

    a = {}
    rows = np.concatenate([np.asarray(meta_tokens), np.asarray(x)[0]], axis=0)
    a["x"] = rows.reshape(KEYS, KC, P).transpose(2, 1, 0)
    half = P // 2
    freq = (np.float32(10000.0) ** (-np.arange(half, dtype=np.float32) / np.float32(half))).astype(np.float32)
    bf = np.zeros((P, 1), np.float32)
    bf[:HEADS, 0] = np.asarray(b_forget)[0]
    vecs = [columns(v) for v in (norm_mix, sb_out_gain, fox_out_gain, fox_q_gain, fox_k_gain, norm_ffn, norm1_g_2,
                                 q_norm_g_2, k_norm_g_2, ssm_d_2, b_glu_2, norm2_g_2, b_mod_2, c_2)]
    vecs += [np.concatenate([freq, freq])[:, None], bf, np.zeros((P, 26), np.float32)]
    a["vecs"] = np.concatenate(vecs, axis=1)
    taps = np.concatenate([np.asarray(conv_w_2)[0], np.asarray(conv_b_2)], axis=0)
    a["convw"] = taps.reshape(4, 2, FC, P).transpose(3, 0, 2, 1).reshape(P, 4, 2 * FC)
    w_all = np.asarray(w_in)[0]
    a["w_in"] = chunks(w_all[:, :56 * P])
    a["w_f"] = w_all[:, 56 * P:].reshape(KC, P, HEADS).transpose(1, 0, 2)
    a["w_out"] = chunks(np.asarray(w_out)[0])
    a["w_query"] = chunks(np.asarray(peer_w_query)[0])
    a["keys"] = np.asarray(peer_sub_keys)[0].reshape(16 * N_SUB, P).T
    a["peer_u"] = np.asarray(peer_u)[0].reshape(N_SUB, N_SUB, KC, P).transpose(1, 3, 2, 0).reshape(N_SUB, P, TILE)
    a["peer_v"] = np.asarray(peer_v)[0].reshape(N_SUB, N_SUB, D).transpose(1, 0, 2)
    a["w_mod"] = np.asarray(w_mod_2)[0].reshape(KC, P, N_MOD, D).transpose(2, 0, 1, 3).reshape(N_MOD * KC, P, D)
    a["w_in_2"] = chunks(np.asarray(w_in_2)[0])
    a["w_glu"] = half_chunks(np.asarray(w_glu_2)[0])
    a["w_attn_br"] = half_chunks(np.asarray(w_attn_br_2)[0])
    a["w_ssm_br"] = half_chunks(np.asarray(w_ssm_br_2)[0])
    a["w_out_2"] = chunks(np.asarray(w_out_2)[0])
    a["w_up"] = chunks(np.asarray(w_up_2)[0]).reshape(2, FC, P, TILE).transpose(1, 0, 2, 3).reshape(2 * FC, P, TILE)
    down = np.asarray(w_down_2)[0].reshape(RING, DOWN_KC, P, KC, P)
    a["w_down"] = down.transpose(3, 0, 2, 1, 4).reshape(KC * RING, P, DOWN_KC * P)
    a["pos"] = np.broadcast_to(np.asarray(positions_2)[0], (P, SEQ))
    lam = [np.asarray(v)[0].reshape(32, P).T for v in (ssm_lambda_re_2, ssm_lambda_im_2)]
    lam.append(np.repeat(np.asarray(ssm_log_dt_2)[0].reshape(32, 2), half, axis=1).T)
    a["lam"] = np.stack(lam, axis=1)
    s5_b = np.zeros((8, 4, 2, 16, 2, 2, half), np.float32)
    s5_c = np.zeros((8, 2, half, 2, 4, 2, 16), np.float32)
    for part, (b, c) in enumerate(((ssm_b_re_2, ssm_c_re_2), (ssm_b_im_2, ssm_c_im_2))):
        b = np.asarray(b)[0].reshape(8, 4, 2, half, 16)
        c = np.asarray(c)[0].reshape(8, 4, 2, 16, half)
        for g in range(2):
            s5_b[:, :, g, :, part, g, :] = b[:, :, g].transpose(0, 1, 3, 2)
            s5_c[:, g, :, part, :, g, :] = c[:, :, g].transpose(0, 3, 1, 2)
    a["s5_b"] = s5_b.reshape(8, P, 2, P)
    a["s5_c"] = s5_c.reshape(8, P, 2, 4, 32)

    nc = bacc.Bacc("TRN2", target_bir_lowering=False, num_devices=1)
    drams = {}
    for name in INPUTS:
        a[name] = np.ascontiguousarray(a[name])
        drams[name] = nc.dram_tensor(name + "_dram", a[name].shape, mybir.dt.from_np(a[name].dtype),
                                     kind="ExternalInput").ap()
    y = nc.dram_tensor("y_dram", (P, KC, SEQ), F32, kind="ExternalOutput").ap()
    build(nc, drams, y)
    r = run_bass_kernel_spmd(nc, [{name + "_dram": a[name] for name in INPUTS}], core_ids=[0])
    return r.results[0]["y_dram"].transpose(2, 1, 0).reshape(1, SEQ, D)
```

```python
from contextlib import ExitStack, contextmanager

import numpy as np
import concourse.bass as bass
from concourse import mybir

F32 = mybir.dt.float32
F32R = mybir.dt.float32r
I32 = mybir.dt.int32
U32 = mybir.dt.uint32
ALU = mybir.AluOpType
ACT = mybir.ActivationFunctionType
AX = mybir.AxisListType

P = 128
SEQ = 256
META = 16
KEYS = META + SEQ
D = 2048
KC = D // P
HEADS = 8
RING = 4
HALF = 1024
PAIRS = 2
SCALE = float(P) ** -0.5
EPS = 1e-6
TOPK = 16
N_SUB = 128
SLOTS = HEADS * TOPK
FFN = 5632
FC = FFN // P
N_MOD = 6
NEG = -1e30
LOWEST = -3.0e38
ROUND = 12582912.0
INV_2PI = 0.15915494309189535
TWO_PI_PARTS = (6.28125, 2029 / 2.0**20, 2 * np.pi - 6.28125 - 2029 / 2.0**20)
PI_BELOW = 3.1415925

STREAM = [("w_in", 112), ("w_out", 32), ("w_query", 32), ("peer_u", 256), ("peer_v", 256), ("w_in_2", 128),
          ("w_glu", 8), ("w_attn_br", 16), ("w_ssm_br", 16), ("w_out_2", 32), ("w_up", 176), ("w_down", 88)]
FIRST = {}
_n = 0
for _name, _halves in STREAM:
    FIRST[_name] = _n
    _n += _halves
TOTAL = _n
SPLITS = {"h": 4, "merged": 8, "h2": 12, "h3": 16, "ys0": 17, "ya": 18, "ys": 19, "m2": 21, "h4": 25}


class Steps:

    def __init__(self, eng, sem):
        self.eng, self.sem, self.done, self.turn = eng, sem, 0, 0

    def link(self, ins):
        ins.then_inc(self.sem, 1)
        self.done += 1
        self.eng.wait_ge(self.sem, self.turn + self.done)

    @contextmanager
    def loop(self, turns, links):
        with self.eng.Fori(0, turns) as i:
            before, self.turn = self.done, i * links
            yield i
            assert self.done - before == links, (self.done - before, links)
            self.turn = 0
            self.done = before + links * turns


def quarter(q):
    return slice(q * HALF // 2, (q + 1) * HALF // 2)


def build(nc, d, out, last_stage=99):
    ctx = ExitStack()
    with ctx:
        def sb(name, shape, dt=F32):
            return ctx.enter_context(nc.sbuf_tensor(name, shape, dt))

        def sem(name):
            return ctx.enter_context(nc.semaphore(name))

        at = -(-nc.sbuf_base // 32) * 32
        arena = sb("arena", [P, 2 * KC * KEYS])
        hhi = nc.alloc_sbuf_tensor_at("hhi", [P, KC, KEYS], F32R, offset=at)
        hlo = nc.alloc_sbuf_tensor_at("hlo", [P, KC, KEYS], F32R, offset=at + KC * KEYS * 4)
        raw = sb("raw", [P, RING, HALF])
        whi = sb("whi", [P, PAIRS, HALF], F32R)
        wlo = sb("wlo", [P, PAIRS, HALF], F32R)
        big = sb("big", [P, 128 * SEQ])
        ident = sb("ident", [P, P])
        ones = sb("ones", [P, P])
        later = sb("later", [P, P])
        swap = sb("swap", [P, P])
        ramp = sb("ramp", [P, SEQ])
        causal = sb("causal", [P, 2, KEYS])
        vecs = sb("vecs", [P, 240])
        mod = sb("mod", [P, N_MOD * KC])
        gmod = sb("gmod", [P, KC])
        rstd = sb("rstd", [P, 2, KEYS])
        small = sb("small", [P, 32])
        late = sb("late", [P, 768])
        picked = late[:, :].rearrange("p (a b) -> p a b", a=3)
        convw = late[:, 0:352].rearrange("p (a b) -> p a b", a=4)
        posi = late[:, 352:608].bitcast(I32)
        lamp = late[:, 608:768].rearrange("p (a b) -> p a b", a=5)
        small_t = sb("small_t", [P, 10, 16])
        small2 = sb("small2", [P, 2, 32])
        idx = sb("idx", [P, 3, 16], U32)
        wf = sb("wf", [P, KC, HEADS])

        PS = ctx.enter_context(nc.psum_tensor("PS", [P, 8, 512], F32))

        def region(start, *shape):
            n = 1
            for s in shape:
                n *= s
            assert start + n <= 128 * SEQ
            v = big[:, start:start + n]
            if len(shape) == 1:
                return v
            names = "abcd"[:len(shape)]
            return v.rearrange(f"p ({' '.join(names)}) -> p {' '.join(names)}",
                               **{k: s for k, s in zip(names, shape)})

        V_MIX, V_SBG, V_FOXG, V_QG, V_KG, V_FFN = 0, 16, 24, 32, 33, 34
        V_N1, V_QG2, V_KG2, V_D, V_BGLU, V_N2, V_BMOD, V_C, V_FREQ, V_BF = 50, 66, 67, 68, 76, 84, 100, 196, 212, 213

        sq0 = region(0, KC, KEYS)
        x0 = region(KC * KEYS, KC, KEYS)
        h0 = region(2 * KC * KEYS, KC, KEYS)
        X1 = 128 * SEQ - KC * KEYS
        xT = region(X1, KC, KEYS)
        x2 = region(128 * SEQ - KC * SEQ, KC, SEQ)
        p1 = region(0, 56, KEYS)
        B1 = 56 * KEYS
        modring = region(B1, 2, D)
        modacc = region(B1 + 2 * D, N_MOD, D)
        seen = region(B1 + 2 * D + N_MOD * D, 3, SEQ)
        sq1 = region(B1, 16, KEYS)
        hm = region(B1 + 9000, KC, SEQ)
        rs1 = region(B1 + 16 * KEYS, 16, KEYS)
        sumf = big[0:HEADS, B1 + 32 * KEYS:B1 + 33 * KEYS]
        pickh = big[0:HEADS, B1 + 33 * KEYS:B1 + 41 * KEYS].rearrange("p (a b) -> p a b", a=HEADS)
        negf = big[0:HEADS, B1 + 41 * KEYS:B1 + 49 * KEYS].rearrange("p (a b) -> p a b", a=HEADS)
        logf = big[0:HEADS, B1 + 49 * KEYS:B1 + 50 * KEYS]
        logt = big[0:HEADS, B1 + 50 * KEYS:B1 + 51 * KEYS]

        def attention_parts(at):
            parts, out = [("q", 256), ("k", 384), ("v", 384), ("vn", 384), ("a", 768), ("e", 768), ("L", 768),
                          ("w", 768), ("P", 2 * KEYS), ("PT", 768)], {}
            for n, size in parts:
                out[n] = region(at, size)
                at += size
            return out

        a1 = attention_parts(B1)
        ga = region(0, N_SUB, SEQ)
        TAIL = 88
        qx = region(TAIL * SEQ, 16, SEQ)
        sx = region((TAIL + 16) * SEQ, 2, 16, N_SUB)
        T0 = (TAIL + 32) * SEQ
        st = region(T0, 256)
        st2 = region(T0 + 256, 256)
        cand = region(T0 + 512, 256)
        oneh = region(T0 + 768, 16, 16)
        sel = region(T0 + 1024, 3, 2, SLOTS)
        sel8 = region(T0 + 1024, 3, 2 * HEADS, TOPK)
        best = region(T0 + 1024 + 768, 16)
        hTf = arena
        oneA = hTf[:, 0:1024].rearrange("p (g t i) -> p g t i", g=2, t=4)
        oneB = hTf[:, 1024:2048].rearrange("p (g t i) -> p g t i", g=2, t=4)
        p2 = region(0, 64, SEQ)
        B2 = 64 * SEQ
        sq2 = region(B2, 16, SEQ)
        rs2 = region(B2 + 4096, 16, SEQ)
        cosr = region(B2 + 8192, SEQ)
        sinr = region(B2 + 8448, SEQ)
        angr = region(B2 + 8704, SEQ)
        numr = region(B2 + 8960, SEQ)
        a2 = attention_parts(B2)
        ust = region(B2, SEQ)
        bst = region(B2 + 256, 2, P)
        cst = region(B2 + 512, 2, 4, 32)
        cc = region(B2 + 768, 2, 4, 32)
        ct = region(B2 + 1024, 2, 4, 32)
        ysum = region(B2 + 1280, SEQ)
        s5 = [region(B2 + 1536 + 1024 * k, 4, SEQ) for k in range(10)]
        s5_ang, s5_num, s5_sin, s5_cos, s5_p, s5_q, s5_zr, s5_zi, s5_xr, s5_xi = s5
        glug = region(B2, 8, SEQ)
        mtmp = region(B2 + 2048, 2, SEQ)
        h2b = region(B2 + 2560, KC, SEQ)
        sqb = region(B2 + 6656, KC, SEQ)
        act = region(0, FC, SEQ)
        cva = region(B2, SEQ)
        cgt = region(B2 + 256, SEQ)
        keysx = region((TAIL - 8) * SEQ, D)

        raw_in = [sem(f"raw_in{s}") for s in range(RING)]
        hi_ready = sem("hi_ready")
        lo_ready = sem("lo_ready")
        quarters_used = sem("quarters_used")
        in_f32, in_hi, in_ready = sem("in_f32"), sem("in_hi"), sem("in_ready")
        stage_hi, stage_lo = sem("stage_hi"), sem("stage_lo")
        x1_saved, x1_back, x0_again = sem("x1_saved"), sem("x1_back"), sem("x0_again")
        banks_free = sem("banks_free")
        vecs_in = sem("vecs_in")
        x_in = sem("x_in")
        pool_steps = sem("pool_steps")
        consts_ready = sem("consts_ready")
        dve_steps = sem("dve_steps")
        act_steps = sem("act_steps")
        squares = sem("squares")
        sums = sem("sums")
        var_ready = sem("var_ready")
        rstd_ready = sem("rstd_ready")
        modw_in = [sem(f"modw_in{s}") for s in range(2)]
        modw_used = sem("modw_used")
        c_ready = sem("c_ready")
        mod_summed = sem("mod_summed")
        flog = sem("flog")
        flog_in = sem("flog_in")
        flog_abs = sem("flog_abs")
        flog_ln = sem("flog_ln")
        decay_ready = sem("decay_ready")
        head_sq = sem("head_sq")
        head_sum = sem("head_sum")
        head_var = sem("head_var")
        head_rstd = sem("head_rstd")
        qk_ready = sem("qk_ready")
        stage_zero = sem("stage_zero")
        sb_staged, sb_z, sb_soft, sb_v, sb_log, sb_after, sb_logw, sb_expw, sb_w, sb_out = (
            sem("sb_" + n) for n in "staged z soft v log after logw expw w out".split())
        fa_staged, fa_scores, fa_v, fa_max, fa_exp, fa_p, fa_pt, fa_ptc, fa_out = (
            sem("fa_" + n) for n in "staged scores v max exp p pt ptc out".split())
        ma_staged, ma_scores, ma_v, ma_max, ma_exp, ma_p, ma_pt, ma_ptc, ma_out = (
            sem("ma_" + n) for n in "staged scores v max exp p pt ptc out".split())
        msq, msum, mvar, mrstd, merged_ready = (sem("m_" + n) for n in "sq sum var rstd ready".split())
        x1_ready = sem("x1_ready")
        keys_in = sem("keys_in")
        sx_done = sem("sx_done")
        sx_copied = sem("sx_copied")
        best_ready, best_exp, picks_done, picks_turned, picks_ready = (
            sem("pk_" + n) for n in "best exp done turned ready".split())
        hots, weighted, gates_done, gates_used = (sem("g_" + n) for n in "hots weighted done used".split())
        experts_done = sem("experts_done")
        x2_ready = sem("x2_ready")
        ang_ready, sin_ready, rot_sq, swapped, rot_done = (sem("r_" + n) for n in "ang sin sq swapped done".split())
        lam_in, lam_a, lam_b, lam_c, lam_d = (sem("l_" + n) for n in "in a b c d".split())
        bc_in, bc_used, s5_u, s5_bu, s5_angr, s5_sinr, s5_x, s5_y, s5_ys, s5_gel = (
            sem("s5_" + n) for n in "bcin bcused u bu ang sin x y ys gelu".split())
        glu_ready = sem("glu_ready")
        gated = sem("gated")
        m_done = sem("m_done")
        x3_ready = sem("x3_ready")
        up_pre, up_silu, act_ready = (sem("up_" + n) for n in "pre silu ready".split())
        y_ready = sem("y_ready")
        y_out = sem("y_out")

        block = ctx.enter_context(nc.Block())
        stage = lambda n: n <= last_stage

        @block.sync
        def _(sp):
            sp.dma_start(x0[:, :, :], d["x"]).then_inc(x_in, 16)
            sp.dma_start(vecs[:, :], d["vecs"]).then_inc(vecs_in, 16)
            sp.dma_start(wf[:, :, :], d["w_f"]).then_inc(vecs_in, 16)
            done_at = {"w_in": 1, "w_out": 4, "w_query": 5, "peer_u": 6, "peer_v": 7, "w_in_2": 8, "w_glu": 11,
                       "w_attn_br": 11, "w_ssm_br": 11, "w_out_2": 11, "w_up": 12, "w_down": 12}
            for name, halves in STREAM:
                cutoff = not stage(done_at[name])
                with sp.Fori(0, 1 if cutoff else halves // RING) as g:
                    for s in range(RING):
                        sp.wait_ge(lo_ready, g * (2 * RING) + 2 * (FIRST[name] + s + 1))
                        sp.dma_start(raw[:, s, :], d[name][g * RING + s]).then_inc(raw_in[s], 16)
                if cutoff:
                    break
            if stage(12):
                sp.wait_ge(y_ready, 16)
                sp.dma_start(out, x2[:, :, :]).then_inc(y_out, 16)
                sp.wait_ge(y_out, 16)

        @block.gpsimd
        def _(pool):
            s = Steps(pool, pool_steps)
            s.link(pool.memset(ident[:, :], 0.0))
            s.link(pool.memset(later[:, :], 1.0))
            s.link(pool.memset(swap[:, :], 0.0))
            s.link(pool.memset(causal[:, :, :], 0.0))
            s.link(pool.memset(seen[:, :, :], 1.0))
            s.link(pool.affine_select(out=ident[:, :], in_=ident[:, :], compare_op=ALU.not_equal, fill=1.0,
                                      base=0, pattern=[[-1, P]], channel_multiplier=1))
            s.link(pool.affine_select(out=later[:, :], in_=later[:, :], compare_op=ALU.is_gt, fill=0.0,
                                      base=0, pattern=[[-1, P]], channel_multiplier=1))
            for shift in (64, -64):
                s.link(pool.affine_select(out=swap[:, :], in_=swap[:, :], compare_op=ALU.not_equal, fill=1.0,
                                          base=shift, pattern=[[-1, P]], channel_multiplier=1))
            s.link(pool.affine_select(out=causal[:, :, :], in_=causal[:, :, :], compare_op=ALU.is_ge, fill=NEG,
                                      base=META, pattern=[[P, 2], [-1, KEYS]], channel_multiplier=1))
            s.link(pool.affine_select(out=seen[:, :, :], in_=seen[:, :, :], compare_op=ALU.is_gt, fill=0.0,
                                      base=META, pattern=[[-P, 3], [1, SEQ]], channel_multiplier=-1))
            pool.iota(ramp[:, :], pattern=[[1, SEQ]], base=0, channel_multiplier=0,
                      allow_small_or_imprecise_dtypes=True).then_inc(consts_ready, 1)
            if stage(1):
                with pool.Fori(0, N_MOD) as part:
                    for kc in range(KC):
                        pool.wait_ge(modw_used, part * KC + kc + 1)
                        pool.dma_start(modring[:, kc % 2, :], d["w_mod"][part * KC + kc]).then_inc(modw_in[kc % 2], 16)
            if stage(2):
                pool.wait_ge(mod_summed, 1)
                s.link(pool.memset(pickh[:, :, :], 0.0))
                pool.affine_select(out=pickh[:, :, :], in_=pickh[:, :, :], compare_op=ALU.not_equal, fill=1.0,
                                   base=0, pattern=[[-1, HEADS], [0, KEYS]],
                                   channel_multiplier=1).then_inc(stage_zero, 1)
            if stage(7):
                with pool.Fori(0, SEQ // 8) as g:
                    for b in range(2):
                        pool.wait_ge(hots, g * 4 + b * 2 + 2)
                        pool.tensor_tensor(oneA[:, b, :, :], oneA[:, b, :, :],
                                           picked[:, 2, bass.ds(g * 8 + b * 4, 4)].unsqueeze(2).to_broadcast([P, 4, P]),
                                           ALU.mult).then_inc(weighted, 1)
            if stage(10):
                pool.wait_ge(ma_out, HEADS)
                with pool.Fori(0, 8) as k:
                    pool.wait_ge(bc_used, k + 1)
                    pool.dma_start(bst[:, :, :], d["s5_b"][k]).then_inc(bc_in, 16)
                    pool.dma_start(cst[:, :, :, :], d["s5_c"][k]).then_inc(bc_in, 16)

        @block.tensor
        def _(pe):
            def sum_features(of, n, bank, width, at, sem_in, value, sem_out):
                pe.wait_ge(sem_in, value)
                for c in range(n):
                    last = pe.matmul(PS[:, bank, at:at + width], ones[:, :], of[:, c, :], start=c == 0, stop=c == n - 1)
                last.then_inc(sem_out, 1)

            def three(out, hi, lo, rhi, rlo, start, stop, **more):
                pe.matmul(out, hi, rhi, start=start, stop=False, **more)
                pe.matmul(out, hi, rlo, start=False, stop=False, **more)
                return pe.matmul(out, lo, rhi, start=False, stop=stop, **more)

            def dense(name, chunk0, width, turns=None):
                h0_ = FIRST[name]
                o = KEYS - width
                n = dict(STREAM)[name] // 8
                with pe.Fori(*(turns or (0, n))) as g:
                    for c in range(4):
                        pe.wait_ge(banks_free, g * 4 + (chunk0 + c + 1))
                        for half in range(2):
                            for kc in range(8):
                                if kc % 4 == 0:
                                    pe.wait_ge(lo_ready, g * 16 + 2 * (RING + h0_ + 2 * c + half) + kc // 4 + 1)
                                at_ = slice(kc * P, (kc + 1) * P)
                                last = three(PS[:, c, 0:width], whi[:, half, at_], wlo[:, half, at_],
                                             hhi[:, half * 8 + kc, o:], hlo[:, half * 8 + kc, o:],
                                             half == 0 and kc == 0, half == 1 and kc == 7)
                                if kc % 4 == 3:
                                    last.then_inc(quarters_used, 1)

            def dense_half(name, chunk0, base):
                h0_ = FIRST[name]
                with pe.Fori(0, dict(STREAM)[name] // 8) as g:
                    for c in range(8):
                        pe.wait_ge(banks_free, g * 8 + (chunk0 + c + 1))
                        for kc in range(8):
                            if kc % 4 == 0:
                                pe.wait_ge(lo_ready, g * 16 + 2 * (RING + h0_ + c) + kc // 4 + 1)
                            at_ = slice(kc * P, (kc + 1) * P)
                            last = three(PS[:, c % 4, 0:SEQ], whi[:, c % 2, at_], wlo[:, c % 2, at_],
                                         hhi[:, base + kc, META:], hlo[:, base + kc, META:], kc == 0, kc == 7)
                            if kc % 4 == 3:
                                last.then_inc(quarters_used, 1)

            def spread(name, turns, first, staged):
                h0_ = FIRST[name]

                def body(g, opening):
                    for b in range(4):
                        pe.wait_ge(stage_lo, g * 4 + (staged + b + 1))
                        for half in range(2):
                            for m in range(8):
                                if m % 4 == 0:
                                    pe.wait_ge(lo_ready, g * 16 + 2 * (RING + h0_ + 2 * b + half) + m // 4 + 1)
                                mm = half * 8 + m
                                at_ = slice(m * P, (m + 1) * P)
                                last = three(PS[:, mm // 2, (mm % 2) * SEQ:(mm % 2 + 1) * SEQ], whi[:, half, at_],
                                             wlo[:, half, at_], hhi[:, b % 2, META:], hlo[:, b % 2, META:],
                                             opening and b == 0 and mm % 2 == 0, False, skip_group_check=True)
                                if m % 4 == 3:
                                    last.then_inc(quarters_used, 1)

                if first:
                    body(0, True)
                with pe.Fori(1 if first else 0, turns) as g:
                    body(g, False)

            def softmax_heads(a, keys, kbase, src, staged, scores, v_ready, p_ready, pt, ptc, done, decays):
                nk = -(-keys // P)
                width = [min(P, keys - P * j) for j in range(nk)]
                with pe.Fori(0, HEADS) as h:
                    pe.wait_ge(staged, h * 2 + 2)
                    for t in range(2):
                        pe.matmul(PS[:, t, 0:keys], a["q"][:, t * P:(t + 1) * P], src[:, h + kbase, 0:keys],
                                  start=True, stop=not decays)
                        if decays:
                            pe.matmul(PS[:, t, 0:keys], sumf[:, META + t * P:META + (t + 1) * P], pickh[:, h, :],
                                      start=False, stop=False)
                            pe.matmul(PS[:, t, 0:keys], ones[0:HEADS, :], negf[:, h, :], start=False, stop=True)
                    for j in range(nk):
                        last = pe.transpose(PS[0:width[j], 2, j * P:(j + 1) * P],
                                            a["v"][:, j * P:j * P + width[j]], ident[:, :])
                    last.then_inc(scores, 1)
                    pe.wait_ge(p_ready, h + 1)
                    for t in range(2):
                        for j in range(nk):
                            last = pe.transpose(PS[0:width[j], 3 + j // 2, (j % 2) * SEQ + t * P:(j % 2) * SEQ + (t + 1) * P],
                                                a["P"].rearrange("p (t s) -> p t s", t=2)[:, t, j * P:j * P + width[j]],
                                                ident[:, :])
                    last.then_inc(pt, 1)
                    pe.wait_ge(ptc, h * (nk - 1) + nk - 1)
                    pe.wait_ge(v_ready, h * (nk - 1) + nk - 1)
                    for j in range(nk):
                        last = pe.matmul(PS[:, 5, 0:SEQ], a["vn"][0:width[j], j * P:(j + 1) * P],
                                         a["PT"][0:width[j], j * SEQ:(j + 1) * SEQ], start=j == 0, stop=j == nk - 1)
                    last.then_inc(done, 1)

            pe.wait_ge(consts_ready, 2)
            if stage(1):
                sum_features(sq0, KC, 7, KEYS, 0, squares, 1, sums)
                pe.wait_ge(in_f32, 4)
                for kc in range(KC):
                    last = pe.matmul(PS[0:HEADS, 5, 0:KEYS], wf[:, kc, :], h0[:, kc, :], start=kc == 0, stop=kc == KC - 1)
                last.then_inc(flog, 1)
                pe.wait_ge(in_ready, SPLITS["h"])
                dense("w_in", 0, KEYS)
                pe.wait_ge(modw_used, N_MOD * KC + 2)
                for n in range(N_MOD * KC):
                    last = pe.matmul(PS[:, 6, n:n + 1], modacc[:, n // KC, (n % KC) * P:(n % KC + 1) * P], ones[:, 0:1],
                                     start=True, stop=True)
                last.then_inc(mod_summed, 1)
            if stage(2):
                pe.wait_ge(head_sq, 1)
                pe.wait_ge(banks_free, 4 + 56)
                for n in range(16):
                    if n >= 4:
                        pe.wait_ge(head_var, n - 3)
                    pe.matmul(PS[:, n % 4, 0:KEYS], ones[:, :], sq1[:, n, :], start=True, stop=True).then_inc(head_sum, 1)
                with pe.Fori(0, HEADS) as h:
                    pe.wait_ge(sb_staged, h * 3 + 3)
                    for j in range(3):
                        pe.matmul(PS[:, j // 2, (j % 2) * SEQ:(j % 2 + 1) * SEQ], a1["k"][:, j * P:(j + 1) * P], a1["q"],
                                  start=True, stop=True)
                    for j in range(3):
                        last = pe.transpose(PS[:, 2, j * P:(j + 1) * P], a1["v"][:, j * P:(j + 1) * P], ident[:, :])
                    last.then_inc(sb_z, 1)
                    pe.wait_ge(sb_log, h + 1)
                    for j in range(3):
                        for k in range(j, 3):
                            last = pe.matmul(PS[:, 3 + j // 2, (j % 2) * SEQ:(j % 2 + 1) * SEQ],
                                             later[:, :] if k == j else ones[:, :], a1["L"][:, k * SEQ:(k + 1) * SEQ],
                                             start=k == j, stop=k == 2)
                    last.then_inc(sb_after, 1)
                    pe.wait_ge(sb_v, h + 1)
                    pe.wait_ge(sb_w, h + 1)
                    for j in range(3):
                        last = pe.matmul(PS[:, 5, 0:SEQ], a1["vn"][:, j * P:(j + 1) * P], a1["w"][:, j * SEQ:(j + 1) * SEQ],
                                         start=j == 0, stop=j == 2)
                    last.then_inc(sb_out, 1)
            if stage(3):
                pe.wait_ge(stage_zero, 1)
                softmax_heads(a1, KEYS, 32, p1, fa_staged, fa_scores, fa_v, fa_p, fa_pt, fa_ptc, fa_out, True)
            if stage(4):
                for part in range(2):
                    pe.wait_ge(msq, 2)
                    for c in range(8):
                        last = pe.matmul(PS[:, 7, part * SEQ:(part + 1) * SEQ], ones[:, :],
                                         sq1[:, part * 8 + c, 0:SEQ], start=c == 0, stop=c == 7)
                    last.then_inc(msum, 1)
                pe.wait_ge(in_ready, SPLITS["merged"])
                dense("w_out", 56, SEQ)
            if stage(5):
                sum_features(sq0[:, :, META:], KC, 7, SEQ, 0, squares, 2, sums)
                pe.wait_ge(in_ready, SPLITS["h2"])
                dense("w_query", 72, SEQ)
                pe.wait_ge(banks_free, 4 + 88)
                pe.wait_ge(keys_in, 16)
                for n in range(8):
                    t, q4 = n // 4, n % 4
                    for k in range(4):
                        hp = q4 * 4 + k
                        last = pe.matmul(PS[:, n, k * P:(k + 1) * P], qx[:, hp, t * P:(t + 1) * P],
                                         keysx[:, hp * P:(hp + 1) * P], start=True, stop=True)
                    last.then_inc(sx_done, 1)
            if stage(6):
                pe.wait_ge(sx_copied, 8)
                dense("peer_u", 88, SEQ, (0, TAIL // 4))
                pe.wait_ge(picks_done, 48)
                for n in range(6):
                    pe.transpose(PS[:, 4 + n // 4, (n % 4) * P:(n % 4 + 1) * P], sel[:, n % 3, n // 3, :],
                                 ident[:, :]).then_inc(picks_turned, 1)
                dense("peer_u", 88, SEQ, (TAIL // 4, N_SUB // 4))
            if stage(7):
                with pe.Fori(0, SEQ // 8) as g:
                    for b in range(2):
                        pe.wait_ge(weighted, g * 2 + b + 1)
                        pe.wait_ge(gates_used, g * 2 + b + 1)
                        for k in range(4):
                            last = pe.matmul(PS[:, b, k * P:(k + 1) * P], oneA[:, b, k, :], oneB[:, b, k, :],
                                             start=True, stop=True)
                        last.then_inc(gates_done, 1)
                pe.wait_ge(gates_used, 2 + SEQ // 4)
                spread("peer_v", N_SUB // 4, True, 0)
            if stage(8):
                pe.wait_ge(experts_done, 1)
                sum_features(sqb, KC, 7, SEQ, 0, squares, 3, sums)
                pe.wait_ge(in_ready, SPLITS["h3"])
                dense("w_in_2", 216, SEQ)
                pe.wait_ge(head_sq, 2)
                pe.wait_ge(banks_free, 4 + 280)
                for n in range(16):
                    if n >= 4:
                        pe.wait_ge(head_var, 17 + n - 3)
                    pe.matmul(PS[:, n % 4, 0:SEQ], ones[:, :], sq2[:, n, :], start=True, stop=True).then_inc(head_sum, 1)
            if stage(9):
                pe.wait_ge(qk_ready, 4)
                with pe.Fori(0, 8) as g:
                    for b in range(2):
                        pe.wait_ge(rot_done, g * 2 + b + 1)
                        pe.matmul(PS[:, b, 0:SEQ], swap[:, :], p2[:, g * 2 + b, :], start=True, stop=True).then_inc(swapped, 1)
                softmax_heads(a2, SEQ, 8, p2, ma_staged, ma_scores, ma_v, ma_p, ma_pt, ma_ptc, ma_out, False)
            if stage(10):
                with pe.Fori(0, 8) as k:
                    pe.wait_ge(bc_in, k * 32 + 32)
                    pe.wait_ge(s5_u, k + 1)
                    for q in range(4):
                        for part in range(2):
                            last = pe.matmul(PS[:, q, part * SEQ:(part + 1) * SEQ],
                                             bst[32 * q:32 * q + 32, part, :], ust[32 * q:32 * q + 32, :],
                                             start=True, stop=True)
                    last.then_inc(s5_bu, 1)
                    pe.wait_ge(s5_x, k + 1)
                    for q in range(4):
                        pe.matmul(PS[32 * q:32 * q + 32, 4, 0:SEQ], cc[:, 0, q, :], s5_xr[:, q, :], start=True, stop=False)
                        last = pe.matmul(PS[32 * q:32 * q + 32, 4, 0:SEQ], cc[:, 1, q, :], s5_xi[:, q, :],
                                         start=False, stop=True)
                    last.then_inc(s5_y, 1)
            if stage(11):
                pe.wait_ge(in_ready, SPLITS["ys0"])
                dense_half("w_glu", 280, 0)
                pe.wait_ge(in_ready, SPLITS["ya"])
                pe.wait_ge(banks_free, 4 + 288)
                dense_half("w_attn_br", 288, 8)
                pe.wait_ge(in_ready, SPLITS["ys"])
                dense_half("w_ssm_br", 304, 0)
                pe.wait_ge(in_ready, SPLITS["m2"])
                dense("w_out_2", 320, SEQ)
            if stage(12):
                sum_features(sqb, KC, 7, SEQ, 0, squares, 4, sums)
                pe.wait_ge(in_ready, SPLITS["h4"])
                dense("w_up", 336, SEQ)
                pe.wait_ge(act_ready, FC + 1)
                spread("w_down", FC // 4, True, N_SUB)

        @block.scalar
        def _(sc):
            s = Steps(sc, act_steps)
            f = sc.activation

            def split(g, first, n):
                for k in range(2):
                    m = first + n + k
                    sc.wait_ge(raw_in[m % RING], g * 32 + 16 * (m // RING + 1))
                    for q in range(2):
                        sc.wait_ge(quarters_used, g * 16 + (2 * m + q + 1))
                        f(whi[:, m % PAIRS, quarter(q)], raw[:, m % RING, quarter(q)], ACT.Copy).then_inc(hi_ready, 1)

            def copy_out(name, chunk0, tiles, at, dst, func, width):
                with sc.Fori(0, tiles // 4) as g:
                    for k in range(4):
                        split(g, FIRST[name] + 2 * at, 2 * k + 2)
                        sc.wait_ge(quarters_used, g * 16 + 2 * (PAIRS + FIRST[name] + 2 * (at + k + 1)))
                        f(dst(g * 4 + (at + k)), PS[:, k, 0:width], func).then_inc(banks_free, 1)

            def split_only(name, tiles):
                with sc.Fori(0, tiles // 4) as g:
                    for k in range(4):
                        split(g, FIRST[name], 2 * k + 2)

            def split_input(n, src, base, group, o):
                for k in range(src.shape[1] // group):
                    sc.wait_ge(in_f32, n + k + 1)
                    f(hhi[:, base + k * group:base + (k + 1) * group, o:], src[:, k * group:(k + 1) * group, :],
                      ACT.Copy).then_inc(in_hi, 1)

            def spread_in(name, turns, of, staged, last):
                def body(g, end):
                    for k in range(4):
                        if not (end and k == 3):
                            sc.wait_ge(quarters_used, g * 16 + 2 * (PAIRS + FIRST[name] + 2 * k))
                            f(hhi[:, (k + 1) % 2, META:], of(g * 4 + (k + 1)), ACT.Copy).then_inc(stage_hi, 1)
                        if not (end and last and k == 3):
                            split(g, FIRST[name], 2 * k + 2)
                f(hhi[:, 0, META:], of(0), ACT.Copy).then_inc(stage_hi, 1)
                with sc.Fori(0, turns - 1) as g:
                    body(g, False)
                body(turns - 1, True)

            def root(n):
                sc.wait_ge(var_ready, n)
                f(rstd[:, 0, :], rstd[:, 0, :], ACT.Sqrt).then_inc(rstd_ready, 1)

            def softmax_heads(a, keys, scores, v_ready, mx, ex, pt, ptc):
                nk = -(-keys // P)
                Pm = a["P"].rearrange("p (t s) -> p t s", t=2)
                with sc.Fori(0, HEADS) as h:
                    sc.wait_ge(scores, h + 1)
                    f(a["vn"][:, 0:SEQ], PS[:, 2, 0:SEQ], ACT.Copy).then_inc(v_ready, 1)
                    if nk == 3:
                        f(a["vn"][0:META, SEQ:SEQ + P], PS[0:META, 2, SEQ:SEQ + P], ACT.Copy).then_inc(v_ready, 1)
                    sc.wait_ge(mx, h + 1)
                    for t in range(2):
                        f(Pm[:, t, 0:keys], Pm[:, t, 0:keys], ACT.Exp, bias=small[:, 2 + t:3 + t],
                          accum_out=small[:, 4 + t:5 + t]).then_inc(ex, 1)
                    sc.wait_ge(pt, h + 1)
                    f(a["PT"][:, 0:2 * SEQ], PS[:, 3, :], ACT.Copy).then_inc(ptc, 1)
                    if nk == 3:
                        f(a["PT"][0:META, 2 * SEQ:3 * SEQ], PS[0:META, 4, 0:SEQ], ACT.Copy).then_inc(ptc, 1)

            sc.wait_ge(vecs_in, 32)
            sc.wait_ge(x_in, 16)
            if stage(1):
                f(small[:, 8:24], vecs[:, V_C:V_C + KC], ACT.Silu).then_inc(c_ready, 1)
                f(sq0[:, :, :], x0[:, :, :], ACT.Square).then_inc(squares, 1)
                root(1)
                for m in range(2):
                    sc.wait_ge(raw_in[m], 16)
                    sc.wait_ge(quarters_used, 2 * m + 2)
                    f(whi[:, m, :], raw[:, m, :], ACT.Copy).then_inc(hi_ready, 2)
                split_input(0, h0, 0, 4, 0)
                copy_out("w_in", 0, 48, 0, lambda c: p1[:, c, :], ACT.Copy, KEYS)
                copy_out("w_in", 0, 8, 48, lambda c: p1[:, c, :], ACT.Sigmoid, KEYS)
            if stage(2):
                sc.wait_ge(flog_in, 1)
                s.link(f(logt, logf, ACT.Abs))
                s.link(f(logt, logt, ACT.Exp, scale=-1.0))
                f(logt, logt, ACT.Ln, bias=1.0).then_inc(flog_ln, 1)
                sc.wait_ge(mod_summed, 1)
                sc.wait_ge(banks_free, 4 + 56)
                f(sq1[:, :, :], p1[:, 24:40, :], ACT.Square).then_inc(head_sq, 1)
                sc.wait_ge(head_var, 17)
                f(rs1[:, :, :], rs1[:, :, :], ACT.Sqrt).then_inc(head_rstd, 1)
                with s.loop(HEADS, 2) as h:
                    sc.wait_ge(sb_z, h + 1)
                    s.link(f(a1["a"], PS[:, 0:2, :].rearrange("p a b -> p (a b)")[:, 0:768], ACT.Abs))
                    s.link(f(a1["e"], a1["a"], ACT.Exp, scale=-1.0))
                    f(a1["e"], a1["e"], ACT.Ln, bias=1.0).then_inc(sb_soft, 1)
                    f(a1["vn"], PS[:, 2, 0:384], ACT.Copy).then_inc(sb_v, 1)
                    sc.wait_ge(sb_logw, h + 1)
                    f(a1["w"], a1["w"], ACT.Exp).then_inc(sb_expw, 1)
            if stage(3):
                softmax_heads(a1, KEYS, fa_scores, fa_v, fa_max, fa_exp, fa_pt, fa_ptc)
            if stage(4):
                sc.wait_ge(fa_ptc, 16)
                sc.wait_ge(fa_staged, 17)
                f(sq1[:, 0:8, 0:SEQ], p1[:, 0:8, META:], ACT.Square).then_inc(msq, 1)
                f(sq1[:, 8:16, 0:SEQ], p1[:, 24:32, META:], ACT.Square).then_inc(msq, 1)
                sc.wait_ge(mvar, 1)
                sc.dma_start(keysx[:, :], d["keys"]).then_inc(keys_in, 16)
                sc.dma_start(xT[:, :, :], d["x"]).then_inc(x0_again, 16)
                f(rstd[:, :, 0:SEQ], rstd[:, :, 0:SEQ], ACT.Sqrt).then_inc(mrstd, 1)
                split_input(SPLITS["h"], hm, 0, 4, META)
                split_only("w_out", 16)
            if stage(5):
                sc.wait_ge(banks_free, 4 + 72)
                f(sq0[:, :, META:], xT[:, :, META:], ACT.Square).then_inc(squares, 1)
                sc.dma_start(d["x1"], xT[:, :, META:]).then_inc(x1_saved, 16)
                root(2)
                split_input(SPLITS["merged"], hm, 0, 4, META)
                copy_out("w_query", 72, 16, 0, lambda c: qx[:, c, :], ACT.Copy, SEQ)
                sc.wait_ge(x1_saved, 16)
                for n in range(8):
                    sc.wait_ge(sx_done, n + 1)
                    f(sx[:, n // 4, (n % 4) * 4:(n % 4) * 4 + 4, :],
                      PS[:, n, :].rearrange("p (a b) -> p a b", a=4), ACT.Copy).then_inc(sx_copied, 1)
            if stage(6):
                def gelus(g, start, k):
                    split(g, FIRST["peer_u"] + 2 * start, 2 * k + 2)
                    sc.wait_ge(quarters_used, g * 16 + 2 * (PAIRS + FIRST["peer_u"] + 2 * (start + k + 1)))
                    f(ga[:, g * 4 + (start + k), :], PS[:, k, 0:SEQ], ACT.Gelu).then_inc(banks_free, 1)

                def gelu_out(start, turns):
                    with sc.Fori(0, turns) as g:
                        for k in range(4):
                            gelus(g, start, k)
                with sc.Fori(0, 16) as u:
                    gelus(u, 0, 0)
                    gelus(u, 0, 1)
                    sc.wait_ge(best_ready, u + 1)
                    f(best, best, ACT.Exp, bias=small[:, 6:7], accum_out=small[:, 7:8]).then_inc(best_exp, 1)
                    gelus(u, 0, 2)
                    gelus(u, 0, 3)
                gelu_out(64, (TAIL - 64) // 4)
                sc.wait_ge(picks_ready, 6)
                gelu_out(TAIL, (N_SUB - TAIL) // 4)
            if stage(7):
                sc.wait_ge(gates_used, 2 + SEQ // 4)
                spread_in("peer_v", N_SUB // 4, lambda j: ga[:, j, :], 0, last_stage == 7)
                sc.wait_ge(quarters_used, 2 * (PAIRS + FIRST["w_in_2"]))
                sc.dma_start(x2[:, :, :], d["x1"]).then_inc(x1_back, 16)
            if stage(8):
                sc.wait_ge(experts_done, 1)
                sc.wait_ge(x2_ready, 1)
                sc.dma_start(convw, d["convw"]).then_inc(lam_in, 16)
                sc.dma_start(posi, d["pos"]).then_inc(lam_in, 16)
                sc.dma_start(lamp[:, 0:3, :], d["lam"]).then_inc(lam_in, 16)
                f(sqb[:, :, :], x2[:, :, :], ACT.Square).then_inc(squares, 1)
                root(3)
                split_input(SPLITS["h2"], h2b, 0, 4, META)
                copy_out("w_in_2", 216, 32, 0, lambda c: p2[:, c, :], ACT.Copy, SEQ)
                copy_out("w_in_2", 216, 32, 32, lambda c: p2[:, c, :], ACT.Sigmoid, SEQ)
                sc.wait_ge(banks_free, 4 + 280)
                f(sq2[:, :, :], p2[:, 0:16, :], ACT.Square).then_inc(head_sq, 1)
                sc.wait_ge(head_var, 17 + 17)
                f(rs2[:, :, :], rs2[:, :, :], ACT.Sqrt).then_inc(head_rstd, 1)
            if stage(9):
                sc.wait_ge(ang_ready, 1)
                s.link(f(sinr, angr, ACT.Sin))
                s.link(f(cosr, angr, ACT.Sin, scale=0.5))
                f(cosr, cosr, ACT.Square).then_inc(sin_ready, 1)
                softmax_heads(a2, SEQ, ma_scores, ma_v, ma_max, ma_exp, ma_pt, ma_ptc)
            if stage(10):
                sc.wait_ge(lam_in, 48)
                f(lamp[:, 2, :], lamp[:, 2, :], ACT.Exp).then_inc(lam_a, 1)
                sc.wait_ge(lam_b, 1)
                f(lamp[:, 3, :], lamp[:, 3, :], ACT.Exp).then_inc(lam_c, 1)
                f(sq2[:, 12, 0:32], lamp[:, 4, :], ACT.Sin).then_inc(lam_c, 1)
                f(sq2[:, 13, 0:32], lamp[:, 4, :], ACT.Sin, scale=0.5).then_inc(lam_c, 1)
                with s.loop(8, 2) as k:
                    sc.wait_ge(s5_angr, k + 1)
                    s.link(f(s5_sin[:, :, :], s5_ang[:, :, :], ACT.Sin))
                    s.link(f(s5_cos[:, :, :], s5_ang[:, :, :], ACT.Sin, scale=0.5))
                    f(s5_cos[:, :, :], s5_cos[:, :, :], ACT.Square).then_inc(s5_sinr, 1)
                    sc.wait_ge(s5_ys, k + 1)
                    f(p2[:, k + 24, :], ysum, ACT.Gelu_apprx_tanh).then_inc(s5_gel, 1)
            if stage(11):
                split_input(SPLITS["h3"], p2[:, 24:32, :], 0, 8, META)
                split_input(SPLITS["ys0"], p2[:, 0:8, :], 8, 8, META)
                for k in range(8):
                    if k % 2 == 0:
                        split(0, FIRST["w_glu"], k + 2)
                    sc.wait_ge(quarters_used, 2 * (PAIRS + FIRST["w_glu"] + k + 1))
                    f(glug[:, k, :], PS[:, k % 4, 0:SEQ], ACT.Sigmoid,
                      bias=vecs[:, V_BGLU + k:V_BGLU + k + 1]).then_inc(banks_free, 1)
                split_only("w_attn_br", 8)
                split_input(SPLITS["ya"], p2[:, 24:32, :], 0, 8, META)
                split_only("w_ssm_br", 8)
                split_input(SPLITS["ys"], h2b, 0, 8, META)
                split_only("w_out_2", 16)
            if stage(12):
                sc.wait_ge(banks_free, 4 + 336)
                f(sqb[:, :, :], x2[:, :, :], ACT.Square).then_inc(squares, 1)
                root(4)
                split_input(SPLITS["m2"], h2b, 0, 4, META)
                with sc.Fori(0, 22) as g:
                    for k in range(4):
                        split(g, FIRST["w_up"], 2 * k + 2)
                        sc.wait_ge(quarters_used, g * 16 + 2 * (PAIRS + FIRST["w_up"] + 2 * (k + 1)))
                        sc.wait_ge(act_ready, g * 2 + k // 2 + 1)
                        f(cva if k % 2 == 0 else cgt, PS[:, k, 0:SEQ], ACT.Identity,
                          scale=convw[:, 2, bass.ds(g * 4 + k, 1)], bias=convw[:, 3, bass.ds(g * 4 + k, 1)]).then_inc(up_pre, 1)
                        if k % 2 == 1:
                            sc.wait_ge(banks_free, g * 4 + (4 + 336 + k + 1))
                            f(cgt, cgt, ACT.Silu).then_inc(up_silu, 1)
                sc.wait_ge(act_ready, FC + 1)
                spread_in("w_down", FC // 4, lambda j: act[:, j, :], N_SUB, True)

        @block.vector
        def _(dv):
            s = Steps(dv, dve_steps)
            link = s.link

            def move(to, of):
                return dv.tensor_scalar(to, of, 1.0, None, ALU.mult)

            def hold():
                dv.memset(small[:, 30:31], 0.0)

            def split(g, first, n):
                for k in range(2):
                    m = first + n + k
                    for q in range(2):
                        dv.wait_ge(hi_ready, g * 16 + (2 * m + q + 1))
                        dv.tensor_tensor(wlo[:, m % PAIRS, quarter(q)], raw[:, m % RING, quarter(q)],
                                         whi[:, m % PAIRS, quarter(q)], ALU.subtract).then_inc(lo_ready, 1)

            def split_only(name, tiles):
                with dv.Fori(0, tiles // 4) as g:
                    for k in range(4):
                        split(g, FIRST[name], 2 * k + 2)

            def split_input(n, src, base, group, o):
                for k in range(src.shape[1] // group):
                    dv.wait_ge(in_hi, n + k + 1)
                    where = slice(base + k * group, base + (k + 1) * group)
                    dv.tensor_tensor(hlo[:, where, o:], src[:, k * group:(k + 1) * group, :], hhi[:, where, o:],
                                     ALU.subtract).then_inc(in_ready, 1)

            def spread_in(name, turns, of, staged, last):
                def body(g, end):
                    for k in range(4):
                        if not (end and k == 3):
                            dv.wait_ge(stage_hi, g * 4 + (staged + k + 2))
                            dv.tensor_tensor(hlo[:, (k + 1) % 2, META:], of(g * 4 + (k + 1)), hhi[:, (k + 1) % 2, META:],
                                             ALU.subtract).then_inc(stage_lo, 1)
                        if not (end and last and k == 3):
                            split(g, FIRST[name], 2 * k + 2)
                dv.wait_ge(stage_hi, staged + 1)
                dv.tensor_tensor(hlo[:, 0, META:], of(0), hhi[:, 0, META:], ALU.subtract).then_inc(stage_lo, 1)
                with dv.Fori(0, turns - 1) as g:
                    body(g, False)
                body(turns - 1, True)

            def normalise(turn, width, x, h, group0, gain, shift=None):
                o = KEYS - width
                dv.wait_ge(sums, turn)
                link(dv.tensor_scalar(rstd[:, 1, 0:width], PS[:, 7, 0:width], 1.0 / D, EPS, ALU.mult, ALU.add))
                dv.reciprocal(rstd[:, 0, 0:width], rstd[:, 1, 0:width]).then_inc(var_ready, 1)
                if turn == 1:
                    for m in range(2):
                        dv.wait_ge(hi_ready, 2 * m + 2)
                        dv.tensor_tensor(wlo[:, m, :], raw[:, m, :], whi[:, m, :], ALU.subtract).then_inc(lo_ready, 2)
                dv.wait_ge(rstd_ready, turn)
                for c in range(KC):
                    i = dv.scalar_tensor_tensor(h[:, c, :], x[:, c, :], gain(c), rstd[:, 0, 0:width], ALU.mult, ALU.mult)
                    if shift is not None:
                        link(i)
                        i = dv.tensor_scalar(h[:, c, :], h[:, c, :], shift(c), None, ALU.add)
                    link(i)
                    if c % 4 == 3:
                        dv.memset(small[:, 26:27], 0.0).then_inc(in_f32, 1)
                        dv.wait_ge(in_f32, group0 + c // 4 + 1)
                split_input(group0, h, 0, 4, o)

            def head_norms(turn, sq, rs, src, base, width, gains):
                for n in range(16):
                    dv.wait_ge(head_sum, turn * 16 + n + 1)
                    dv.tensor_scalar(rs[:, n, :], PS[:, n % 4, 0:width], 1.0 / P, EPS, ALU.mult, ALU.add).then_inc(head_var, 1)
                dv.wait_ge(head_var, turn * 17 + 16)
                dv.reciprocal(rs[:, :, :], rs[:, :, :]).then_inc(head_var, 1)
                dv.wait_ge(head_rstd, turn + 1)
                for half in range(2):
                    dv.scalar_tensor_tensor(src[:, base + half * 8:base + half * 8 + 8, :],
                                            src[:, base + half * 8:base + half * 8 + 8, :],
                                            vecs[:, gains[half]:gains[half] + 1], rs[:, half * 8:half * 8 + 8, :],
                                            ALU.mult, ALU.mult).then_inc(qk_ready, 1)
                dv.wait_ge(qk_ready, turn * 2 + 2)

            def softmax_heads(a, keys, src, qbase, vbase, o, staged, scores, mx, ex, p_ready, done):
                Pm = a["P"].rearrange("p (t s) -> p t s", t=2)[:, :, 0:keys]
                cm = causal[:, :, KEYS - keys:]
                with s.loop(HEADS, 4) as h:
                    dv.tensor_scalar(a["q"], src[:, h + qbase, o:], SCALE, None, ALU.mult).then_inc(staged, 1)
                    dv.tensor_copy(a["v"][:, 0:keys], src[:, h + vbase, 0:keys]).then_inc(staged, 1)
                    dv.wait_ge(scores, h + 1)
                    link(dv.tensor_tensor(Pm, PS[:, 0:2, 0:keys], cm, ALU.add))
                    link(dv.tensor_reduce(small[:, 0:2], Pm, AX.X, ALU.max))
                    dv.tensor_scalar(small[:, 2:4], small[:, 0:2], -1.0, None, ALU.mult).then_inc(mx, 1)
                    dv.wait_ge(ex, h * 2 + 2)
                    link(dv.reciprocal(small[:, 24:26], small[:, 4:6]))
                    dv.tensor_tensor(Pm, Pm, small[:, 24:26].unsqueeze(2).to_broadcast([P, 2, keys]),
                                     ALU.mult).then_inc(p_ready, 1)
                    dv.wait_ge(done, h + 1)
                    link(move(src[:, h + qbase, o:], PS[:, 5, 0:SEQ]))

            def reduce_angle(ang, num):
                link(dv.tensor_scalar(num, num, ROUND, -ROUND, ALU.add, ALU.add))
                for c in TWO_PI_PARTS:
                    link(dv.scalar_tensor_tensor(ang, num, -float(c), ang, ALU.mult, ALU.add))
                return dv.tensor_scalar(ang, ang, PI_BELOW, -PI_BELOW, ALU.min, ALU.max)

            link(dv.memset(ones[:, :], 1.0))
            link(dv.memset(rstd[:, :, :], 1.0))
            dv.memset(small[:, 26:27], 0.0).then_inc(lo_ready, 2 * RING)
            dv.memset(gmod[:, 4:5], 0.0).then_inc(quarters_used, 2 * PAIRS)
            dv.memset(small[:, 27:28], 0.0).then_inc(banks_free, 4)
            dv.memset(small[:, 28:29], 0.0).then_inc(modw_used, 2)
            for n, one in enumerate((rot_done, bc_used, act_ready)):
                dv.memset(gmod[:, n:n + 1], 0.0).then_inc(one, 1)
            dv.memset(small[:, 29:30], 0.0).then_inc(consts_ready, 1)
            dv.wait_ge(consts_ready, 2)
            dv.wait_ge(vecs_in, 32)
            dv.wait_ge(x_in, 16)
            vec = lambda c: vecs[:, c:c + 1]
            if stage(1):
                normalise(1, KEYS, x0, h0, 0, lambda c: vec(V_MIX + c))
                dv.wait_ge(c_ready, 1)
                done = 0
                with dv.Fori(0, N_MOD) as part:
                    for kc in range(KC):
                        if kc % 2 == 0:
                            split(part * 2, 0, kc + 2)
                        dv.wait_ge(modw_in[kc % 2], (part * (KC // 2) + (kc // 2 + 1)) * 16)
                        dv.wait_ge(modw_used, part * KC + (kc + 2))
                        if kc == 0:
                            i = dv.tensor_scalar(modacc[:, part, :], modring[:, 0, :], small[:, 8:9], None, ALU.mult)
                        else:
                            i = dv.scalar_tensor_tensor(modacc[:, part, :], modring[:, kc % 2, :],
                                                        small[:, 8 + kc:9 + kc], modacc[:, part, :], ALU.mult, ALU.add)
                        i.then_inc(modw_used, 1)
                with dv.Fori(0, 2) as g:
                    for k in range(4):
                        split(g, 96, 2 * k + 2)
                dv.wait_ge(mod_summed, 1)
                link(dv.tensor_tensor(mod[:, :], PS[:, 6, 0:N_MOD * KC], vecs[:, V_BMOD:V_BMOD + N_MOD * KC], ALU.add))
            if stage(2):
                dv.wait_ge(flog, 1)
                dv.tensor_scalar(logf, PS[0:HEADS, 5, 0:KEYS], vecs[0:HEADS, V_BF:V_BF + 1], None, ALU.add).then_inc(flog_in, 1)
                dv.wait_ge(flog_ln, 1)
                link(dv.scalar_tensor_tensor(logf, logf, 0.0, logt, ALU.min, ALU.subtract))
                link(dv.tensor_tensor_scan(sumf, ones[0:HEADS, 0:1].to_broadcast([HEADS, KEYS]), logf, 0.0, ALU.mult, ALU.add))
                dv.wait_ge(stage_zero, 1)
                link(dv.scalar_tensor_tensor(negf[:, :, :], pickh[:, :, :], -1.0,
                                             sumf.unsqueeze(1).to_broadcast([HEADS, HEADS, KEYS]), ALU.mult, ALU.mult))
                head_norms(0, sq1, rs1, p1, 24, KEYS, (V_QG, V_KG))
                link(dv.memset(a1["k"][:, KEYS:], 0.0))
                link(dv.memset(a1["v"][:, KEYS:], 0.0))
                z = PS[:, 0:2, :].rearrange("p a b -> p (a b)")[:, 0:768]
                after = PS[:, 3:5, :].rearrange("p a b -> p (a b)")[:, 0:768]
                seenf = seen[:, :, :].rearrange("p a b -> p (a b)")
                with s.loop(HEADS, 4) as h:
                    dv.tensor_scalar(a1["q"], p1[:, h, META:], SCALE, None, ALU.mult).then_inc(sb_staged, 1)
                    dv.tensor_copy(a1["k"][:, 0:KEYS], p1[:, h + 8, :]).then_inc(sb_staged, 1)
                    dv.tensor_copy(a1["v"][:, 0:KEYS], p1[:, h + 16, :]).then_inc(sb_staged, 1)
                    dv.wait_ge(sb_soft, h + 1)
                    link(dv.scalar_tensor_tensor(a1["L"], z, 0.0, a1["e"], ALU.max, ALU.add))
                    link(dv.tensor_tensor(a1["w"], z, a1["L"], ALU.subtract))
                    dv.scalar_tensor_tensor(a1["L"], a1["L"], -1.0, seenf, ALU.mult, ALU.mult).then_inc(sb_log, 1)
                    dv.wait_ge(sb_after, h + 1)
                    link(dv.tensor_tensor(a1["w"], a1["w"], after, ALU.add))
                    dv.tensor_scalar(a1["w"], a1["w"], 0.0, None, ALU.min).then_inc(sb_logw, 1)
                    dv.wait_ge(sb_expw, h + 1)
                    dv.tensor_tensor(a1["w"], a1["w"], seenf, ALU.mult).then_inc(sb_w, 1)
                    dv.wait_ge(sb_out, h + 1)
                    link(move(p1[:, h, META:], PS[:, 5, 0:SEQ]))
            if stage(3):
                softmax_heads(a1, KEYS, p1, 24, 40, META, fa_staged, fa_scores, fa_max, fa_exp, fa_p, fa_out)
                dv.memset(small[:, 26:27], 0.0).then_inc(fa_staged, 1)
            if stage(4):
                dv.wait_ge(msum, 2)
                link(dv.tensor_scalar(rs1[:, 0:2, 0:SEQ], PS[:, 7, :].rearrange("p (a b) -> p a b", a=2),
                                      1.0 / 1024, EPS, ALU.mult, ALU.add))
                dv.reciprocal(rstd[:, :, 0:SEQ], rs1[:, 0:2, 0:SEQ]).then_inc(mvar, 1)
                dv.wait_ge(mrstd, 1)
                for c in range(8):
                    link(dv.scalar_tensor_tensor(hm[:, c, :], p1[:, c, META:], vec(V_SBG + c), rstd[:, 0, 0:SEQ],
                                                 ALU.mult, ALU.mult))
                    link(dv.scalar_tensor_tensor(hm[:, 8 + c, :], p1[:, 24 + c, META:], vec(V_FOXG + c),
                                                 rstd[:, 1, 0:SEQ], ALU.mult, ALU.mult))
                link(dv.tensor_tensor(hm[:, 8:16, :], hm[:, 8:16, :], p1[:, 48:56, META:], ALU.mult))
                dv.memset(small[:, 26:27], 0.0).then_inc(in_f32, 4)
                split_input(SPLITS["h"], hm, 0, 4, META)
                dv.wait_ge(x0_again, 16)
                with dv.Fori(0, 4) as g:
                    for k in range(4):
                        split(g, FIRST["w_out"], 2 * k + 2)
                        dv.wait_ge(quarters_used, g * 16 + 2 * (PAIRS + FIRST["w_out"] + 2 * (k + 1)))
                        dv.tensor_tensor(xT[:, g * 4 + k, META:], xT[:, g * 4 + k, META:], PS[:, k, 0:SEQ],
                                         ALU.add).then_inc(banks_free, 1)
            if stage(5):
                dv.wait_ge(banks_free, 4 + 72)
                normalise(2, SEQ, xT[:, :, META:], hm, SPLITS["merged"], lambda c: vec(V_FFN + c))
                split_only("w_query", 16)
            if stage(6):
                dv.wait_ge(sx_copied, 8)
                v1, v2, vb = (small_t[:, k, :] for k in range(3))
                with s.loop(16, 28) as u:
                    split(u, FIRST["peer_u"], 2)
                    t_h = sx.rearrange("p t (h s) n -> p (t h) (s n)", s=2)
                    link(move(st, t_h[:, u, :]))
                    for side, v in ((0, v1), (1, v2)):
                        a = st[:, side * N_SUB:(side + 1) * N_SUB]
                        b = st2[:, side * N_SUB:(side + 1) * N_SUB]
                        hold()
                        link(dv.max(v[:, 0:8], a))
                        hold()
                        dv.max_index(idx[:, side, 0:8], v[:, 0:8], a)
                        link(dv.match_replace(b, v[:, 0:8], a, LOWEST))
                        hold()
                        link(dv.max(v[:, 8:16], b))
                        hold()
                        link(dv.max_index(idx[:, side, 8:16], v[:, 8:16], b))
                    link(dv.tensor_copy(small_t[:, 3:5, :], idx[:, 0:2, :]))
                    split(u, FIRST["peer_u"], 4)
                    c3 = cand.rearrange("p (a b) -> p a b", a=16)
                    link(dv.tensor_tensor(c3, v1.unsqueeze(2).to_broadcast([P, 16, 16]),
                                          v2.unsqueeze(1).to_broadcast([P, 16, 16]), ALU.add))
                    hold()
                    link(dv.max(vb[:, 0:8], cand))
                    link(dv.tensor_scalar(small[:, 6:7], vb[:, 0:1], -1.0, None, ALU.mult))
                    hold()
                    dv.max_index(idx[:, 2, 0:8], vb[:, 0:8], cand)
                    link(dv.match_replace(st2, vb[:, 0:8], cand, LOWEST))
                    hold()
                    link(dv.max(vb[:, 8:16], st2))
                    link(dv.tensor_copy(best, vb))
                    dv.memset(small[:, 26:27], 0.0).then_inc(best_ready, 1)
                    link(dv.max_index(idx[:, 2, 8:16], vb[:, 8:16], st2))
                    split(u, FIRST["peer_u"], 6)
                    link(dv.tensor_scalar(idx[:, 0, :], idx[:, 2, :], 4, None, ALU.logical_shift_right))
                    link(dv.tensor_scalar(idx[:, 1, :], idx[:, 2, :], 15, None, ALU.bitwise_and))
                    link(dv.tensor_copy(small_t[:, 5:7, :], idx[:, 0:2, :]))
                    for side in range(2):
                        link(dv.tensor_tensor(oneh, ramp[:, 0:16].unsqueeze(1).to_broadcast([P, 16, 16]),
                                              small_t[:, 5 + side, :].unsqueeze(2).to_broadcast([P, 16, 16]), ALU.is_equal))
                        link(dv.tensor_tensor(oneh, oneh, small_t[:, 3 + side, :].unsqueeze(1).to_broadcast([P, 16, 16]),
                                              ALU.mult))
                        link(dv.tensor_reduce(small_t[:, 7 + side, :], oneh, AX.X, ALU.add))
                    dv.wait_ge(best_exp, u + 1)
                    link(dv.reciprocal(small[:, 27:28], small[:, 7:8]))
                    link(dv.tensor_scalar(small_t[:, 9, :], best, small[:, 27:28], None, ALU.mult))
                    split(u, FIRST["peer_u"], 8)
                    for c in range(3):
                        move(sel8[:, c, u, :], small_t[:, 7 + c, :]).then_inc(picks_done, 1)
                with dv.Fori(16, TAIL // 4) as g:
                    for k in range(4):
                        split(g, FIRST["peer_u"], 2 * k + 2)
                dv.wait_ge(picks_turned, 6)
                for n in range(6):
                    dv.tensor_copy(picked[:, n % 3, (n // 3) * P:(n // 3 + 1) * P],
                                   PS[:, 4 + n // 4, (n % 4) * P:(n % 4 + 1) * P]).then_inc(picks_ready, 1)
                with dv.Fori(TAIL // 4, N_SUB // 4) as g:
                    for k in range(4):
                        split(g, FIRST["peer_u"], 2 * k + 2)
            if stage(7):
                dv.wait_ge(picks_ready, 6)
                dv.wait_ge(banks_free, 4 + 216)
                dv.wait_ge(quarters_used, 2 * (PAIRS + FIRST["peer_v"]))
                dv.memset(small[:, 26:27], 0.0).then_inc(gates_used, 2)

                with dv.Fori(0, SEQ // 8) as g:
                    for b in range(2):
                        for side, one in ((1, oneB), (0, oneA)):
                            dv.tensor_tensor(one[:, b, :, :], ramp[:, 0:P].unsqueeze(1).to_broadcast([P, 4, P]),
                                             picked[:, side, bass.ds(g * 8 + b * 4, 4)].unsqueeze(2).to_broadcast([P, 4, P]),
                                             ALU.is_equal).then_inc(hots, 1)
                    for b in range(2):
                        dv.wait_ge(gates_done, g * 2 + b + 1)
                        part = ga[:, :, bass.ds(g * 8 + b * 4, 4)]
                        dv.tensor_tensor(part, part, PS[:, b, :].rearrange("p (t j) -> p j t", t=4),
                                         ALU.mult).then_inc(gates_used, 1)
                dv.wait_ge(gates_used, 2 + SEQ // 4)
                spread_in("peer_v", N_SUB // 4, lambda j: ga[:, j, :], 0, last_stage == 7)
                dv.wait_ge(quarters_used, 2 * (PAIRS + FIRST["w_in_2"]))
                dv.wait_ge(x1_back, 16)
                link(dv.tensor_tensor(x2[:, :, :], x2[:, :, :], PS[:, :, :].rearrange("p a (b t) -> p (a b) t", b=2), ALU.add))
                dv.memset(small[:, 26:27], 0.0).then_inc(experts_done, 1)
                dv.memset(small[:, 27:28], 0.0).then_inc(x2_ready, 1)
            if stage(8):
                link(dv.scalar_tensor_tensor(gmod[:, :], mod[:, 16:32], 1.0, vecs[:, V_N1:V_N1 + KC], ALU.add, ALU.mult))
                normalise(3, SEQ, x2, h2b, SPLITS["h2"], lambda c: gmod[:, c:c + 1], lambda c: mod[:, c:c + 1])
                split_only("w_in_2", 64)
                head_norms(1, sq2, rs2, p2, 0, SEQ, (V_QG2, V_KG2))
            if stage(9):
                dv.wait_ge(lam_in, 48)
                link(dv.tensor_copy(numr, posi))
                link(dv.tensor_scalar(angr, numr, vec(V_FREQ), None, ALU.mult))
                link(dv.tensor_scalar(numr, angr, INV_2PI, None, ALU.mult))
                reduce_angle(angr, numr).then_inc(ang_ready, 1)
                dv.wait_ge(sin_ready, 1)
                link(dv.tensor_scalar(cosr, cosr, -2.0, 1.0, ALU.mult, ALU.add))
                link(dv.tensor_scalar(sinr[0:64, :], sinr[0:64, :], -1.0, None, ALU.mult))
                with s.loop(8, 4) as g:
                    for b in range(2):
                        dv.wait_ge(swapped, g * 2 + b + 1)
                        link(dv.tensor_tensor(numr, PS[:, b, 0:SEQ], sinr, ALU.mult))
                        link(dv.tensor_tensor(p2[:, g * 2 + b, :], p2[:, g * 2 + b, :], cosr, ALU.mult))
                        dv.tensor_tensor(p2[:, g * 2 + b, :], p2[:, g * 2 + b, :], numr, ALU.add).then_inc(rot_done, 1)
                        dv.wait_ge(rot_done, g * 2 + b + 2)
                softmax_heads(a2, SEQ, p2, 0, 16, 0, ma_staged, ma_scores, ma_max, ma_exp, ma_p, ma_out)
            if stage(10):
                lr, li, dt, mag, phi = (lamp[:, k, :] for k in range(5))
                t = [sq2[:, 8 + k, 0:32] for k in range(4)]
                sn, sh = sq2[:, 12, 0:32], sq2[:, 13, 0:32]
                cre, cim = small2[:, 0, :], small2[:, 1, :]
                dv.wait_ge(lam_a, 1)
                link(dv.tensor_tensor(mag, lr, dt, ALU.mult))
                link(dv.tensor_tensor(phi, li, dt, ALU.mult))
                link(dv.tensor_scalar(t[0], phi, INV_2PI, None, ALU.mult))
                reduce_angle(phi, t[0]).then_inc(lam_b, 1)
                dv.wait_ge(lam_c, 3)
                link(dv.tensor_tensor(t[0], sh, sh, ALU.mult))
                link(dv.tensor_tensor(t[0], t[0], mag, ALU.mult))
                link(dv.tensor_scalar(t[1], mag, -1.0, None, ALU.add))
                link(dv.scalar_tensor_tensor(t[0], t[0], -2.0, t[1], ALU.mult, ALU.add))
                link(dv.tensor_tensor(t[1], mag, sn, ALU.mult))
                link(dv.tensor_tensor(t[2], lr, lr, ALU.mult))
                link(dv.tensor_tensor(t[3], li, li, ALU.mult))
                link(dv.tensor_tensor(t[2], t[2], t[3], ALU.add))
                link(dv.reciprocal(t[3], t[2]))
                link(dv.tensor_tensor(cre, t[0], lr, ALU.mult))
                link(dv.tensor_tensor(t[2], t[1], li, ALU.mult))
                link(dv.tensor_tensor(cre, cre, t[2], ALU.add))
                link(dv.tensor_tensor(cre, cre, t[3], ALU.mult))
                link(dv.tensor_tensor(cim, t[1], lr, ALU.mult))
                link(dv.tensor_tensor(t[2], t[0], li, ALU.mult))
                link(dv.tensor_tensor(cim, cim, t[2], ALU.subtract))
                link(dv.tensor_tensor(cim, cim, t[3], ALU.mult))
                link(dv.tensor_scalar(dt, phi, INV_2PI, None, ALU.mult))
                wide = lambda v, k, n: v[:, bass.ds(k * 4, 4)].unsqueeze(2).to_broadcast([P, 4, n])
                steps = ramp[:, :].unsqueeze(1).to_broadcast([P, 4, SEQ])
                bre = PS[:, 0:4, 0:SEQ]
                bim = PS[:, 0:4, SEQ:]
                with s.loop(8, 22) as k:
                    move(ust, p2[:, k + 24, :]).then_inc(s5_u, 1)
                    dv.tensor_tensor(s5_num, steps, wide(dt, k, SEQ), ALU.mult)
                    link(dv.tensor_tensor(s5_ang, steps, wide(phi, k, SEQ), ALU.mult))
                    reduce_angle(s5_ang, s5_num).then_inc(s5_angr, 1)
                    dv.wait_ge(bc_in, k * 32 + 32)
                    link(dv.tensor_tensor(cc[:, 0, :, :], cst[:, 0, :, :], wide(cre, k, 32), ALU.mult))
                    link(dv.tensor_tensor(ct[:, 0, :, :], cst[:, 1, :, :], wide(cim, k, 32), ALU.mult))
                    link(dv.tensor_tensor(cc[:, 0, :, :], cc[:, 0, :, :], ct[:, 0, :, :], ALU.subtract))
                    link(dv.tensor_tensor(cc[:, 1, :, :], cst[:, 0, :, :], wide(cim, k, 32), ALU.mult))
                    link(dv.tensor_tensor(ct[:, 1, :, :], cst[:, 1, :, :], wide(cre, k, 32), ALU.mult))
                    link(dv.scalar_tensor_tensor(cc[:, 1, :, :], cc[:, 1, :, :], -1.0, ct[:, 1, :, :], ALU.mult, ALU.subtract))
                    dv.wait_ge(s5_sinr, k + 1)
                    link(dv.tensor_scalar(s5_cos, s5_cos, -2.0, 1.0, ALU.mult, ALU.add))
                    dv.wait_ge(s5_bu, k + 1)
                    dv.tensor_tensor(s5_p, s5_cos, bre, ALU.mult)
                    link(dv.tensor_tensor(s5_xr, s5_sin, bim, ALU.mult))
                    link(dv.tensor_tensor(s5_p, s5_p, s5_xr, ALU.add))
                    dv.tensor_tensor(s5_q, s5_cos, bim, ALU.mult)
                    link(dv.tensor_tensor(s5_xi, s5_sin, bre, ALU.mult))
                    link(dv.tensor_tensor(s5_q, s5_q, s5_xi, ALU.subtract))
                    for q in range(4):
                        decay = mag[:, bass.ds(k * 4 + q, 1)].to_broadcast([P, SEQ])
                        dv.tensor_tensor_scan(s5_zr[:, q, :], decay, s5_p[:, q, :], 0.0, ALU.mult, ALU.add)
                        i = dv.tensor_tensor_scan(s5_zi[:, q, :], decay, s5_q[:, q, :], 0.0, ALU.mult, ALU.add)
                    link(i)
                    dv.tensor_tensor(s5_xr, s5_cos, s5_zr, ALU.mult)
                    link(dv.tensor_tensor(s5_p, s5_sin, s5_zi, ALU.mult))
                    link(dv.tensor_tensor(s5_xr, s5_xr, s5_p, ALU.subtract))
                    dv.tensor_tensor(s5_xi, s5_cos, s5_zi, ALU.mult)
                    link(dv.tensor_tensor(s5_q, s5_sin, s5_zr, ALU.mult))
                    link(dv.tensor_tensor(s5_xi, s5_xi, s5_q, ALU.add))
                    dv.memset(small[:, 26:27], 0.0).then_inc(s5_x, 1)
                    dv.wait_ge(s5_y, k + 1)
                    link(dv.scalar_tensor_tensor(ysum, ust, vecs[:, bass.ds(k + V_D, 1)], PS[:, 4, 0:SEQ], ALU.mult, ALU.add))
                    dv.memset(small[:, 27:28], 0.0).then_inc(s5_ys, 1)
                    dv.wait_ge(s5_gel, k + 1)
                    dv.memset(small[:, 28:29], 0.0).then_inc(bc_used, 1)
            if stage(11):
                dv.wait_ge(bc_used, 9)
                dv.memset(small[:, 26:27], 0.0).then_inc(in_f32, 2)
                split_input(SPLITS["h3"], p2[:, 24:32, :], 0, 8, META)
                split_input(SPLITS["ys0"], p2[:, 0:8, :], 8, 8, META)
                for k in range(4):
                    split(0, FIRST["w_glu"], 2 * k + 2)
                with dv.Fori(0, 2) as g:
                    for k in range(8):
                        if k % 2 == 0:
                            split(g, FIRST["w_attn_br"], k + 2)
                        dv.wait_ge(quarters_used, g * 16 + 2 * (PAIRS + FIRST["w_attn_br"] + k + 1))
                        dv.tensor_tensor(h2b[:, g * 8 + k, :], PS[:, k % 4, 0:SEQ], p2[:, g * 8 + (32 + k), :],
                                         ALU.mult).then_inc(banks_free, 1)
                dv.wait_ge(banks_free, 4 + 304)
                link(dv.tensor_tensor(p2[:, 24:32, :], p2[:, 24:32, :], glug[:, :, :], ALU.mult))
                dv.memset(small[:, 27:28], 0.0).then_inc(in_f32, 1)
                split_input(SPLITS["ya"], p2[:, 24:32, :], 0, 8, META)
                with s.loop(2, 8) as g:
                    for k in range(8):
                        if k % 2 == 0:
                            split(g, FIRST["w_ssm_br"], k + 2)
                        dv.wait_ge(quarters_used, g * 16 + 2 * (PAIRS + FIRST["w_ssm_br"] + k + 1))
                        dv.tensor_tensor(mtmp[:, k % 2, :], PS[:, k % 4, 0:SEQ], p2[:, g * 8 + (48 + k), :],
                                         ALU.mult).then_inc(banks_free, 1)
                        dv.wait_ge(banks_free, g * 8 + (4 + 304 + k + 1))
                        link(dv.tensor_tensor(h2b[:, g * 8 + k, :], h2b[:, g * 8 + k, :], mtmp[:, k % 2, :], ALU.add))
                dv.memset(small[:, 26:27], 0.0).then_inc(in_f32, 2)
                split_input(SPLITS["ys"], h2b, 0, 8, META)
                with dv.Fori(0, 4) as g:
                    for k in range(4):
                        split(g, FIRST["w_out_2"], 2 * k + 2)
                        dv.wait_ge(quarters_used, g * 16 + 2 * (PAIRS + FIRST["w_out_2"] + 2 * (k + 1)))
                        dv.scalar_tensor_tensor(x2[:, g * 4 + k, :], PS[:, k, 0:SEQ], mod[:, bass.ds(g * 4 + (32 + k), 1)],
                                                x2[:, g * 4 + k, :], ALU.mult, ALU.add).then_inc(banks_free, 1)
            if stage(12):
                dv.wait_ge(banks_free, 4 + 336)
                link(dv.scalar_tensor_tensor(gmod[:, :], mod[:, 64:80], 1.0, vecs[:, V_N2:V_N2 + KC], ALU.add, ALU.mult))
                normalise(4, SEQ, x2, h2b, SPLITS["m2"], lambda c: gmod[:, c:c + 1], lambda c: mod[:, 48 + c:49 + c])
                with s.loop(22, 4) as g:
                    for k in range(4):
                        split(g, FIRST["w_up"], 2 * k + 2)
                        dst = cva if k % 2 == 0 else cgt
                        dv.wait_ge(up_pre, g * 4 + (k + 1))
                        link(dv.scalar_tensor_tensor(dst[:, 1:], PS[:, k, 0:SEQ - 1], convw[:, 1, bass.ds(g * 4 + k, 1)],
                                                     dst[:, 1:], ALU.mult, ALU.add))
                        dv.scalar_tensor_tensor(dst[:, 2:], PS[:, k, 0:SEQ - 2], convw[:, 0, bass.ds(g * 4 + k, 1)],
                                                dst[:, 2:], ALU.mult, ALU.add).then_inc(banks_free, 1)
                        if k % 2 == 1:
                            dv.wait_ge(banks_free, g * 4 + (4 + 336 + k + 1))
                            dv.wait_ge(up_silu, g * 2 + (k // 2 + 1))
                            dv.tensor_tensor(act[:, g * 2 + k // 2, :], cva, cgt, ALU.mult).then_inc(act_ready, 1)
                spread_in("w_down", FC // 4, lambda j: act[:, j, :], N_SUB, True)
                dv.wait_ge(quarters_used, 2 * (PAIRS + TOTAL))
                for c in range(KC):
                    link(dv.scalar_tensor_tensor(x2[:, c, :], PS[:, c // 2, (c % 2) * SEQ:(c % 2 + 1) * SEQ],
                                                 mod[:, 80 + c:81 + c], x2[:, c, :], ALU.mult, ALU.add))
                dv.memset(small[:, 26:27], 0.0).then_inc(y_ready, 16)


INPUTS = ("x", "vecs", "convw", "w_f", "keys", "pos", "lam", "s5_b", "s5_c", "w_mod") + tuple(n for n, _ in STREAM)


def kernel(x, meta_tokens, norm_mix, w_in, b_forget, fox_q_gain, fox_k_gain, sb_out_gain, fox_out_gain, w_out,
           norm_ffn, peer_w_query, peer_sub_keys, peer_u, peer_v, c_2, positions_2, w_mod_2, b_mod_2, norm1_g_2,
           w_in_2, q_norm_g_2, k_norm_g_2, ssm_lambda_re_2, ssm_lambda_im_2, ssm_log_dt_2, ssm_b_re_2, ssm_b_im_2,
           ssm_c_re_2, ssm_c_im_2, ssm_d_2, w_glu_2, b_glu_2, w_attn_br_2, w_ssm_br_2, w_out_2, norm2_g_2, w_up_2,
           conv_w_2, conv_b_2, w_down_2):
    import concourse.bacc as bacc
    from concourse.bass_utils import run_bass_kernel_spmd

    def columns(v):
        return np.asarray(v).reshape(-1, P).T

    def chunks(w):
        w = np.asarray(w).reshape(w.shape[0] // HALF, 8, P, w.shape[-1] // P, P)
        return w.transpose(3, 0, 2, 1, 4).reshape(-1, P, HALF)

    def rows_of(w):
        return w.reshape(-1, P, 2, HALF).transpose(0, 2, 1, 3).reshape(-1, P, HALF)

    a = {}
    rows = np.concatenate([np.asarray(meta_tokens), np.asarray(x)[0]], axis=0)
    a["x"] = rows.reshape(KEYS, KC, P).transpose(2, 1, 0)
    half = P // 2
    freq = (np.float32(10000.0) ** (-np.arange(half, dtype=np.float32) / np.float32(half))).astype(np.float32)
    bf = np.zeros((P, 1), np.float32)
    bf[:HEADS, 0] = np.asarray(b_forget)[0]
    vecs = [columns(v) for v in (norm_mix, sb_out_gain, fox_out_gain, fox_q_gain, fox_k_gain, norm_ffn, norm1_g_2,
                                 q_norm_g_2, k_norm_g_2, ssm_d_2, b_glu_2, norm2_g_2, b_mod_2, c_2)]
    vecs += [np.concatenate([freq, freq])[:, None], bf, np.zeros((P, 26), np.float32)]
    a["vecs"] = np.concatenate(vecs, axis=1)
    taps = np.concatenate([np.asarray(conv_w_2)[0], np.asarray(conv_b_2)], axis=0)
    a["convw"] = taps.reshape(4, 2, FC, P).transpose(3, 0, 2, 1).reshape(P, 4, 2 * FC)
    w_all = np.asarray(w_in)[0]
    a["w_in"] = chunks(w_all[:, :56 * P])
    a["w_f"] = w_all[:, 56 * P:].reshape(KC, P, HEADS).transpose(1, 0, 2)
    a["w_out"] = chunks(np.asarray(w_out)[0])
    a["w_query"] = chunks(np.asarray(peer_w_query)[0])
    a["keys"] = np.asarray(peer_sub_keys)[0].reshape(16 * N_SUB, P).T
    a["peer_u"] = np.asarray(peer_u)[0]
    a["peer_u"] = a["peer_u"].reshape(N_SUB, N_SUB, 2, 8, P).transpose(1, 2, 4, 3, 0).reshape(-1, P, HALF)
    a["peer_v"] = np.asarray(peer_v)[0].reshape(N_SUB, N_SUB, D).transpose(1, 0, 2)
    a["peer_v"] = rows_of(a["peer_v"])
    a["w_mod"] = np.asarray(w_mod_2)[0].reshape(KC, P, N_MOD, D).transpose(2, 0, 1, 3).reshape(N_MOD * KC, P, D)
    a["w_in_2"] = chunks(np.asarray(w_in_2)[0])
    a["w_glu"] = chunks(np.asarray(w_glu_2)[0])
    a["w_attn_br"] = chunks(np.asarray(w_attn_br_2)[0])
    a["w_ssm_br"] = chunks(np.asarray(w_ssm_br_2)[0])
    a["w_out_2"] = chunks(np.asarray(w_out_2)[0])
    up = chunks(np.asarray(w_up_2)[0]).reshape(2, FC, 2, P, HALF)
    a["w_up"] = up.transpose(1, 0, 2, 3, 4).reshape(-1, P, HALF)
    a["w_down"] = rows_of(np.asarray(w_down_2)[0])
    a["pos"] = np.broadcast_to(np.asarray(positions_2)[0], (P, SEQ))
    lam = [np.asarray(v)[0].reshape(32, P).T for v in (ssm_lambda_re_2, ssm_lambda_im_2)]
    lam.append(np.repeat(np.asarray(ssm_log_dt_2)[0].reshape(32, 2), half, axis=1).T)
    a["lam"] = np.stack(lam, axis=1)
    s5_b = np.zeros((8, 4, 2, 16, 2, 2, half), np.float32)
    s5_c = np.zeros((8, 2, half, 2, 4, 2, 16), np.float32)
    for part, (b, c) in enumerate(((ssm_b_re_2, ssm_c_re_2), (ssm_b_im_2, ssm_c_im_2))):
        b = np.asarray(b)[0].reshape(8, 4, 2, half, 16)
        c = np.asarray(c)[0].reshape(8, 4, 2, 16, half)
        for g in range(2):
            s5_b[:, :, g, :, part, g, :] = b[:, :, g].transpose(0, 1, 3, 2)
            s5_c[:, g, :, part, :, g, :] = c[:, :, g].transpose(0, 3, 1, 2)
    a["s5_b"] = s5_b.reshape(8, P, 2, P)
    a["s5_c"] = s5_c.reshape(8, P, 2, 4, 32)

    nc = bacc.Bacc("TRN2", target_bir_lowering=False, num_devices=1)
    drams = {}
    for name in INPUTS:
        a[name] = np.ascontiguousarray(a[name])
        drams[name] = nc.dram_tensor(name + "_dram", a[name].shape, mybir.dt.from_np(a[name].dtype),
                                     kind="ExternalInput").ap()
    y = nc.dram_tensor("y_dram", (P, KC, SEQ), F32, kind="ExternalOutput").ap()
    drams["x1"] = nc.dram_tensor("x1_dram", (P, KC, SEQ), F32, kind="Internal").ap()
    build(nc, drams, y)
    r = run_bass_kernel_spmd(nc, [{name + "_dram": a[name] for name in INPUTS}], core_ids=[0])
    return r.results[0]["y_dram"].transpose(2, 1, 0).reshape(1, SEQ, D)
```

```python
from contextlib import ExitStack, contextmanager

import numpy as np
import concourse.bass as bass
from concourse import mybir

F32 = mybir.dt.float32
F32R = mybir.dt.float32r
I32 = mybir.dt.int32
U32 = mybir.dt.uint32
ALU = mybir.AluOpType
ACT = mybir.ActivationFunctionType
AX = mybir.AxisListType

P = 128
SEQ = 256
META = 16
KEYS = META + SEQ
D = 2048
KC = D // P
HEADS = 8
RING = 4
HALF = 1024
PAIRS = 2
SCALE = float(P) ** -0.5
EPS = 1e-6
TOPK = 16
N_SUB = 128
SLOTS = HEADS * TOPK
FFN = 5632
FC = FFN // P
N_MOD = 6
MOD_FIRST = 3
MOD_RING = 4
MOD_LATE_RING = 2
NEG = -1e30
LOWEST = -3.0e38
ROUND = 12582912.0
INV_2PI = 0.15915494309189535
TWO_PI_PARTS = (6.28125, 2029 / 2.0**20, 2 * np.pi - 6.28125 - 2029 / 2.0**20)
PI_BELOW = 3.1415925

STREAM = [("w_in", 112), ("w_out", 32), ("w_query", 32), ("peer_u", 256), ("peer_v", 256), ("w_in_2", 128),
          ("w_glu", 8), ("w_attn_br", 16), ("w_ssm_br", 16), ("w_out_2", 32), ("w_up", 176), ("w_down", 88)]
FIRST = {}
_n = 0
for _name, _halves in STREAM:
    FIRST[_name] = _n
    _n += _halves
TOTAL = _n
SPLITS = {"h": 4, "merged": 8, "h2": 12, "h3": 16, "ys0": 17, "ya": 18, "ys": 19, "m2": 21, "h4": 25}


class Steps:

    def __init__(self, eng, sem):
        self.eng, self.sem, self.done, self.turn = eng, sem, 0, 0

    def link(self, ins):
        ins.then_inc(self.sem, 1)
        self.done += 1
        self.eng.wait_ge(self.sem, self.turn + self.done)

    @contextmanager
    def loop(self, turns, links):
        with self.eng.Fori(0, turns) as i:
            before, self.turn = self.done, i * links
            yield i
            assert self.done - before == links, (self.done - before, links)
            self.turn = 0
            self.done = before + links * turns


def quarter(q):
    return slice(q * HALF // 2, (q + 1) * HALF // 2)


def build(nc, d, out):
    ctx = ExitStack()
    with ctx:
        def sb(name, shape, dt=F32):
            return ctx.enter_context(nc.sbuf_tensor(name, shape, dt))

        def sem(name):
            return ctx.enter_context(nc.semaphore(name))

        at = -(-nc.sbuf_base // 32) * 32
        arena = sb("arena", [P, 2 * KC * KEYS])
        hhi = nc.alloc_sbuf_tensor_at("hhi", [P, KC, KEYS], F32R, offset=at)
        hlo = nc.alloc_sbuf_tensor_at("hlo", [P, KC, KEYS], F32R, offset=at + KC * KEYS * 4)
        raw = sb("raw", [P, RING, HALF])
        whi = sb("whi", [P, PAIRS, HALF], F32R)
        wlo = sb("wlo", [P, PAIRS, HALF], F32R)
        big = sb("big", [P, 128 * SEQ])
        ident = sb("ident", [P, P])
        ones = sb("ones", [P, P])
        later = sb("later", [P, P])
        swap = sb("swap", [P, P])
        ramp = sb("ramp", [P, SEQ])
        causal = sb("causal", [P, 2, KEYS])
        vecs = sb("vecs", [P, 240])
        mod = sb("mod", [P, N_MOD * KC])
        gmod = sb("gmod", [P, KC])
        rstd = sb("rstd", [P, 2, KEYS])
        small = sb("small", [P, 44])
        late = sb("late", [P, 768])
        picked = late[:, :].rearrange("p (a b) -> p a b", a=3)
        convw = late[:, 0:352].rearrange("p (a b) -> p a b", a=4)
        posi = late[:, 352:608].bitcast(I32)
        lamp = late[:, 608:768].rearrange("p (a b) -> p a b", a=5)
        small_t = sb("small_t", [P, 10, 16])
        small2 = sb("small2", [P, 2, 32])
        idx = sb("idx", [P, 3, 16], U32)
        wf = sb("wf", [P, KC, HEADS])

        PS = ctx.enter_context(nc.psum_tensor("PS", [P, 8, 512], F32))

        def region(start, *shape):
            n = 1
            for s in shape:
                n *= s
            assert start + n <= 128 * SEQ
            v = big[:, start:start + n]
            if len(shape) == 1:
                return v
            names = "abcd"[:len(shape)]
            return v.rearrange(f"p ({' '.join(names)}) -> p {' '.join(names)}",
                               **{k: s for k, s in zip(names, shape)})

        V_MIX, V_SBG, V_FOXG, V_QG, V_KG, V_FFN = 0, 16, 24, 32, 33, 34
        V_N1, V_QG2, V_KG2, V_D, V_BGLU, V_N2, V_BMOD, V_C, V_FREQ, V_BF = 50, 66, 67, 68, 76, 84, 100, 196, 212, 213

        sq0 = region(0, KC, KEYS)
        x0 = region(KC * KEYS, KC, KEYS)
        h0 = region(2 * KC * KEYS, KC, KEYS)
        X1 = 128 * SEQ - KC * KEYS
        xT = region(X1, KC, KEYS)
        x2 = region(128 * SEQ - KC * SEQ, KC, SEQ)
        p1 = region(0, 56, KEYS)
        B1 = 56 * KEYS
        seen = late[:, :].rearrange("p (a b) -> p a b", a=3)
        modring = region(B1, MOD_RING, D)
        modacc = region(B1 + 32 * KEYS, MOD_FIRST, D)
        sq1 = region(B1, 16, KEYS)
        hm = region(B1 + 9000, KC, SEQ)
        rs1 = region(B1 + 16 * KEYS, 16, KEYS)
        sumf = big[0:HEADS, B1 + 32 * KEYS:B1 + 33 * KEYS]
        pickh = big[0:HEADS, B1 + 33 * KEYS:B1 + 41 * KEYS].rearrange("p (a b) -> p a b", a=HEADS)
        negf = big[0:HEADS, B1 + 41 * KEYS:B1 + 49 * KEYS].rearrange("p (a b) -> p a b", a=HEADS)
        logf = big[0:HEADS, B1 + 49 * KEYS:B1 + 50 * KEYS]
        logt = big[0:HEADS, B1 + 50 * KEYS:B1 + 51 * KEYS]

        def attention_parts(of, at):
            parts, out = [("q", 256), ("k", 384), ("v", 384), ("vn", 384), ("a", 768), ("e", 768), ("L", 768),
                          ("w", 768), ("P", 2 * KEYS), ("PT", 768)], {}
            for n, size in parts:
                out[n] = of[:, at:at + size]
                at += size
            return out

        a1 = [attention_parts(big, B1), attention_parts(arena, 0)]
        sums_of = [small[:, 0:8], small[:, 36:44]]
        ga = region(0, N_SUB, SEQ)
        TAIL = 88
        qx = region(TAIL * SEQ, 16, SEQ)
        sx = region((TAIL + 16) * SEQ, 2, 16, N_SUB)
        T0 = (TAIL + 32) * SEQ
        st = region(T0, 256)
        st2 = region(T0 + 256, 256)
        cand = region(T0 + 512, 256)
        oneh = region(T0 + 768, 16, 16)
        sel = region(T0 + 1024, 3, 2, SLOTS)
        sel8 = region(T0 + 1024, 3, 2 * HEADS, TOPK)
        best = region(T0 + 1024 + 768, 16)
        hTf = arena
        oneA = hTf[:, 0:2048].rearrange("p (g t i) -> p g t i", g=4, t=4)
        oneB = hTf[:, 2048:4096].rearrange("p (g t i) -> p g t i", g=4, t=4)
        p2 = region(0, 64, SEQ)
        B2 = 64 * SEQ
        sq2 = arena[:, 0:16 * SEQ].rearrange("p (a b) -> p a b", a=16)
        rs2 = arena[:, 16 * SEQ:32 * SEQ].rearrange("p (a b) -> p a b", a=16)
        cosr = region(B2 + 8192, SEQ)
        sinr = region(B2 + 8448, SEQ)
        angr = region(B2 + 8704, SEQ)
        numr = region(B2 + 8960, SEQ)
        modlring = region(B2, MOD_LATE_RING, D)
        modlate = region(B2 + 12288 - (N_MOD - MOD_FIRST) * D, N_MOD - MOD_FIRST, D)
        a2 = [attention_parts(big, B2), a1[1]]
        ust = region(B2, SEQ)
        bst = region(B2 + 256, 2, 2, P)
        cst = region(B2 + 768, 2, 2, 4, 32)
        cc = region(B2 + 1280, 3, 4, 32)
        ct = region(B2 + 1664, 2, 4, 32)
        ysum = region(B2 + 1920, SEQ)
        wide_tile = lambda v: v.rearrange("p (a b) -> p a b", a=4)
        s5_p, s5_q, s5_zr, s5_zi, s5_ta, s5_tb = (region(B2 + 2176 + 1024 * k, 4, SEQ) for k in range(6))
        s5_cos = [region(B2 + 2176 + 1024 * k, 4, SEQ) for k in (6, 7)]
        s5_ang, s5_num = (wide_tile(arena[:, 1024 * k:1024 * (k + 1)]) for k in (0, 1))
        s5_sin = [wide_tile(arena[:, 1024 * k:1024 * (k + 1)]) for k in (2, 3)]
        s5_out = [wide_tile(arena[:, 1024 * k:1024 * (k + 1)]) for k in (4, 5, 6, 7)]
        glug = region(B2, 8, SEQ)
        mtmp = region(B2 + 2048, 2, SEQ)
        h2b = region(B2 + 2560, KC, SEQ)
        sqb = region(B2 + 6656, KC, SEQ)
        act = region(0, FC, SEQ)
        cva = region(B2, SEQ)
        cgt = region(B2 + 256, SEQ)
        keysx = region((TAIL - 8) * SEQ, D)

        raw_in = [sem(f"raw_in{s}") for s in range(RING)]
        hi_ready = sem("hi_ready")
        lo_ready = sem("lo_ready")
        quarters_used = sem("quarters_used")
        in_f32, in_hi, in_ready = sem("in_f32"), sem("in_hi"), sem("in_ready")
        stage_hi, stage_lo = sem("stage_hi"), sem("stage_lo")
        x1_saved, x1_back, x0_again = sem("x1_saved"), sem("x1_back"), sem("x0_again")
        banks_free = sem("banks_free")
        vecs_in = sem("vecs_in")
        x_in = sem("x_in")
        pool_steps = sem("pool_steps")
        consts_ready = sem("consts_ready")
        dve_steps = sem("dve_steps")
        act_steps = sem("act_steps")
        squares = sem("squares")
        sums = sem("sums")
        var_ready = sem("var_ready")
        rstd_ready = sem("rstd_ready")
        modw_in = [sem(f"modw_in{s}") for s in range(MOD_RING)]
        modl_in = [sem(f"modl_in{s}") for s in range(MOD_LATE_RING)]
        modw_used = sem("modw_used")
        c_ready = sem("c_ready")
        mod_summed = sem("mod_summed")
        flog = sem("flog")
        flog_in = sem("flog_in")
        flog_abs = sem("flog_abs")
        flog_ln = sem("flog_ln")
        decay_ready = sem("decay_ready")
        head_sq = sem("head_sq")
        head_sum = sem("head_sum")
        head_var = sem("head_var")
        head_rstd = sem("head_rstd")
        qk_ready = sem("qk_ready")
        stage_zero = sem("stage_zero")
        sb_staged, sb_z, sb_soft, sb_v, sb_log, sb_after, sb_logw, sb_expw, sb_w, sb_out = (
            sem("sb_" + n) for n in "staged z soft v log after logw expw w out".split())
        sb_free, fa_free, ma_free = (sem(n + "_free") for n in ("sb", "fa", "ma"))
        fa_staged, fa_scores, fa_v, fa_max, fa_exp, fa_p, fa_pt, fa_ptc, fa_out = (
            sem("fa_" + n) for n in "staged scores v max exp p pt ptc out".split())
        ma_staged, ma_scores, ma_v, ma_max, ma_exp, ma_p, ma_pt, ma_ptc, ma_out = (
            sem("ma_" + n) for n in "staged scores v max exp p pt ptc out".split())
        msq, msum, mvar, mrstd, merged_ready = (sem("m_" + n) for n in "sq sum var rstd ready".split())
        x1_ready = sem("x1_ready")
        keys_in = sem("keys_in")
        sx_done = sem("sx_done")
        sx_copied = sem("sx_copied")
        best_ready, best_exp, picks_done, picks_turned, picks_ready = (
            sem("pk_" + n) for n in "best exp done turned ready".split())
        hots, weighted, gates_done, gates_used = (sem("g_" + n) for n in "hots weighted done used".split())
        experts_done = sem("experts_done")
        x2_ready = sem("x2_ready")
        ang_ready, sin_ready, rot_sq, swapped, rot_done = (sem("r_" + n) for n in "ang sin sq swapped done".split())
        lam_in, lam_a, lam_b, lam_c, lam_d = (sem("l_" + n) for n in "in a b c d".split())
        bc_in = [sem(f"s5_bcin{s}") for s in range(2)]
        s5_z, s5_xp = sem("s5_z"), sem("s5_xp")
        bc_used, s5_lam, s5_raw, s5_u, s5_bu, s5_angr, s5_sinr, s5_x, s5_y, s5_ys, s5_gel = (
            sem("s5_" + n) for n in "bcused lam raw u bu ang sin x y ys gelu".split())
        glu_ready = sem("glu_ready")
        gated = sem("gated")
        m_done = sem("m_done")
        x3_ready = sem("x3_ready")
        up_pre, up_silu, act_ready = (sem("up_" + n) for n in "pre silu ready".split())
        y_ready = sem("y_ready")
        y_out = sem("y_out")

        block = ctx.enter_context(nc.Block())

        @block.sync
        def _(sp):
            sp.dma_start(x0[:, :, :], d["x"]).then_inc(x_in, 16)
            sp.dma_start(vecs[:, :], d["vecs"]).then_inc(vecs_in, 16)
            sp.dma_start(wf[:, :, :], d["w_f"]).then_inc(vecs_in, 16)
            for name, halves in STREAM:
                with sp.Fori(0, halves // RING) as g:
                    for s in range(RING):
                        sp.wait_ge(lo_ready, g * (2 * RING) + 2 * (FIRST[name] + s + 1))
                        sp.dma_start(raw[:, s, :], d[name][g * RING + s]).then_inc(raw_in[s], 16)
            sp.wait_ge(y_ready, 16)
            sp.dma_start(out, x2[:, :, :]).then_inc(y_out, 16)
            sp.wait_ge(y_out, 16)

        @block.gpsimd
        def _(pool):
            s = Steps(pool, pool_steps)
            s.link(pool.memset(ident[:, :], 0.0))
            s.link(pool.memset(later[:, :], 1.0))
            s.link(pool.memset(swap[:, :], 0.0))
            s.link(pool.memset(causal[:, :, :], 0.0))
            s.link(pool.memset(seen[:, :, :], 1.0))
            s.link(pool.affine_select(out=ident[:, :], in_=ident[:, :], compare_op=ALU.not_equal, fill=1.0,
                                      base=0, pattern=[[-1, P]], channel_multiplier=1))
            s.link(pool.affine_select(out=later[:, :], in_=later[:, :], compare_op=ALU.is_gt, fill=0.0,
                                      base=0, pattern=[[-1, P]], channel_multiplier=1))
            for shift in (64, -64):
                s.link(pool.affine_select(out=swap[:, :], in_=swap[:, :], compare_op=ALU.not_equal, fill=1.0,
                                          base=shift, pattern=[[-1, P]], channel_multiplier=1))
            s.link(pool.affine_select(out=causal[:, :, :], in_=causal[:, :, :], compare_op=ALU.is_ge, fill=NEG,
                                      base=META, pattern=[[P, 2], [-1, KEYS]], channel_multiplier=1))
            s.link(pool.affine_select(out=seen[:, :, :], in_=seen[:, :, :], compare_op=ALU.is_gt, fill=0.0,
                                      base=META, pattern=[[-P, 3], [1, SEQ]], channel_multiplier=-1))
            pool.iota(ramp[:, :], pattern=[[1, SEQ]], base=0, channel_multiplier=0,
                      allow_small_or_imprecise_dtypes=True).then_inc(consts_ready, 1)
            with pool.Fori(0, MOD_FIRST) as part:
                for kc in range(KC):
                    pool.wait_ge(modw_used, part * KC + kc + 1)
                    pool.dma_start(modring[:, kc % MOD_RING, :],
                                   d["w_mod"][part * KC + kc]).then_inc(modw_in[kc % MOD_RING], 16)
            pool.wait_ge(mod_summed, 1)
            s.link(pool.memset(pickh[:, :, :], 0.0))
            pool.affine_select(out=pickh[:, :, :], in_=pickh[:, :, :], compare_op=ALU.not_equal, fill=1.0,
                               base=0, pattern=[[-1, HEADS], [0, KEYS]],
                               channel_multiplier=1).then_inc(stage_zero, 1)
            with pool.Fori(0, SEQ // 16) as g:
                for b in range(4):
                    pool.wait_ge(hots, g * 8 + b * 2 + 2)
                    pool.tensor_tensor(oneA[:, b, :, :], oneA[:, b, :, :],
                                       picked[:, 2, bass.ds(g * 16 + b * 4, 4)].unsqueeze(2).to_broadcast([P, 4, P]),
                                       ALU.mult).then_inc(weighted, 1)
            pool.wait_ge(in_ready, SPLITS["h3"])
            with pool.Fori(MOD_FIRST, N_MOD) as part:
                for kc in range(KC):
                    pool.wait_ge(modw_used, part * KC + (kc + MOD_RING - MOD_LATE_RING + 1))
                    pool.dma_start(modlring[:, kc % MOD_LATE_RING, :],
                                   d["w_mod"][part * KC + kc]).then_inc(modl_in[kc % MOD_LATE_RING], 16)
            pool.wait_ge(ma_out, HEADS)
            for b in range(2):
                pool.dma_start(bst[:, b, :, :], d["s5_b"][b]).then_inc(bc_in[b], 16)
                pool.dma_start(cst[:, b, :, :, :], d["s5_c"][b]).then_inc(bc_in[b], 16)

            def turn_back(g, b):
                pool.wait_ge(s5_z, g * 2 + (b + 1))
                pool.tensor_tensor(s5_out[2], s5_cos[b], s5_zi, ALU.mult)
                pool.tensor_tensor(s5_out[3], s5_sin[b], s5_zr, ALU.mult).then_inc(s5_xp, 1)

            with pool.Fori(0, 3) as g:
                for b in range(2):
                    turn_back(g, b)
                    pool.wait_ge(bc_used, g * 2 + (b + 1))
                    pool.dma_start(bst[:, b, :, :], d["s5_b"][g * 2 + (b + 2)]).then_inc(bc_in[b], 16)
                    pool.dma_start(cst[:, b, :, :, :], d["s5_c"][g * 2 + (b + 2)]).then_inc(bc_in[b], 16)
            turn_back(3, 0)
            turn_back(3, 1)

        @block.tensor
        def _(pe):
            def sum_features(of, n, bank, width, at, sem_in, value, sem_out):
                pe.wait_ge(sem_in, value)
                for c in range(n):
                    last = pe.matmul(PS[:, bank, at:at + width], ones[:, :], of[:, c, :], start=c == 0, stop=c == n - 1)
                last.then_inc(sem_out, 1)

            def three(out, hi, lo, rhi, rlo, start, stop, **more):
                pe.matmul(out, hi, rhi, start=start, stop=False, **more)
                pe.matmul(out, hi, rlo, start=False, stop=False, **more)
                return pe.matmul(out, lo, rhi, start=False, stop=stop, **more)

            def dense(name, chunk0, width, turns=None):
                h0_ = FIRST[name]
                o = KEYS - width
                n = dict(STREAM)[name] // 8
                with pe.Fori(*(turns or (0, n))) as g:
                    for c in range(4):
                        pe.wait_ge(banks_free, g * 4 + (chunk0 + c + 1))
                        for half in range(2):
                            for kc in range(8):
                                if kc % 4 == 0:
                                    pe.wait_ge(lo_ready, g * 16 + 2 * (RING + h0_ + 2 * c + half) + kc // 4 + 1)
                                at_ = slice(kc * P, (kc + 1) * P)
                                last = three(PS[:, c, 0:width], whi[:, half, at_], wlo[:, half, at_],
                                             hhi[:, half * 8 + kc, o:], hlo[:, half * 8 + kc, o:],
                                             half == 0 and kc == 0, half == 1 and kc == 7)
                                if kc % 4 == 3:
                                    last.then_inc(quarters_used, 1)

            def dense_half(name, chunk0, base):
                h0_ = FIRST[name]
                with pe.Fori(0, dict(STREAM)[name] // 8) as g:
                    for c in range(8):
                        pe.wait_ge(banks_free, g * 8 + (chunk0 + c + 1))
                        for kc in range(8):
                            if kc % 4 == 0:
                                pe.wait_ge(lo_ready, g * 16 + 2 * (RING + h0_ + c) + kc // 4 + 1)
                            at_ = slice(kc * P, (kc + 1) * P)
                            last = three(PS[:, c % 4, 0:SEQ], whi[:, c % 2, at_], wlo[:, c % 2, at_],
                                         hhi[:, base + kc, META:], hlo[:, base + kc, META:], kc == 0, kc == 7)
                            if kc % 4 == 3:
                                last.then_inc(quarters_used, 1)

            def spread(name, turns, first, staged):
                h0_ = FIRST[name]

                def body(g, opening):
                    for b in range(4):
                        pe.wait_ge(stage_lo, g * 4 + (staged + b + 1))
                        for half in range(2):
                            for m in range(8):
                                if m % 4 == 0:
                                    pe.wait_ge(lo_ready, g * 16 + 2 * (RING + h0_ + 2 * b + half) + m // 4 + 1)
                                mm = half * 8 + m
                                at_ = slice(m * P, (m + 1) * P)
                                last = three(PS[:, mm // 2, (mm % 2) * SEQ:(mm % 2 + 1) * SEQ], whi[:, half, at_],
                                             wlo[:, half, at_], hhi[:, b % 2, META:], hlo[:, b % 2, META:],
                                             opening and b == 0 and mm % 2 == 0, False, skip_group_check=True)
                                if m % 4 == 3:
                                    last.then_inc(quarters_used, 1)

                if first:
                    body(0, True)
                with pe.Fori(1 if first else 0, turns) as g:
                    body(g, False)

            def softmax_heads(a, keys, kbase, src, staged, scores, v_ready, p_ready, pt, ptc, done, decays):
                nk = -(-keys // P)
                width = [min(P, keys - P * j) for j in range(nk)]
                free = fa_free if decays else ma_free

                def scores_of(g, ahead):
                    for b in range(2):
                        h, B = g * 2 + (2 * ahead + b), 3 * b
                        pe.wait_ge(staged, g * 4 + (4 * ahead + b * 2 + 2))
                        if ahead:
                            pe.wait_ge(ptc, g * (2 * (nk - 1)) + (b + 1) * (nk - 1))
                        for t in range(2):
                            pe.matmul(PS[:, B + t, 0:keys], a[b]["q"][:, t * P:(t + 1) * P],
                                      src[:, g * 2 + (2 * ahead + b + kbase), 0:keys], start=True, stop=not decays)
                            if decays:
                                pe.matmul(PS[:, B + t, 0:keys], sumf[:, META + t * P:META + (t + 1) * P], pickh[:, h, :],
                                          start=False, stop=False)
                                pe.matmul(PS[:, B + t, 0:keys], ones[0:HEADS, :], negf[:, h, :], start=False, stop=True)
                        for j in range(nk):
                            last = pe.transpose(PS[0:width[j], B + 2, j * P:(j + 1) * P],
                                                a[b]["v"][:, j * P:j * P + width[j]], ident[:, :])
                        last.then_inc(scores, 1)

                def turned(g):
                    for b in range(2):
                        pe.wait_ge(p_ready, g * 2 + (b + 1))
                        for t in range(2):
                            for j in range(nk):
                                last = pe.transpose(PS[0:width[j], 3 * b + j // 2,
                                                       (j % 2) * SEQ + t * P:(j % 2) * SEQ + (t + 1) * P],
                                                    a[b]["P"].rearrange("p (t s) -> p t s", t=2)[:, t, j * P:j * P + width[j]],
                                                    ident[:, :])
                        last.then_inc(pt, 1)

                def sums_of_values(g):
                    for b in range(2):
                        pe.wait_ge(ptc, g * (2 * (nk - 1)) + (b + 1) * (nk - 1))
                        pe.wait_ge(v_ready, g * (2 * (nk - 1)) + (b + 1) * (nk - 1))
                        pe.wait_ge(free, g * 2 + (b + 1))
                        for j in range(nk):
                            last = pe.matmul(PS[:, 6 + b, 0:SEQ], a[b]["vn"][0:width[j], j * P:(j + 1) * P],
                                             a[b]["PT"][0:width[j], j * SEQ:(j + 1) * SEQ], start=j == 0, stop=j == nk - 1)
                        last.then_inc(done, 1)

                scores_of(0, 0)
                with pe.Fori(0, HEADS // 2 - 1) as g:
                    turned(g)
                    scores_of(g, 1)
                    sums_of_values(g)
                turned(HEADS // 2 - 1)
                sums_of_values(HEADS // 2 - 1)

            def sum_mod(acc, first, parts):
                for n in range(parts * KC):
                    last = pe.matmul(PS[:, 6, first * KC + n:first * KC + n + 1], acc[:, n * P:(n + 1) * P], ones[:, 0:1],
                                     start=True, stop=True)
                last.then_inc(mod_summed, 1)

            pe.wait_ge(consts_ready, 2)
            sum_features(sq0, KC, 7, KEYS, 0, squares, 1, sums)
            pe.wait_ge(in_f32, 4)
            for kc in range(KC):
                last = pe.matmul(PS[0:HEADS, 5, 0:KEYS], wf[:, kc, :], h0[:, kc, :], start=kc == 0, stop=kc == KC - 1)
            last.then_inc(flog, 1)
            pe.wait_ge(in_ready, SPLITS["h"])
            dense("w_in", 0, KEYS)
            pe.wait_ge(head_sq, 1)
            pe.wait_ge(banks_free, 4 + 56)
            for n in range(16):
                if n >= 4:
                    pe.wait_ge(head_var, n - 3)
                pe.matmul(PS[:, n % 4, 0:KEYS], ones[:, :], sq1[:, n, :], start=True, stop=True).then_inc(head_sum, 1)
            pe.wait_ge(modw_used, MOD_FIRST * KC + MOD_RING)
            sum_mod(modacc.rearrange("p a b -> p (a b)"), 0, MOD_FIRST)
            def sb_scores(g, ahead):
                for b in range(2):
                    pe.wait_ge(sb_staged, g * 6 + (6 * ahead + b * 3 + 3))
                    if ahead:
                        pe.wait_ge(sb_logw, g * 2 + (b + 1))
                        pe.wait_ge(sb_v, g * 2 + (b + 1))
                    for j in range(3):
                        pe.matmul(PS[:, 3 * b + j // 2, (j % 2) * SEQ:(j % 2 + 1) * SEQ],
                                  a1[b]["k"][:, j * P:(j + 1) * P], a1[b]["q"], start=True, stop=True)
                    for j in range(3):
                        last = pe.transpose(PS[:, 3 * b + 2, j * P:(j + 1) * P], a1[b]["v"][:, j * P:(j + 1) * P],
                                            ident[:, :])
                    last.then_inc(sb_z, 1)

            def sb_later(g):
                for b in range(2):
                    pe.wait_ge(sb_log, g * 2 + (b + 1))
                    for j in range(3):
                        for k in range(j, 3):
                            last = pe.matmul(PS[:, 3 * b + j // 2, (j % 2) * SEQ:(j % 2 + 1) * SEQ],
                                             later[:, :] if k == j else ones[:, :], a1[b]["L"][:, k * SEQ:(k + 1) * SEQ],
                                             start=k == j, stop=k == 2)
                    last.then_inc(sb_after, 1)

            def sb_sums(g):
                for b in range(2):
                    pe.wait_ge(sb_v, g * 2 + (b + 1))
                    pe.wait_ge(sb_w, g * 2 + (b + 1))
                    pe.wait_ge(sb_free, g * 2 + (b + 1))
                    for j in range(3):
                        last = pe.matmul(PS[:, 6 + b, 0:SEQ], a1[b]["vn"][:, j * P:(j + 1) * P],
                                         a1[b]["w"][:, j * SEQ:(j + 1) * SEQ], start=j == 0, stop=j == 2)
                    last.then_inc(sb_out, 1)

            sb_scores(0, 0)
            with pe.Fori(0, HEADS // 2 - 1) as g:
                sb_later(g)
                sb_scores(g, 1)
                sb_sums(g)
            sb_later(HEADS // 2 - 1)
            sb_sums(HEADS // 2 - 1)
            pe.wait_ge(stage_zero, 1)
            softmax_heads(a1, KEYS, 32, p1, fa_staged, fa_scores, fa_v, fa_p, fa_pt, fa_ptc, fa_out, True)
            for part in range(2):
                pe.wait_ge(msq, 2)
                for c in range(8):
                    last = pe.matmul(PS[:, 7, part * SEQ:(part + 1) * SEQ], ones[:, :],
                                     sq1[:, part * 8 + c, 0:SEQ], start=c == 0, stop=c == 7)
                last.then_inc(msum, 1)
            pe.wait_ge(in_ready, SPLITS["merged"])
            dense("w_out", 56, SEQ)
            sum_features(sq0[:, :, META:], KC, 7, SEQ, 0, squares, 2, sums)
            pe.wait_ge(in_ready, SPLITS["h2"])
            dense("w_query", 72, SEQ)
            pe.wait_ge(banks_free, 4 + 88)
            pe.wait_ge(keys_in, 16)
            for n in range(8):
                t, q4 = n // 4, n % 4
                for k in range(4):
                    hp = q4 * 4 + k
                    last = pe.matmul(PS[:, n, k * P:(k + 1) * P], qx[:, hp, t * P:(t + 1) * P],
                                     keysx[:, hp * P:(hp + 1) * P], start=True, stop=True)
                last.then_inc(sx_done, 1)
            pe.wait_ge(sx_copied, 8)
            dense("peer_u", 88, SEQ, (0, TAIL // 4))
            pe.wait_ge(picks_done, 48)
            for n in range(6):
                pe.transpose(PS[:, 4 + n // 4, (n % 4) * P:(n % 4 + 1) * P], sel[:, n % 3, n // 3, :],
                             ident[:, :]).then_inc(picks_turned, 1)
            dense("peer_u", 88, SEQ, (TAIL // 4, N_SUB // 4))
            with pe.Fori(0, SEQ // 16) as g:
                for b in range(4):
                    pe.wait_ge(weighted, g * 4 + b + 1)
                    pe.wait_ge(gates_used, g * 4 + b + 1)
                    for k in range(4):
                        last = pe.matmul(PS[:, b, k * P:(k + 1) * P], oneA[:, b, k, :], oneB[:, b, k, :],
                                         start=True, stop=True)
                    last.then_inc(gates_done, 1)
            pe.wait_ge(gates_used, 4 + SEQ // 4)
            spread("peer_v", N_SUB // 4, True, 0)
            pe.wait_ge(experts_done, 1)
            sum_features(sqb, KC, 7, SEQ, 0, squares, 3, sums)
            pe.wait_ge(in_ready, SPLITS["h3"])
            dense("w_in_2", 216, SEQ)
            pe.wait_ge(head_sq, 2)
            pe.wait_ge(banks_free, 4 + 280)
            for n in range(16):
                if n >= 4:
                    pe.wait_ge(head_var, 17 + n - 3)
                pe.matmul(PS[:, n % 4, 0:SEQ], ones[:, :], sq2[:, n, :], start=True, stop=True).then_inc(head_sum, 1)
            pe.wait_ge(modw_used, N_MOD * KC + MOD_RING)
            sum_mod(modlate.rearrange("p a b -> p (a b)"), MOD_FIRST, N_MOD - MOD_FIRST)
            pe.wait_ge(qk_ready, 4)
            with pe.Fori(0, 8) as g:
                for b in range(2):
                    pe.wait_ge(rot_done, g * 2 + b + 1)
                    pe.matmul(PS[:, b, 0:SEQ], swap[:, :], p2[:, g * 2 + b, :], start=True, stop=True).then_inc(swapped, 1)
            softmax_heads(a2, SEQ, 8, p2, ma_staged, ma_scores, ma_v, ma_p, ma_pt, ma_ptc, ma_out, False)
            def project(g, c):
                pe.wait_ge(bc_in[c % 2], (g + c // 2) * 32 + 32)
                pe.wait_ge(s5_u, g * 2 + (c + 1))
                for q in range(4):
                    for part in range(2):
                        last = pe.matmul(PS[:, q, part * SEQ:(part + 1) * SEQ],
                                         bst[32 * q:32 * q + 32, c % 2, part, :], ust[32 * q:32 * q + 32, :],
                                         start=True, stop=True)
                last.then_inc(s5_bu, 1)

            def read_out(g, c):
                pe.wait_ge(s5_x, g * 2 + (c + 1))
                for q in range(4):
                    if q == 0:
                        pe.wait_ge(s5_xp, g * 2 + (c + 1))
                    for n, part in enumerate((0, 2, 1, 1)):
                        last = pe.matmul(PS[32 * q:32 * q + 32, 4, 0:SEQ], cc[:, part, q, :], s5_out[n][:, q, :],
                                         start=n == 0, stop=n == 3)
                last.then_inc(s5_y, 1)

            project(0, 0)
            with pe.Fori(0, 3) as g:
                for b in range(2):
                    project(g, b + 1)
                    read_out(g, b)
            project(3, 1)
            read_out(3, 0)
            read_out(3, 1)
            pe.wait_ge(in_ready, SPLITS["ys0"])
            dense_half("w_glu", 280, 0)
            pe.wait_ge(in_ready, SPLITS["ya"])
            pe.wait_ge(banks_free, 4 + 288)
            dense_half("w_attn_br", 288, 8)
            pe.wait_ge(in_ready, SPLITS["ys"])
            dense_half("w_ssm_br", 304, 0)
            pe.wait_ge(in_ready, SPLITS["m2"])
            dense("w_out_2", 320, SEQ)
            sum_features(sqb, KC, 7, SEQ, 0, squares, 4, sums)
            pe.wait_ge(in_ready, SPLITS["h4"])
            dense("w_up", 336, SEQ)
            pe.wait_ge(act_ready, FC + 1)
            spread("w_down", FC // 4, True, N_SUB)

        @block.scalar
        def _(sc):
            s = Steps(sc, act_steps)
            f = sc.activation

            def split(g, first, n):
                for k in range(2):
                    m = first + n + k
                    sc.wait_ge(raw_in[m % RING], g * 32 + 16 * (m // RING + 1))
                    for q in range(2):
                        sc.wait_ge(quarters_used, g * 16 + (2 * m + q + 1))
                        f(whi[:, m % PAIRS, quarter(q)], raw[:, m % RING, quarter(q)], ACT.Copy).then_inc(hi_ready, 1)

            def copy_out(name, chunk0, tiles, at, dst, func, width):
                with sc.Fori(0, tiles // 4) as g:
                    for k in range(4):
                        split(g, FIRST[name] + 2 * at, 2 * k + 2)
                        sc.wait_ge(quarters_used, g * 16 + 2 * (PAIRS + FIRST[name] + 2 * (at + k + 1)))
                        f(dst(g * 4 + (at + k)), PS[:, k, 0:width], func).then_inc(banks_free, 1)

            def split_only(name, tiles):
                with sc.Fori(0, tiles // 4) as g:
                    for k in range(4):
                        split(g, FIRST[name], 2 * k + 2)

            def split_input(n, src, base, group, o):
                for k in range(src.shape[1] // group):
                    sc.wait_ge(in_f32, n + k + 1)
                    f(hhi[:, base + k * group:base + (k + 1) * group, o:], src[:, k * group:(k + 1) * group, :],
                      ACT.Copy).then_inc(in_hi, 1)

            def spread_in(name, turns, of, staged, last):
                def body(g, end):
                    for k in range(4):
                        if not (end and k == 3):
                            sc.wait_ge(quarters_used, g * 16 + 2 * (PAIRS + FIRST[name] + 2 * k))
                            f(hhi[:, (k + 1) % 2, META:], of(g * 4 + (k + 1)), ACT.Copy).then_inc(stage_hi, 1)
                        if not (end and last and k == 3):
                            split(g, FIRST[name], 2 * k + 2)
                f(hhi[:, 0, META:], of(0), ACT.Copy).then_inc(stage_hi, 1)
                with sc.Fori(0, turns - 1) as g:
                    body(g, False)
                body(turns - 1, True)

            def root(n):
                sc.wait_ge(var_ready, n)
                f(rstd[:, 0, :], rstd[:, 0, :], ACT.Sqrt).then_inc(rstd_ready, 1)

            def softmax_heads(a, keys, scores, v_ready, mx, ex, pt, ptc):
                nk = -(-keys // P)
                with sc.Fori(0, HEADS // 2) as g:
                    for b in range(2):
                        sc.wait_ge(scores, g * 2 + (b + 1))
                        sc.wait_ge(fa_free if nk == 3 else ma_free, g * 2 + (b + 1))
                        f(a[b]["vn"][:, 0:SEQ], PS[:, 3 * b + 2, 0:SEQ], ACT.Copy).then_inc(v_ready, 1)
                        if nk == 3:
                            f(a[b]["vn"][0:META, SEQ:SEQ + P], PS[0:META, 3 * b + 2, SEQ:SEQ + P],
                              ACT.Copy).then_inc(v_ready, 1)
                    for b in range(2):
                        Pm = a[b]["P"].rearrange("p (t s) -> p t s", t=2)
                        sc.wait_ge(mx, g * 2 + (b + 1))
                        for t in range(2):
                            f(Pm[:, t, 0:keys], Pm[:, t, 0:keys], ACT.Exp, bias=sums_of[b][:, 2 + t:3 + t],
                              accum_out=sums_of[b][:, 4 + t:5 + t]).then_inc(ex, 1)
                    for b in range(2):
                        sc.wait_ge(pt, g * 2 + (b + 1))
                        f(a[b]["PT"][:, 0:2 * SEQ], PS[:, 3 * b, :], ACT.Copy).then_inc(ptc, 1)
                        if nk == 3:
                            f(a[b]["PT"][0:META, 2 * SEQ:3 * SEQ], PS[0:META, 3 * b + 1, 0:SEQ],
                              ACT.Copy).then_inc(ptc, 1)

            sc.wait_ge(vecs_in, 32)
            sc.wait_ge(x_in, 16)
            f(small[:, 8:24], vecs[:, V_C:V_C + KC], ACT.Silu).then_inc(c_ready, 1)
            f(sq0[:, :, :], x0[:, :, :], ACT.Square).then_inc(squares, 1)
            root(1)
            for m in range(2):
                sc.wait_ge(raw_in[m], 16)
                sc.wait_ge(quarters_used, 2 * m + 2)
                f(whi[:, m, :], raw[:, m, :], ACT.Copy).then_inc(hi_ready, 2)
            split_input(0, h0, 0, 4, 0)
            copy_out("w_in", 0, 48, 0, lambda c: p1[:, c, :], ACT.Copy, KEYS)
            copy_out("w_in", 0, 8, 48, lambda c: p1[:, c, :], ACT.Sigmoid, KEYS)
            sc.wait_ge(banks_free, 4 + 56)
            sc.wait_ge(modw_used, MOD_FIRST * KC + MOD_RING)
            f(sq1[:, :, :], p1[:, 24:40, :], ACT.Square).then_inc(head_sq, 1)
            sc.wait_ge(head_var, 17)
            f(rs1[:, :, :], rs1[:, :, :], ACT.Sqrt).then_inc(head_rstd, 1)
            sc.wait_ge(flog_in, 1)
            s.link(f(logt, logf, ACT.Abs))
            s.link(f(logt, logt, ACT.Exp, scale=-1.0))
            f(logt, logt, ACT.Ln, bias=1.0).then_inc(flog_ln, 1)
            with s.loop(HEADS // 2, 4) as g:
                for b in range(2):
                    z = PS[:, 3 * b:3 * b + 2, :].rearrange("p a b -> p (a b)")[:, 0:768]
                    sc.wait_ge(sb_z, g * 2 + (b + 1))
                    s.link(f(a1[b]["a"], z, ACT.Abs))
                    s.link(f(a1[b]["e"], a1[b]["a"], ACT.Exp, scale=-1.0))
                    f(a1[b]["e"], a1[b]["e"], ACT.Ln, bias=1.0).then_inc(sb_soft, 1)
                for b in range(2):
                    sc.wait_ge(sb_free, g * 2 + (b + 1))
                    f(a1[b]["vn"], PS[:, 3 * b + 2, 0:384], ACT.Copy).then_inc(sb_v, 1)
                for b in range(2):
                    sc.wait_ge(sb_logw, g * 2 + (b + 1))
                    f(a1[b]["w"], a1[b]["w"], ACT.Exp).then_inc(sb_expw, 1)
            softmax_heads(a1, KEYS, fa_scores, fa_v, fa_max, fa_exp, fa_pt, fa_ptc)
            sc.wait_ge(fa_ptc, 16)
            sc.wait_ge(fa_staged, 17)
            f(sq1[:, 0:8, 0:SEQ], p1[:, 0:8, META:], ACT.Square).then_inc(msq, 1)
            f(sq1[:, 8:16, 0:SEQ], p1[:, 24:32, META:], ACT.Square).then_inc(msq, 1)
            sc.wait_ge(mvar, 1)
            sc.dma_start(keysx[:, :], d["keys"]).then_inc(keys_in, 16)
            sc.dma_start(xT[:, :, :], d["x"]).then_inc(x0_again, 16)
            f(rstd[:, :, 0:SEQ], rstd[:, :, 0:SEQ], ACT.Sqrt).then_inc(mrstd, 1)
            split_input(SPLITS["h"], hm, 0, 4, META)
            split_only("w_out", 16)
            sc.wait_ge(banks_free, 4 + 72)
            f(sq0[:, :, META:], xT[:, :, META:], ACT.Square).then_inc(squares, 1)
            sc.dma_start(d["x1"], xT[:, :, META:]).then_inc(x1_saved, 16)
            root(2)
            split_input(SPLITS["merged"], hm, 0, 4, META)
            copy_out("w_query", 72, 16, 0, lambda c: qx[:, c, :], ACT.Copy, SEQ)
            sc.wait_ge(x1_saved, 16)
            for n in range(8):
                sc.wait_ge(sx_done, n + 1)
                f(sx[:, n // 4, (n % 4) * 4:(n % 4) * 4 + 4, :],
                  PS[:, n, :].rearrange("p (a b) -> p a b", a=4), ACT.Copy).then_inc(sx_copied, 1)
            def gelus(g, start, k):
                split(g, FIRST["peer_u"] + 2 * start, 2 * k + 2)
                sc.wait_ge(quarters_used, g * 16 + 2 * (PAIRS + FIRST["peer_u"] + 2 * (start + k + 1)))
                f(ga[:, g * 4 + (start + k), :], PS[:, k, 0:SEQ], ACT.Gelu).then_inc(banks_free, 1)

            def gelu_out(start, turns):
                with sc.Fori(0, turns) as g:
                    for k in range(4):
                        gelus(g, start, k)
            with sc.Fori(0, 16) as u:
                gelus(u, 0, 0)
                gelus(u, 0, 1)
                gelus(u, 0, 2)
                sc.wait_ge(best_ready, u + 1)
                f(best, best, ACT.Exp, bias=small[:, 6:7], accum_out=small[:, 7:8]).then_inc(best_exp, 1)
                gelus(u, 0, 3)
            gelu_out(64, (TAIL - 64) // 4)
            sc.wait_ge(picks_ready, 6)
            gelu_out(TAIL, (N_SUB - TAIL) // 4)
            sc.wait_ge(gates_used, 4 + SEQ // 4)
            spread_in("peer_v", N_SUB // 4, lambda j: ga[:, j, :], 0, False)
            sc.wait_ge(quarters_used, 2 * (PAIRS + FIRST["w_in_2"]))
            sc.dma_start(x2[:, :, :], d["x1"]).then_inc(x1_back, 16)
            sc.wait_ge(experts_done, 1)
            sc.wait_ge(x2_ready, 1)
            sc.dma_start(convw, d["convw"]).then_inc(lam_in, 16)
            sc.dma_start(posi, d["pos"]).then_inc(lam_in, 16)
            sc.dma_start(lamp[:, 0:3, :], d["lam"]).then_inc(lam_in, 16)
            f(sqb[:, :, :], x2[:, :, :], ACT.Square).then_inc(squares, 1)
            root(3)
            split_input(SPLITS["h2"], h2b, 0, 4, META)
            copy_out("w_in_2", 216, 32, 0, lambda c: p2[:, c, :], ACT.Copy, SEQ)
            copy_out("w_in_2", 216, 32, 32, lambda c: p2[:, c, :], ACT.Sigmoid, SEQ)
            sc.wait_ge(banks_free, 4 + 280)
            f(sq2[:, :, :], p2[:, 0:16, :], ACT.Square).then_inc(head_sq, 1)
            sc.wait_ge(head_var, 17 + 17)
            f(rs2[:, :, :], rs2[:, :, :], ACT.Sqrt).then_inc(head_rstd, 1)
            sc.wait_ge(ang_ready, 1)
            s.link(f(sinr, angr, ACT.Sin))
            s.link(f(cosr, angr, ACT.Sin, scale=0.5))
            f(cosr, cosr, ACT.Square).then_inc(sin_ready, 1)
            softmax_heads(a2, SEQ, ma_scores, ma_v, ma_max, ma_exp, ma_pt, ma_ptc)
            sc.wait_ge(lam_in, 48)
            f(lamp[:, 2, :], lamp[:, 2, :], ACT.Exp).then_inc(lam_a, 1)
            sc.wait_ge(lam_b, 1)
            f(lamp[:, 3, :], lamp[:, 3, :], ACT.Exp).then_inc(lam_c, 1)
            f(sq2[:, 12, 0:32], lamp[:, 4, :], ACT.Sin).then_inc(lam_c, 1)
            f(sq2[:, 13, 0:32], lamp[:, 4, :], ACT.Sin, scale=0.5).then_inc(lam_c, 1)
            sc.wait_ge(s5_lam, 1)

            def angles(g, c):
                for q in range(4):
                    f(s5_num[:, q, :], ramp[:, :], ACT.Copy, scale=lamp[:, 2, bass.ds(g * 8 + (c * 4 + q), 1)])
                for q in range(4):
                    last = f(s5_ang[:, q, :], ramp[:, :], ACT.Copy,
                             scale=lamp[:, 4, bass.ds(g * 8 + (c * 4 + q), 1)])
                last.then_inc(s5_raw, 1)
                sc.wait_ge(s5_angr, g * 2 + (c + 1))
                if c >= 2:
                    sc.wait_ge(s5_xp, g * 2 + (c - 1))
                s.link(f(s5_sin[c % 2], s5_ang, ACT.Sin))
                s.link(f(s5_cos[c % 2], s5_ang, ACT.Sin, scale=0.5))
                s.link(f(s5_cos[c % 2], s5_cos[c % 2], ACT.Square))
                f(s5_cos[c % 2], s5_cos[c % 2], ACT.Copy, scale=-2.0, bias=1.0).then_inc(s5_sinr, 1)

            def gelu(g, c):
                sc.wait_ge(s5_ys, g * 2 + (c + 1))
                f(p2[:, g * 2 + (c + 24), :], ysum, ACT.Gelu_apprx_tanh).then_inc(s5_gel, 1)

            angles(0, 0)
            angles(0, 1)
            with s.loop(3, 6) as g:
                for b in range(2):
                    angles(g, b + 2)
                    gelu(g, b)
            gelu(3, 0)
            gelu(3, 1)
            split_input(SPLITS["h3"], p2[:, 24:32, :], 0, 8, META)
            split_input(SPLITS["ys0"], p2[:, 0:8, :], 8, 8, META)
            for k in range(8):
                if k % 2 == 0:
                    split(0, FIRST["w_glu"], k + 2)
                sc.wait_ge(quarters_used, 2 * (PAIRS + FIRST["w_glu"] + k + 1))
                f(glug[:, k, :], PS[:, k % 4, 0:SEQ], ACT.Sigmoid,
                  bias=vecs[:, V_BGLU + k:V_BGLU + k + 1]).then_inc(banks_free, 1)
            split_only("w_attn_br", 8)
            split_input(SPLITS["ya"], p2[:, 24:32, :], 0, 8, META)
            split_only("w_ssm_br", 8)
            split_input(SPLITS["ys"], h2b, 0, 8, META)
            split_only("w_out_2", 16)
            sc.wait_ge(banks_free, 4 + 336)
            f(sqb[:, :, :], x2[:, :, :], ACT.Square).then_inc(squares, 1)
            root(4)
            split_input(SPLITS["m2"], h2b, 0, 4, META)
            with sc.Fori(0, 22) as g:
                for k in range(4):
                    split(g, FIRST["w_up"], 2 * k + 2)
                    sc.wait_ge(quarters_used, g * 16 + 2 * (PAIRS + FIRST["w_up"] + 2 * (k + 1)))
                    sc.wait_ge(act_ready, g * 2 + k // 2 + 1)
                    f(cva if k % 2 == 0 else cgt, PS[:, k, 0:SEQ], ACT.Identity,
                      scale=convw[:, 2, bass.ds(g * 4 + k, 1)], bias=convw[:, 3, bass.ds(g * 4 + k, 1)]).then_inc(up_pre, 1)
                    if k % 2 == 1:
                        sc.wait_ge(banks_free, g * 4 + (4 + 336 + k + 1))
                        f(cgt, cgt, ACT.Silu).then_inc(up_silu, 1)
            sc.wait_ge(act_ready, FC + 1)
            spread_in("w_down", FC // 4, lambda j: act[:, j, :], N_SUB, True)

        @block.vector
        def _(dv):
            s = Steps(dv, dve_steps)
            link = s.link

            def move(to, of):
                return dv.tensor_scalar(to, of, 1.0, None, ALU.mult)

            def hold():
                dv.memset(small[:, 30:31], 0.0)

            def split(g, first, n):
                for k in range(2):
                    m = first + n + k
                    for q in range(2):
                        dv.wait_ge(hi_ready, g * 16 + (2 * m + q + 1))
                        dv.tensor_tensor(wlo[:, m % PAIRS, quarter(q)], raw[:, m % RING, quarter(q)],
                                         whi[:, m % PAIRS, quarter(q)], ALU.subtract).then_inc(lo_ready, 1)

            def split_only(name, tiles):
                with dv.Fori(0, tiles // 4) as g:
                    for k in range(4):
                        split(g, FIRST[name], 2 * k + 2)

            def split_input(n, src, base, group, o):
                for k in range(src.shape[1] // group):
                    dv.wait_ge(in_hi, n + k + 1)
                    where = slice(base + k * group, base + (k + 1) * group)
                    dv.tensor_tensor(hlo[:, where, o:], src[:, k * group:(k + 1) * group, :], hhi[:, where, o:],
                                     ALU.subtract).then_inc(in_ready, 1)

            def spread_in(name, turns, of, staged, last):
                def body(g, end):
                    for k in range(4):
                        if not (end and k == 3):
                            dv.wait_ge(stage_hi, g * 4 + (staged + k + 2))
                            dv.tensor_tensor(hlo[:, (k + 1) % 2, META:], of(g * 4 + (k + 1)), hhi[:, (k + 1) % 2, META:],
                                             ALU.subtract).then_inc(stage_lo, 1)
                        if not (end and last and k == 3):
                            split(g, FIRST[name], 2 * k + 2)
                dv.wait_ge(stage_hi, staged + 1)
                dv.tensor_tensor(hlo[:, 0, META:], of(0), hhi[:, 0, META:], ALU.subtract).then_inc(stage_lo, 1)
                with dv.Fori(0, turns - 1) as g:
                    body(g, False)
                body(turns - 1, True)

            def normalise(turn, width, x, h, group0, gain, shift=None):
                o = KEYS - width
                dv.wait_ge(sums, turn)
                link(dv.tensor_scalar(rstd[:, 1, 0:width], PS[:, 7, 0:width], 1.0 / D, EPS, ALU.mult, ALU.add))
                dv.reciprocal(rstd[:, 0, 0:width], rstd[:, 1, 0:width]).then_inc(var_ready, 1)
                if turn == 1:
                    for m in range(2):
                        dv.wait_ge(hi_ready, 2 * m + 2)
                        dv.tensor_tensor(wlo[:, m, :], raw[:, m, :], whi[:, m, :], ALU.subtract).then_inc(lo_ready, 2)
                dv.wait_ge(rstd_ready, turn)
                for c in range(KC):
                    i = dv.scalar_tensor_tensor(h[:, c, :], x[:, c, :], gain(c), rstd[:, 0, 0:width], ALU.mult, ALU.mult)
                    if shift is not None:
                        link(i)
                        i = dv.tensor_scalar(h[:, c, :], h[:, c, :], shift(c), None, ALU.add)
                    link(i)
                    if c % 4 == 3:
                        dv.memset(small[:, 26:27], 0.0).then_inc(in_f32, 1)
                        dv.wait_ge(in_f32, group0 + c // 4 + 1)
                split_input(group0, h, 0, 4, o)

            def head_norms(turn, sq, rs, src, base, width, gains):
                for n in range(16):
                    dv.wait_ge(head_sum, turn * 16 + n + 1)
                    dv.tensor_scalar(rs[:, n, :], PS[:, n % 4, 0:width], 1.0 / P, EPS, ALU.mult, ALU.add).then_inc(head_var, 1)
                dv.wait_ge(head_var, turn * 17 + 16)
                dv.reciprocal(rs[:, :, :], rs[:, :, :]).then_inc(head_var, 1)
                dv.wait_ge(head_rstd, turn + 1)
                for half in range(2):
                    dv.scalar_tensor_tensor(src[:, base + half * 8:base + half * 8 + 8, :],
                                            src[:, base + half * 8:base + half * 8 + 8, :],
                                            vecs[:, gains[half]:gains[half] + 1], rs[:, half * 8:half * 8 + 8, :],
                                            ALU.mult, ALU.mult).then_inc(qk_ready, 1)
                dv.wait_ge(qk_ready, turn * 2 + 2)

            def softmax_heads(a, keys, src, qbase, vbase, o, staged, scores, mx, ex, p_ready, done, free):
                cm = causal[:, :, KEYS - keys:]
                Pm = [a[b]["P"].rearrange("p (t s) -> p t s", t=2)[:, :, 0:keys] for b in range(2)]
                def stage_heads(g, ahead):
                    for b in range(2):
                        dv.tensor_scalar(a[b]["q"], src[:, g * 2 + (2 * ahead + b + qbase), o:], SCALE, None,
                                         ALU.mult).then_inc(staged, 1)
                        move(a[b]["v"][:, 0:keys], src[:, g * 2 + (2 * ahead + b + vbase), 0:keys]).then_inc(staged, 1)

                def heads(g, last):
                    for b in range(2):
                        dv.wait_ge(scores, g * 2 + (b + 1))
                        link(dv.tensor_tensor(Pm[b], PS[:, 3 * b:3 * b + 2, 0:keys], cm, ALU.add))
                        link(dv.tensor_reduce(sums_of[b][:, 0:2], Pm[b], AX.X, ALU.max))
                        dv.tensor_scalar(sums_of[b][:, 2:4], sums_of[b][:, 0:2], -1.0, None, ALU.mult).then_inc(mx, 1)
                    if not last:
                        stage_heads(g, 1)
                    for b in range(2):
                        dv.wait_ge(ex, g * 4 + (b * 2 + 2))
                        link(dv.reciprocal(sums_of[b][:, 6:8], sums_of[b][:, 4:6]))
                        dv.tensor_tensor(Pm[b], Pm[b], sums_of[b][:, 6:8].unsqueeze(2).to_broadcast([P, 2, keys]),
                                         ALU.mult).then_inc(p_ready, 1)
                    for b in range(2):
                        dv.wait_ge(done, g * 2 + (b + 1))
                        move(src[:, g * 2 + (b + qbase), o:], PS[:, 6 + b, 0:SEQ]).then_inc(free, 1)

                stage_heads(0, 0)
                with s.loop(HEADS // 2 - 1, 6) as g:
                    heads(g, False)
                heads(HEADS // 2 - 1, True)
                dv.wait_ge(free, HEADS + 2)

            def reduce_angle(ang, num):
                link(dv.tensor_scalar(num, num, ROUND, -ROUND, ALU.add, ALU.add))
                for c in TWO_PI_PARTS:
                    link(dv.scalar_tensor_tensor(ang, num, -float(c), ang, ALU.mult, ALU.add))
                return dv.tensor_scalar(ang, ang, PI_BELOW, -PI_BELOW, ALU.min, ALU.max)

            link(dv.memset(ones[:, :], 1.0))
            link(dv.memset(rstd[:, :, :], 1.0))
            dv.memset(small[:, 26:27], 0.0).then_inc(lo_ready, 2 * RING)
            dv.memset(gmod[:, 15:16], 0.0).then_inc(quarters_used, 2 * PAIRS)
            dv.memset(small[:, 27:28], 0.0).then_inc(banks_free, 4)
            dv.memset(small[:, 28:29], 0.0).then_inc(modw_used, MOD_RING)
            for n, one in enumerate((s5_gel, sb_free, sb_free, fa_free, fa_free, ma_free, ma_free, rot_done, act_ready)):
                dv.memset(gmod[:, n:n + 1], 0.0).then_inc(one, 1)
            dv.memset(small[:, 29:30], 0.0).then_inc(consts_ready, 1)
            dv.wait_ge(consts_ready, 2)
            dv.wait_ge(vecs_in, 32)
            dv.wait_ge(x_in, 16)
            vec = lambda c: vecs[:, c:c + 1]
            normalise(1, KEYS, x0, h0, 0, lambda c: vec(V_MIX + c))
            dv.wait_ge(c_ready, 1)
            done = 0
            with dv.Fori(0, MOD_FIRST) as part:
                for kc in range(KC):
                    split(part * 4, 0, 2 * kc + 2)
                    dv.wait_ge(modw_in[kc % MOD_RING], part * (KC // MOD_RING * 16) + (kc // MOD_RING + 1) * 16)
                    dv.wait_ge(modw_used, part * KC + (kc + MOD_RING))
                    if kc == 0:
                        i = dv.tensor_scalar(modacc[:, part, :], modring[:, 0, :], small[:, 8:9], None, ALU.mult)
                    else:
                        i = dv.scalar_tensor_tensor(modacc[:, part, :], modring[:, kc % MOD_RING, :],
                                                    small[:, 8 + kc:9 + kc], modacc[:, part, :], ALU.mult, ALU.add)
                    i.then_inc(modw_used, 1)
            with dv.Fori(0, 2) as g:
                for k in range(4):
                    split(g, 96, 2 * k + 2)
            head_norms(0, sq1, rs1, p1, 24, KEYS, (V_QG, V_KG))
            dv.wait_ge(flog, 1)
            dv.wait_ge(mod_summed, 1)
            n = MOD_FIRST * KC
            link(dv.tensor_tensor(mod[:, 0:n], PS[:, 6, 0:n], vecs[:, V_BMOD:V_BMOD + n], ALU.add))
            dv.tensor_scalar(logf, PS[0:HEADS, 5, 0:KEYS], vecs[0:HEADS, V_BF:V_BF + 1], None, ALU.add).then_inc(flog_in, 1)
            dv.wait_ge(flog_ln, 1)
            link(dv.scalar_tensor_tensor(logf, logf, 0.0, logt, ALU.min, ALU.subtract))
            link(dv.tensor_tensor_scan(sumf, ones[0:HEADS, 0:1].to_broadcast([HEADS, KEYS]), logf, 0.0, ALU.mult, ALU.add))
            dv.wait_ge(stage_zero, 1)
            link(dv.scalar_tensor_tensor(negf[:, :, :], pickh[:, :, :], -1.0,
                                         sumf.unsqueeze(1).to_broadcast([HEADS, HEADS, KEYS]), ALU.mult, ALU.mult))
            for b in range(2):
                link(dv.memset(a1[b]["k"][:, KEYS:], 0.0))
                link(dv.memset(a1[b]["v"][:, KEYS:], 0.0))
            seenf = seen[:, :, :].rearrange("p a b -> p (a b)")

            def sb_stage(g, ahead):
                for b in range(2):
                    n = 2 * ahead + b
                    dv.tensor_scalar(a1[b]["q"], p1[:, g * 2 + n, META:], SCALE, None, ALU.mult).then_inc(sb_staged, 1)
                    move(a1[b]["k"][:, 0:KEYS], p1[:, g * 2 + (n + 8), :]).then_inc(sb_staged, 1)
                    move(a1[b]["v"][:, 0:KEYS], p1[:, g * 2 + (n + 16), :]).then_inc(sb_staged, 1)

            def sb_heads(g, last):
                for b in range(2):
                    z = PS[:, 3 * b:3 * b + 2, :].rearrange("p a b -> p (a b)")[:, 0:768]
                    L, w = a1[b]["L"], a1[b]["w"]
                    dv.wait_ge(sb_soft, g * 2 + (b + 1))
                    link(dv.scalar_tensor_tensor(L, z, 0.0, a1[b]["e"], ALU.max, ALU.add))
                    link(dv.tensor_tensor(w, z, L, ALU.subtract))
                    dv.scalar_tensor_tensor(L, L, -1.0, seenf, ALU.mult, ALU.mult).then_inc(sb_log, 1)
                if not last:
                    sb_stage(g, 1)
                for b in range(2):
                    after = PS[:, 3 * b:3 * b + 2, :].rearrange("p a b -> p (a b)")[:, 0:768]
                    w = a1[b]["w"]
                    dv.wait_ge(sb_after, g * 2 + (b + 1))
                    link(dv.tensor_tensor(w, w, after, ALU.add))
                    dv.tensor_scalar(w, w, 0.0, None, ALU.min).then_inc(sb_logw, 1)
                for b in range(2):
                    w = a1[b]["w"]
                    dv.wait_ge(sb_expw, g * 2 + (b + 1))
                    dv.tensor_tensor(w, w, seenf, ALU.mult).then_inc(sb_w, 1)
                for b in range(2):
                    dv.wait_ge(sb_out, g * 2 + (b + 1))
                    move(p1[:, g * 2 + b, META:], PS[:, 6 + b, 0:SEQ]).then_inc(sb_free, 1)

            sb_stage(0, 0)
            with s.loop(HEADS // 2 - 1, 6) as g:
                sb_heads(g, False)
            sb_heads(HEADS // 2 - 1, True)
            dv.wait_ge(sb_free, HEADS + 2)
            softmax_heads(a1, KEYS, p1, 24, 40, META, fa_staged, fa_scores, fa_max, fa_exp, fa_p, fa_out, fa_free)
            dv.memset(small[:, 26:27], 0.0).then_inc(fa_staged, 1)
            dv.wait_ge(msum, 2)
            link(dv.tensor_scalar(rs1[:, 0:2, 0:SEQ], PS[:, 7, :].rearrange("p (a b) -> p a b", a=2),
                                  1.0 / 1024, EPS, ALU.mult, ALU.add))
            dv.reciprocal(rstd[:, :, 0:SEQ], rs1[:, 0:2, 0:SEQ]).then_inc(mvar, 1)
            dv.wait_ge(mrstd, 1)
            for c in range(8):
                link(dv.scalar_tensor_tensor(hm[:, c, :], p1[:, c, META:], vec(V_SBG + c), rstd[:, 0, 0:SEQ],
                                             ALU.mult, ALU.mult))
                link(dv.scalar_tensor_tensor(hm[:, 8 + c, :], p1[:, 24 + c, META:], vec(V_FOXG + c),
                                             rstd[:, 1, 0:SEQ], ALU.mult, ALU.mult))
            link(dv.tensor_tensor(hm[:, 8:16, :], hm[:, 8:16, :], p1[:, 48:56, META:], ALU.mult))
            dv.memset(small[:, 26:27], 0.0).then_inc(in_f32, 4)
            split_input(SPLITS["h"], hm, 0, 4, META)
            dv.wait_ge(x0_again, 16)
            with dv.Fori(0, 4) as g:
                for k in range(4):
                    split(g, FIRST["w_out"], 2 * k + 2)
                    dv.wait_ge(quarters_used, g * 16 + 2 * (PAIRS + FIRST["w_out"] + 2 * (k + 1)))
                    dv.tensor_tensor(xT[:, g * 4 + k, META:], xT[:, g * 4 + k, META:], PS[:, k, 0:SEQ],
                                     ALU.add).then_inc(banks_free, 1)
            dv.wait_ge(banks_free, 4 + 72)
            normalise(2, SEQ, xT[:, :, META:], hm, SPLITS["merged"], lambda c: vec(V_FFN + c))
            split_only("w_query", 16)
            dv.wait_ge(sx_copied, 8)
            v1, v2, vb = (small_t[:, k, :] for k in range(3))
            with s.loop(16, 28) as u:
                split(u, FIRST["peer_u"], 2)
                t_h = sx.rearrange("p t (h s) n -> p (t h) (s n)", s=2)
                link(move(st, t_h[:, u, :]))
                for side, v in ((0, v1), (1, v2)):
                    a = st[:, side * N_SUB:(side + 1) * N_SUB]
                    b = st2[:, side * N_SUB:(side + 1) * N_SUB]
                    hold()
                    link(dv.max(v[:, 0:8], a))
                    hold()
                    dv.max_index(idx[:, side, 0:8], v[:, 0:8], a)
                    link(dv.match_replace(b, v[:, 0:8], a, LOWEST))
                    hold()
                    link(dv.max(v[:, 8:16], b))
                    hold()
                    link(dv.max_index(idx[:, side, 8:16], v[:, 8:16], b))
                link(dv.tensor_copy(small_t[:, 3:5, :], idx[:, 0:2, :]))
                split(u, FIRST["peer_u"], 4)
                c3 = cand.rearrange("p (a b) -> p a b", a=16)
                link(dv.tensor_tensor(c3, v1.unsqueeze(2).to_broadcast([P, 16, 16]),
                                      v2.unsqueeze(1).to_broadcast([P, 16, 16]), ALU.add))
                hold()
                link(dv.max(vb[:, 0:8], cand))
                link(dv.tensor_scalar(small[:, 6:7], vb[:, 0:1], -1.0, None, ALU.mult))
                hold()
                dv.max_index(idx[:, 2, 0:8], vb[:, 0:8], cand)
                link(dv.match_replace(st2, vb[:, 0:8], cand, LOWEST))
                hold()
                link(dv.max(vb[:, 8:16], st2))
                link(dv.tensor_copy(best, vb))
                dv.memset(small[:, 26:27], 0.0).then_inc(best_ready, 1)
                link(dv.max_index(idx[:, 2, 8:16], vb[:, 8:16], st2))
                split(u, FIRST["peer_u"], 6)
                link(dv.tensor_scalar(idx[:, 0, :], idx[:, 2, :], 4, None, ALU.logical_shift_right))
                link(dv.tensor_scalar(idx[:, 1, :], idx[:, 2, :], 15, None, ALU.bitwise_and))
                link(dv.tensor_copy(small_t[:, 5:7, :], idx[:, 0:2, :]))
                for side in range(2):
                    link(dv.tensor_tensor(oneh, ramp[:, 0:16].unsqueeze(1).to_broadcast([P, 16, 16]),
                                          small_t[:, 5 + side, :].unsqueeze(2).to_broadcast([P, 16, 16]), ALU.is_equal))
                    link(dv.tensor_tensor(oneh, oneh, small_t[:, 3 + side, :].unsqueeze(1).to_broadcast([P, 16, 16]),
                                          ALU.mult))
                    link(dv.tensor_reduce(small_t[:, 7 + side, :], oneh, AX.X, ALU.add))
                split(u, FIRST["peer_u"], 8)
                dv.wait_ge(best_exp, u + 1)
                link(dv.reciprocal(small[:, 27:28], small[:, 7:8]))
                link(dv.tensor_scalar(small_t[:, 9, :], best, small[:, 27:28], None, ALU.mult))
                for c in range(3):
                    move(sel8[:, c, u, :], small_t[:, 7 + c, :]).then_inc(picks_done, 1)
            with dv.Fori(16, TAIL // 4) as g:
                for k in range(4):
                    split(g, FIRST["peer_u"], 2 * k + 2)
            dv.wait_ge(picks_turned, 6)
            for n in range(6):
                dv.tensor_copy(picked[:, n % 3, (n // 3) * P:(n // 3 + 1) * P],
                               PS[:, 4 + n // 4, (n % 4) * P:(n % 4 + 1) * P]).then_inc(picks_ready, 1)
            with dv.Fori(TAIL // 4, N_SUB // 4) as g:
                for k in range(4):
                    split(g, FIRST["peer_u"], 2 * k + 2)
            dv.wait_ge(picks_ready, 6)
            dv.wait_ge(banks_free, 4 + 216)
            dv.wait_ge(quarters_used, 2 * (PAIRS + FIRST["peer_v"]))
            dv.memset(small[:, 26:27], 0.0).then_inc(gates_used, 4)

            def one_hots(g, b):
                for side, one in ((1, oneB), (0, oneA)):
                    dv.tensor_tensor(one[:, b % 4, :, :], ramp[:, 0:P].unsqueeze(1).to_broadcast([P, 4, P]),
                                     picked[:, side, bass.ds(g * 16 + b * 4, 4)].unsqueeze(2).to_broadcast([P, 4, P]),
                                     ALU.is_equal).then_inc(hots, 1)

            def apply_gates(g, b):
                dv.wait_ge(gates_done, g * 4 + b + 1)
                part = ga[:, :, bass.ds(g * 16 + b * 4, 4)]
                dv.tensor_tensor(part, part, PS[:, b, :].rearrange("p (t j) -> p j t", t=4),
                                 ALU.mult).then_inc(gates_used, 1)

            one_hots(0, 0)
            one_hots(0, 1)
            with dv.Fori(0, SEQ // 16 - 1) as g:
                for b in range(4):
                    one_hots(g, b + 2)
                    apply_gates(g, b)
            for b in range(4):
                if b < 2:
                    one_hots(SEQ // 16 - 1, b + 2)
                apply_gates(SEQ // 16 - 1, b)
            dv.wait_ge(gates_used, 4 + SEQ // 4)
            spread_in("peer_v", N_SUB // 4, lambda j: ga[:, j, :], 0, False)
            dv.wait_ge(quarters_used, 2 * (PAIRS + FIRST["w_in_2"]))
            dv.wait_ge(x1_back, 16)
            link(dv.tensor_tensor(x2[:, :, :], x2[:, :, :], PS[:, :, :].rearrange("p a (b t) -> p (a b) t", b=2), ALU.add))
            dv.memset(small[:, 26:27], 0.0).then_inc(experts_done, 1)
            dv.memset(small[:, 27:28], 0.0).then_inc(x2_ready, 1)
            link(dv.scalar_tensor_tensor(gmod[:, :], mod[:, 16:32], 1.0, vecs[:, V_N1:V_N1 + KC], ALU.add, ALU.mult))
            normalise(3, SEQ, x2, h2b, SPLITS["h2"], lambda c: gmod[:, c:c + 1], lambda c: mod[:, c:c + 1])
            with dv.Fori(0, N_MOD - MOD_FIRST) as part:
                for kc in range(KC):
                    split(part * 5, FIRST["w_in_2"], 2 * (kc + (kc + 3) // 4) + 2)
                    dv.wait_ge(modl_in[kc % MOD_LATE_RING],
                               part * (KC // MOD_LATE_RING * 16) + (kc // MOD_LATE_RING + 1) * 16)
                    dv.wait_ge(modw_used, part * KC + (MOD_FIRST * KC + kc + MOD_RING))
                    if kc == 0:
                        i = dv.tensor_scalar(modlate[:, part, :], modlring[:, 0, :], small[:, 8:9], None, ALU.mult)
                    else:
                        i = dv.scalar_tensor_tensor(modlate[:, part, :], modlring[:, kc % MOD_LATE_RING, :],
                                                    small[:, 8 + kc:9 + kc], modlate[:, part, :], ALU.mult, ALU.add)
                    i.then_inc(modw_used, 1)
                    if kc % 4 == 0:
                        split(part * 5, FIRST["w_in_2"], 2 * (kc + (kc + 3) // 4 + 1) + 2)
            split(15, FIRST["w_in_2"], 2)
            split(15, FIRST["w_in_2"], 4)
            split(15, FIRST["w_in_2"], 6)
            split(15, FIRST["w_in_2"], 8)
            head_norms(1, sq2, rs2, p2, 0, SEQ, (V_QG2, V_KG2))
            dv.wait_ge(lam_in, 48)
            dv.wait_ge(mod_summed, 2)
            n = MOD_FIRST * KC
            link(dv.tensor_tensor(mod[:, n:], PS[:, 6, n:N_MOD * KC], vecs[:, V_BMOD + n:V_BMOD + N_MOD * KC], ALU.add))
            link(dv.tensor_copy(numr, posi))
            link(dv.tensor_scalar(angr, numr, vec(V_FREQ), None, ALU.mult))
            link(dv.tensor_scalar(numr, angr, INV_2PI, None, ALU.mult))
            reduce_angle(angr, numr).then_inc(ang_ready, 1)
            dv.wait_ge(sin_ready, 1)
            link(dv.tensor_scalar(cosr, cosr, -2.0, 1.0, ALU.mult, ALU.add))
            link(dv.tensor_scalar(sinr[0:64, :], sinr[0:64, :], -1.0, None, ALU.mult))
            with s.loop(8, 4) as g:
                for b in range(2):
                    dv.wait_ge(swapped, g * 2 + b + 1)
                    link(dv.tensor_tensor(numr, PS[:, b, 0:SEQ], sinr, ALU.mult))
                    link(dv.tensor_tensor(p2[:, g * 2 + b, :], p2[:, g * 2 + b, :], cosr, ALU.mult))
                    dv.tensor_tensor(p2[:, g * 2 + b, :], p2[:, g * 2 + b, :], numr, ALU.add).then_inc(rot_done, 1)
                    dv.wait_ge(rot_done, g * 2 + b + 2)
            softmax_heads(a2, SEQ, p2, 0, 16, 0, ma_staged, ma_scores, ma_max, ma_exp, ma_p, ma_out, ma_free)
            lr, li, dt, mag, phi = (lamp[:, k, :] for k in range(5))
            t = [sq2[:, 8 + k, 0:32] for k in range(4)]
            sn, sh = sq2[:, 12, 0:32], sq2[:, 13, 0:32]
            cre, cim = small2[:, 0, :], small2[:, 1, :]
            dv.wait_ge(lam_a, 1)
            link(dv.tensor_tensor(mag, lr, dt, ALU.mult))
            link(dv.tensor_tensor(phi, li, dt, ALU.mult))
            link(dv.tensor_scalar(t[0], phi, INV_2PI, None, ALU.mult))
            reduce_angle(phi, t[0]).then_inc(lam_b, 1)
            dv.wait_ge(lam_c, 3)
            link(dv.tensor_tensor(t[0], sh, sh, ALU.mult))
            link(dv.tensor_tensor(t[0], t[0], mag, ALU.mult))
            link(dv.tensor_scalar(t[1], mag, -1.0, None, ALU.add))
            link(dv.scalar_tensor_tensor(t[0], t[0], -2.0, t[1], ALU.mult, ALU.add))
            link(dv.tensor_tensor(t[1], mag, sn, ALU.mult))
            link(dv.tensor_tensor(t[2], lr, lr, ALU.mult))
            link(dv.tensor_tensor(t[3], li, li, ALU.mult))
            link(dv.tensor_tensor(t[2], t[2], t[3], ALU.add))
            link(dv.reciprocal(t[3], t[2]))
            link(dv.tensor_tensor(cre, t[0], lr, ALU.mult))
            link(dv.tensor_tensor(t[2], t[1], li, ALU.mult))
            link(dv.tensor_tensor(cre, cre, t[2], ALU.add))
            link(dv.tensor_tensor(cre, cre, t[3], ALU.mult))
            link(dv.tensor_tensor(cim, t[1], lr, ALU.mult))
            link(dv.tensor_tensor(t[2], t[0], li, ALU.mult))
            link(dv.tensor_tensor(cim, cim, t[2], ALU.subtract))
            link(dv.tensor_tensor(cim, cim, t[3], ALU.mult))
            link(dv.tensor_scalar(dt, phi, INV_2PI, None, ALU.mult))
            dv.memset(small[:, 26:27], 0.0).then_inc(s5_lam, 1)
            wide = lambda v, g, c: v[:, bass.ds(g * 8 + c * 4, 4)].unsqueeze(2).to_broadcast([P, 4, 32])
            bre = PS[:, 0:4, 0:SEQ]
            bim = PS[:, 0:4, SEQ:]

            def output(g, c):
                dv.wait_ge(s5_y, g * 2 + (c + 1))
                dv.wait_ge(s5_gel, g * 2 + c + 1)
                link(dv.scalar_tensor_tensor(ysum, p2[:, g * 2 + (c + 24), :], vecs[:, bass.ds(g * 2 + (c + V_D), 1)],
                                             PS[:, 4, 0:SEQ], ALU.mult, ALU.add))
                dv.memset(small[:, 27:28], 0.0).then_inc(s5_ys, 1)

            def chunk(g, c, first=False, last=False):
                cos, sin = s5_cos[c % 2], s5_sin[c % 2]
                if not last:
                    dv.wait_ge(s5_raw, g * 2 + (c + 2))
                    reduce_angle(s5_ang, s5_num).then_inc(s5_angr, 1)
                if not first:
                    dv.wait_ge(s5_xp, g * 2 + c)
                dv.wait_ge(s5_sinr, g * 2 + (c + 1))
                dv.wait_ge(s5_bu, g * 2 + (c + 1))
                dv.tensor_tensor(s5_p, cos, bre, ALU.mult)
                dv.tensor_tensor(s5_ta, sin, bim, ALU.mult)
                dv.tensor_tensor(s5_q, cos, bim, ALU.mult)
                link(dv.tensor_tensor(s5_tb, sin, bre, ALU.mult))
                if not last:
                    move(ust, p2[:, g * 2 + (c + 25), :]).then_inc(s5_u, 1)
                dv.tensor_tensor(s5_p, s5_p, s5_ta, ALU.add)
                link(dv.tensor_tensor(s5_q, s5_q, s5_tb, ALU.subtract))
                for q in range(4):
                    decay = mag[:, bass.ds(g * 8 + (c * 4 + q), 1)].to_broadcast([P, SEQ])
                    dv.tensor_tensor_scan(s5_zr[:, q, :], decay, s5_p[:, q, :], 0.0, ALU.mult, ALU.add)
                    i = dv.tensor_tensor_scan(s5_zi[:, q, :], decay, s5_q[:, q, :], 0.0, ALU.mult, ALU.add)
                link(i)
                if not first:
                    output(g, c - 1)
                dv.memset(small[:, 28:29], 0.0).then_inc(s5_z, 1)
                dv.wait_ge(bc_in[c % 2], (g + c // 2) * 32 + 32)
                cr, ci = cst[:, c % 2, 0, :, :], cst[:, c % 2, 1, :, :]
                dv.tensor_tensor(cc[:, 0, :, :], cr, wide(cre, g, c), ALU.mult)
                link(dv.tensor_tensor(ct[:, 0, :, :], ci, wide(cim, g, c), ALU.mult))
                dv.tensor_tensor(cc[:, 2, :, :], ct[:, 0, :, :], cc[:, 0, :, :], ALU.subtract)
                link(dv.tensor_tensor(cc[:, 0, :, :], cc[:, 0, :, :], ct[:, 0, :, :], ALU.subtract))
                dv.tensor_tensor(cc[:, 1, :, :], cr, wide(cim, g, c), ALU.mult)
                link(dv.tensor_tensor(ct[:, 1, :, :], ci, wide(cre, g, c), ALU.mult))
                dv.scalar_tensor_tensor(cc[:, 1, :, :], cc[:, 1, :, :], -1.0, ct[:, 1, :, :],
                                        ALU.mult, ALU.subtract).then_inc(bc_used, 1)
                dv.tensor_tensor(s5_out[0], cos, s5_zr, ALU.mult)
                dv.tensor_tensor(s5_out[1], sin, s5_zi, ALU.mult).then_inc(s5_x, 1)

            move(ust, p2[:, 24, :]).then_inc(s5_u, 1)
            dv.wait_ge(s5_raw, 1)
            reduce_angle(s5_ang, s5_num).then_inc(s5_angr, 1)
            chunk(0, 0, first=True)
            with s.loop(3, 22) as g:
                for b in range(2):
                    chunk(g, b + 1)
            chunk(3, 1, last=True)
            output(3, 1)
            dv.wait_ge(s5_gel, 9)
            dv.memset(small[:, 26:27], 0.0).then_inc(in_f32, 2)
            split_input(SPLITS["h3"], p2[:, 24:32, :], 0, 8, META)
            split_input(SPLITS["ys0"], p2[:, 0:8, :], 8, 8, META)
            for k in range(4):
                split(0, FIRST["w_glu"], 2 * k + 2)
            with dv.Fori(0, 2) as g:
                for k in range(8):
                    if k % 2 == 0:
                        split(g, FIRST["w_attn_br"], k + 2)
                    dv.wait_ge(quarters_used, g * 16 + 2 * (PAIRS + FIRST["w_attn_br"] + k + 1))
                    dv.tensor_tensor(h2b[:, g * 8 + k, :], PS[:, k % 4, 0:SEQ], p2[:, g * 8 + (32 + k), :],
                                     ALU.mult).then_inc(banks_free, 1)
            dv.wait_ge(banks_free, 4 + 304)
            link(dv.tensor_tensor(p2[:, 24:32, :], p2[:, 24:32, :], glug[:, :, :], ALU.mult))
            dv.memset(small[:, 27:28], 0.0).then_inc(in_f32, 1)
            split_input(SPLITS["ya"], p2[:, 24:32, :], 0, 8, META)
            with s.loop(2, 8) as g:
                for k in range(8):
                    if k % 2 == 0:
                        split(g, FIRST["w_ssm_br"], k + 2)
                    dv.wait_ge(quarters_used, g * 16 + 2 * (PAIRS + FIRST["w_ssm_br"] + k + 1))
                    dv.tensor_tensor(mtmp[:, k % 2, :], PS[:, k % 4, 0:SEQ], p2[:, g * 8 + (48 + k), :],
                                     ALU.mult).then_inc(banks_free, 1)
                    dv.wait_ge(banks_free, g * 8 + (4 + 304 + k + 1))
                    link(dv.tensor_tensor(h2b[:, g * 8 + k, :], h2b[:, g * 8 + k, :], mtmp[:, k % 2, :], ALU.add))
            dv.memset(small[:, 26:27], 0.0).then_inc(in_f32, 2)
            split_input(SPLITS["ys"], h2b, 0, 8, META)
            with dv.Fori(0, 4) as g:
                for k in range(4):
                    split(g, FIRST["w_out_2"], 2 * k + 2)
                    dv.wait_ge(quarters_used, g * 16 + 2 * (PAIRS + FIRST["w_out_2"] + 2 * (k + 1)))
                    dv.scalar_tensor_tensor(x2[:, g * 4 + k, :], PS[:, k, 0:SEQ], mod[:, bass.ds(g * 4 + (32 + k), 1)],
                                            x2[:, g * 4 + k, :], ALU.mult, ALU.add).then_inc(banks_free, 1)
            dv.wait_ge(banks_free, 4 + 336)
            link(dv.scalar_tensor_tensor(gmod[:, :], mod[:, 64:80], 1.0, vecs[:, V_N2:V_N2 + KC], ALU.add, ALU.mult))
            normalise(4, SEQ, x2, h2b, SPLITS["m2"], lambda c: gmod[:, c:c + 1], lambda c: mod[:, 48 + c:49 + c])
            with s.loop(22, 4) as g:
                for k in range(4):
                    split(g, FIRST["w_up"], 2 * k + 2)
                    dst = cva if k % 2 == 0 else cgt
                    dv.wait_ge(up_pre, g * 4 + (k + 1))
                    link(dv.scalar_tensor_tensor(dst[:, 1:], PS[:, k, 0:SEQ - 1], convw[:, 1, bass.ds(g * 4 + k, 1)],
                                                 dst[:, 1:], ALU.mult, ALU.add))
                    dv.scalar_tensor_tensor(dst[:, 2:], PS[:, k, 0:SEQ - 2], convw[:, 0, bass.ds(g * 4 + k, 1)],
                                            dst[:, 2:], ALU.mult, ALU.add).then_inc(banks_free, 1)
                    if k % 2 == 1:
                        dv.wait_ge(banks_free, g * 4 + (4 + 336 + k + 1))
                        dv.wait_ge(up_silu, g * 2 + (k // 2 + 1))
                        dv.tensor_tensor(act[:, g * 2 + k // 2, :], cva, cgt, ALU.mult).then_inc(act_ready, 1)
            spread_in("w_down", FC // 4, lambda j: act[:, j, :], N_SUB, True)
            dv.wait_ge(quarters_used, 2 * (PAIRS + TOTAL))
            for c in range(KC):
                link(dv.scalar_tensor_tensor(x2[:, c, :], PS[:, c // 2, (c % 2) * SEQ:(c % 2 + 1) * SEQ],
                                             mod[:, 80 + c:81 + c], x2[:, c, :], ALU.mult, ALU.add))
            dv.memset(small[:, 26:27], 0.0).then_inc(y_ready, 16)


INPUTS = ("x", "vecs", "convw", "w_f", "keys", "pos", "lam", "s5_b", "s5_c", "w_mod") + tuple(n for n, _ in STREAM)


def kernel(x, meta_tokens, norm_mix, w_in, b_forget, fox_q_gain, fox_k_gain, sb_out_gain, fox_out_gain, w_out,
           norm_ffn, peer_w_query, peer_sub_keys, peer_u, peer_v, c_2, positions_2, w_mod_2, b_mod_2, norm1_g_2,
           w_in_2, q_norm_g_2, k_norm_g_2, ssm_lambda_re_2, ssm_lambda_im_2, ssm_log_dt_2, ssm_b_re_2, ssm_b_im_2,
           ssm_c_re_2, ssm_c_im_2, ssm_d_2, w_glu_2, b_glu_2, w_attn_br_2, w_ssm_br_2, w_out_2, norm2_g_2, w_up_2,
           conv_w_2, conv_b_2, w_down_2):
    import concourse.bacc as bacc
    from concourse.bass_utils import run_bass_kernel_spmd

    def columns(v):
        return np.asarray(v).reshape(-1, P).T

    def chunks(w):
        w = np.asarray(w).reshape(w.shape[0] // HALF, 8, P, w.shape[-1] // P, P)
        return w.transpose(3, 0, 2, 1, 4).reshape(-1, P, HALF)

    def rows_of(w):
        return w.reshape(-1, P, 2, HALF).transpose(0, 2, 1, 3).reshape(-1, P, HALF)

    a = {}
    rows = np.concatenate([np.asarray(meta_tokens), np.asarray(x)[0]], axis=0)
    a["x"] = rows.reshape(KEYS, KC, P).transpose(2, 1, 0)
    half = P // 2
    freq = (np.float32(10000.0) ** (-np.arange(half, dtype=np.float32) / np.float32(half))).astype(np.float32)
    bf = np.zeros((P, 1), np.float32)
    bf[:HEADS, 0] = np.asarray(b_forget)[0]
    vecs = [columns(v) for v in (norm_mix, sb_out_gain, fox_out_gain, fox_q_gain, fox_k_gain, norm_ffn, norm1_g_2,
                                 q_norm_g_2, k_norm_g_2, ssm_d_2, b_glu_2, norm2_g_2, b_mod_2, c_2)]
    vecs += [np.concatenate([freq, freq])[:, None], bf, np.zeros((P, 26), np.float32)]
    a["vecs"] = np.concatenate(vecs, axis=1)
    taps = np.concatenate([np.asarray(conv_w_2)[0], np.asarray(conv_b_2)], axis=0)
    a["convw"] = taps.reshape(4, 2, FC, P).transpose(3, 0, 2, 1).reshape(P, 4, 2 * FC)
    w_all = np.asarray(w_in)[0]
    a["w_in"] = chunks(w_all[:, :56 * P])
    a["w_f"] = w_all[:, 56 * P:].reshape(KC, P, HEADS).transpose(1, 0, 2)
    a["w_out"] = chunks(np.asarray(w_out)[0])
    a["w_query"] = chunks(np.asarray(peer_w_query)[0])
    a["keys"] = np.asarray(peer_sub_keys)[0].reshape(16 * N_SUB, P).T
    a["peer_u"] = np.asarray(peer_u)[0]
    a["peer_u"] = a["peer_u"].reshape(N_SUB, N_SUB, 2, 8, P).transpose(1, 2, 4, 3, 0).reshape(-1, P, HALF)
    a["peer_v"] = np.asarray(peer_v)[0].reshape(N_SUB, N_SUB, D).transpose(1, 0, 2)
    a["peer_v"] = rows_of(a["peer_v"])
    a["w_mod"] = np.asarray(w_mod_2)[0].reshape(KC, P, N_MOD, D).transpose(2, 0, 1, 3).reshape(N_MOD * KC, P, D)
    a["w_in_2"] = chunks(np.asarray(w_in_2)[0])
    a["w_glu"] = chunks(np.asarray(w_glu_2)[0])
    a["w_attn_br"] = chunks(np.asarray(w_attn_br_2)[0])
    a["w_ssm_br"] = chunks(np.asarray(w_ssm_br_2)[0])
    a["w_out_2"] = chunks(np.asarray(w_out_2)[0])
    up = chunks(np.asarray(w_up_2)[0]).reshape(2, FC, 2, P, HALF)
    a["w_up"] = up.transpose(1, 0, 2, 3, 4).reshape(-1, P, HALF)
    a["w_down"] = rows_of(np.asarray(w_down_2)[0])
    a["pos"] = np.broadcast_to(np.asarray(positions_2)[0], (P, SEQ))
    lam = [np.asarray(v)[0].reshape(32, P).T for v in (ssm_lambda_re_2, ssm_lambda_im_2)]
    lam.append(np.repeat(np.asarray(ssm_log_dt_2)[0].reshape(32, 2), half, axis=1).T)
    a["lam"] = np.stack(lam, axis=1)
    s5_b = np.zeros((8, 4, 2, 16, 2, 2, half), np.float32)
    s5_c = np.zeros((8, 2, half, 2, 4, 2, 16), np.float32)
    for part, (b, c) in enumerate(((ssm_b_re_2, ssm_c_re_2), (ssm_b_im_2, ssm_c_im_2))):
        b = np.asarray(b)[0].reshape(8, 4, 2, half, 16)
        c = np.asarray(c)[0].reshape(8, 4, 2, 16, half)
        for g in range(2):
            s5_b[:, :, g, :, part, g, :] = b[:, :, g].transpose(0, 1, 3, 2)
            s5_c[:, g, :, part, :, g, :] = c[:, :, g].transpose(0, 3, 1, 2)
    a["s5_b"] = s5_b.reshape(8, P, 2, P)
    a["s5_c"] = s5_c.reshape(8, P, 2, 4, 32)

    nc = bacc.Bacc("TRN2", target_bir_lowering=False, num_devices=1)
    drams = {}
    for name in INPUTS:
        a[name] = np.ascontiguousarray(a[name])
        drams[name] = nc.dram_tensor(name + "_dram", a[name].shape, mybir.dt.from_np(a[name].dtype),
                                     kind="ExternalInput").ap()
    y = nc.dram_tensor("y_dram", (P, KC, SEQ), F32, kind="ExternalOutput").ap()
    drams["x1"] = nc.dram_tensor("x1_dram", (P, KC, SEQ), F32, kind="Internal").ap()
    build(nc, drams, y)
    r = run_bass_kernel_spmd(nc, [{name + "_dram": a[name] for name in INPUTS}], core_ids=[0])
    return r.results[0]["y_dram"].transpose(2, 1, 0).reshape(1, SEQ, D)
```
